# Optimizing a Trainium2 kernel written in Bass

```python
import math
import jax, jax.numpy as jnp
from jax import lax
import numpy as np

D_MODEL = 1024
BATCH = 1
SEQ = 256
DEPTH = 2

D_MLSTM = D_MODEL
N_MLSTM_HEADS = 4
MLSTM_HEAD_DIM = D_MLSTM // N_MLSTM_HEADS
D_CONV = D_MODEL
N_CONV_GROUPS = 8
D_MIX = D_MLSTM + D_CONV
D_IN_PROJ = 2 * D_MLSTM + 2 * D_CONV
MLSTM_CONV_K = 4
CONFORMER_CONV_K = 31
CHUNK = 128
D_FF = 4 * D_MODEL
N_ADA = 6
EPS = 1e-6


def rms_norm(x, g):
    xf = x.astype(jnp.float32)
    y = xf * lax.rsqrt(jnp.mean(xf * xf, axis=-1, keepdims=True) + EPS)
    return (y * g.astype(jnp.float32)).astype(x.dtype)

def group_layer_norm(x, n_groups, g, b=None):
    shp = x.shape
    xf = x.astype(jnp.float32).reshape(*shp[:-1], n_groups, shp[-1] // n_groups)
    mu = jnp.mean(xf, axis=-1, keepdims=True)
    xc = xf - mu
    var = jnp.mean(xc * xc, axis=-1, keepdims=True)
    y = (xc * lax.rsqrt(var + EPS)).reshape(shp) * g.astype(jnp.float32)
    if b is not None:
        y = y + b.astype(jnp.float32)
    return y.astype(x.dtype)

def causal_depthwise_conv(x, w, b):
    K, C = w.shape
    y = lax.conv_general_dilated(
        x, w[:, None, :].astype(x.dtype), window_strides=(1,), padding=[(K - 1, 0)],
        dimension_numbers=("NWC", "WIO", "NWC"), feature_group_count=C)
    return y + b.astype(x.dtype)

def mlstm_chunkwise(q, k, v, ig, lf):
    B, T, H, Dh = q.shape
    nc = T // CHUNK

    def to_chunks(a):
        a = a.astype(jnp.float32).reshape(B, nc, CHUNK, H, *a.shape[3:])
        return jnp.moveaxis(a, (1, 3), (0, 2))

    xs = (to_chunks(q), to_chunks(k), to_chunks(v), to_chunks(ig), to_chunks(lf))
    causal = jnp.tril(jnp.ones((CHUNK, CHUNK), dtype=bool))

    def body(carry, inp):
        C, n, m = carry
        qc, kc, vc, igc, lfc = inp
        b = jnp.cumsum(lfc, axis=-1)
        logw = b[..., :, None] - b[..., None, :] + igc[..., None, :]
        logw = jnp.where(causal, logw, -jnp.inf)
        g = b + m[..., None]
        m_t = jnp.maximum(g, jnp.max(logw, axis=-1))
        w = jnp.exp(logw - m_t[..., None])
        inter = jnp.exp(g - m_t)
        s = jnp.einsum("bhtd,bhsd->bhts", qc, kc) * w
        num = jnp.einsum("bhts,bhse->bhte", s, vc) + inter[..., None] * jnp.einsum("bhtd,bhde->bhte", qc, C)
        den = jnp.sum(s, axis=-1) + inter * jnp.einsum("bhtd,bhd->bht", qc, n)
        h = num / jnp.maximum(jnp.abs(den), jnp.exp(-m_t))[..., None]
        b_last = b[..., -1]
        a = b_last[..., None] - b + igc
        m_new = jnp.maximum(b_last + m, jnp.max(a, axis=-1))
        wk = jnp.exp(a - m_new[..., None])
        decay = jnp.exp(b_last + m - m_new)
        C_new = decay[..., None, None] * C + jnp.einsum("bhs,bhsd,bhse->bhde", wk, kc, vc)
        n_new = decay[..., None] * n + jnp.einsum("bhs,bhsd->bhd", wk, kc)
        return (C_new, n_new, m_new), h

    init = (jnp.zeros((B, H, Dh, Dh), jnp.float32), jnp.zeros((B, H, Dh), jnp.float32),
            jnp.zeros((B, H), jnp.float32))
    _, hs = lax.scan(body, init, xs)
    return jnp.moveaxis(hs, (0, 2), (1, 3)).reshape(B, T, H, Dh)

def mixer(h, w_in, w_conv_m, b_conv_m, w_q, w_k, w_v, w_gates, b_gates, g_mh,
          w_dw, b_dw, g_cn, b_cn, w_out):
    B, T, _ = h.shape
    H, Dh = N_MLSTM_HEADS, MLSTM_HEAD_DIM
    u = h @ w_in.astype(h.dtype)
    x_m, z, glu_a, glu_b = jnp.split(u, [D_MLSTM, 2 * D_MLSTM, 2 * D_MLSTM + D_CONV], axis=-1)

    x_c = jax.nn.silu(causal_depthwise_conv(x_m, w_conv_m, b_conv_m))
    xc_h = x_c.reshape(B, T, H, Dh)
    xm_h = x_m.reshape(B, T, H, Dh)
    q = jnp.einsum("bthd,hde->bthe", xc_h, w_q.astype(h.dtype))
    k = jnp.einsum("bthd,hde->bthe", xc_h, w_k.astype(h.dtype))
    v = jnp.einsum("bthd,hde->bthe", xm_h, w_v.astype(h.dtype))
    qkv = jnp.concatenate([q, k, v], axis=-1).reshape(B, T, H, 3 * Dh)
    qkv = jnp.moveaxis(qkv, 2, 3).reshape(B, T, 3 * D_MLSTM)
    gates = (qkv @ w_gates.astype(h.dtype) + b_gates.astype(h.dtype)).astype(jnp.float32)
    ig, fg = gates[..., :H], gates[..., H:]
    lf = jax.nn.log_sigmoid(fg)
    h_m = mlstm_chunkwise(q, k * (Dh ** -0.5), v, ig, lf)
    h_m = group_layer_norm(h_m.reshape(B, T, D_MLSTM), H, g_mh).astype(h.dtype)
    h_m = jax.nn.sigmoid(z) * h_m

    a = glu_a * jax.nn.sigmoid(glu_b)
    a = causal_depthwise_conv(a, w_dw, b_dw)
    a = jax.nn.silu(group_layer_norm(a, N_CONV_GROUPS, g_cn, b_cn))

    return jnp.concatenate([h_m, a], axis=-1) @ w_out.astype(h.dtype)

def first_inputs(seed: int = 0) -> dict:
    key = jax.random.key(seed)
    ks = jax.random.split(key, 26)
    f32 = jnp.float32

    def nrm(k, shape, fan_in, scale=1.0):
        return jax.random.normal(k, shape, f32) * (scale * fan_in ** -0.5)

    def gain(k, shape):
        return 1.0 + 0.05 * jax.random.normal(k, shape, f32)

    def small(k, shape):
        return 0.02 * jax.random.normal(k, shape, f32)

    H = N_MLSTM_HEADS
    ig_bias = 0.1 * jax.random.normal(ks[24], (DEPTH, H), f32)
    fg_bias = jnp.linspace(3.0, 6.0, H, dtype=f32)[None, :] + 0.1 * jax.random.normal(ks[25], (DEPTH, H), f32)
    return {
        "x": jax.random.normal(ks[0], (BATCH, SEQ, D_MODEL), f32),
        "c": jax.random.normal(ks[1], (BATCH, D_MODEL), f32),
        "w_ada": nrm(ks[2], (DEPTH, D_MODEL, N_ADA * D_MODEL), D_MODEL, 0.5),
        "b_ada": small(ks[3], (DEPTH, N_ADA * D_MODEL)),
        "g_pre_mix": gain(ks[4], (DEPTH, D_MODEL)),
        "g_post_mix": gain(ks[5], (DEPTH, D_MODEL)),
        "g_pre_mlp": gain(ks[6], (DEPTH, D_MODEL)),
        "g_post_mlp": gain(ks[7], (DEPTH, D_MODEL)),
        "w_in": nrm(ks[8], (DEPTH, D_MODEL, D_IN_PROJ), D_MODEL),
        "w_conv_m": nrm(ks[9], (DEPTH, MLSTM_CONV_K, D_MLSTM), MLSTM_CONV_K),
        "b_conv_m": small(ks[10], (DEPTH, D_MLSTM)),
        "w_q": nrm(ks[11], (DEPTH, H, MLSTM_HEAD_DIM, MLSTM_HEAD_DIM), MLSTM_HEAD_DIM),
        "w_k": nrm(ks[12], (DEPTH, H, MLSTM_HEAD_DIM, MLSTM_HEAD_DIM), MLSTM_HEAD_DIM),
        "w_v": nrm(ks[13], (DEPTH, H, MLSTM_HEAD_DIM, MLSTM_HEAD_DIM), MLSTM_HEAD_DIM),
        "w_gates": nrm(ks[14], (DEPTH, 3 * D_MLSTM, 2 * H), 3 * D_MLSTM),
        "b_gates": jnp.concatenate([ig_bias, fg_bias], axis=-1),
        "g_mh": gain(ks[15], (DEPTH, D_MLSTM)),
        "w_dw": nrm(ks[16], (DEPTH, CONFORMER_CONV_K, D_CONV), CONFORMER_CONV_K),
        "b_dw": small(ks[17], (DEPTH, D_CONV)),
        "g_cn": gain(ks[18], (DEPTH, D_CONV)),
        "b_cn": small(ks[19], (DEPTH, D_CONV)),
        "w_out": nrm(ks[20], (DEPTH, D_MIX, D_MODEL), D_MIX),
        "w_ff1": nrm(ks[21], (DEPTH, D_MODEL, D_FF), D_MODEL),
        "w_ff2": nrm(ks[22], (DEPTH, D_FF, D_MODEL), D_FF),
    }

def first_block(x, c, w_ada, b_ada, g_pre_mix, g_post_mix, g_pre_mlp, g_post_mlp, w_in,
              w_conv_m, b_conv_m, w_q, w_k, w_v, w_gates, b_gates, g_mh, w_dw, b_dw,
              g_cn, b_cn, w_out, w_ff1, w_ff2):
    c_act = jax.nn.silu(c.astype(jnp.float32))
    for l in range(DEPTH):
        mod = (c_act @ w_ada[l].astype(jnp.float32) + b_ada[l].astype(jnp.float32)).astype(x.dtype)
        sh_mix, sc_mix, gt_mix, sh_mlp, sc_mlp, gt_mlp = [m[:, None, :] for m in jnp.split(mod, N_ADA, axis=-1)]

        h = rms_norm(x, g_pre_mix[l]) * (1 + sc_mix) + sh_mix
        y = mixer(h, w_in[l], w_conv_m[l], b_conv_m[l], w_q[l], w_k[l], w_v[l], w_gates[l], b_gates[l],
                  g_mh[l], w_dw[l], b_dw[l], g_cn[l], b_cn[l], w_out[l])
        x = x + gt_mix * rms_norm(y, g_post_mix[l])

        h = rms_norm(x, g_pre_mlp[l]) * (1 + sc_mlp) + sh_mlp
        f = jnp.square(jax.nn.relu(h @ w_ff1[l].astype(h.dtype))) @ w_ff2[l].astype(h.dtype)
        x = x + gt_mlp * rms_norm(f, g_post_mlp[l])
    return x


DEPTH_2 = 1

MEM_LEN = 256
RMS_EPS = 1e-6
NEG_INF = -1e30
FORCE = 1e6

POOL_WINDOWS = (2, 4, 8, 16)
POOL_GROUPS = len(POOL_WINDOWS)
POOL_GROUP_DIM = D_MODEL // 8
POOL_WIDTH = POOL_GROUPS * POOL_GROUP_DIM

NSA_HEADS = 16
NSA_KV_HEADS = 4
NSA_GROUP = NSA_HEADS // NSA_KV_HEADS
HEAD_DIM = 64
NSA_WIDTH = NSA_HEADS * HEAD_DIM
KV_WIDTH = NSA_KV_HEADS * HEAD_DIM
CMP_LEN = 32
CMP_STRIDE = 16
SEL_BLOCK = 64
N_SELECT = 16
WINDOW = 512
NSA_Q_BLOCK = 64

X_HEADS = 4
X_HEAD_DIM = 128
X_WIDTH = X_HEADS * X_HEAD_DIM

N_BUCKETS = 32
MAX_DISTANCE = 128

PEER_HEADS = 8
N_KEYS = 128
N_EXPERTS = N_KEYS * N_KEYS
PEER_QDIM = 256
PEER_HALF = PEER_QDIM // 2
PEER_TOPK = 16
PEER_TOKEN_BLOCK = 128

N_BRANCHES = 3
IN_WIDTHS = (POOL_WIDTH, NSA_WIDTH, 6 * KV_WIDTH, 3 * NSA_HEADS, X_WIDTH, N_BRANCHES * D_MODEL)
IN_SPLITS = tuple(int(s) for s in np.cumsum(IN_WIDTHS)[:-1])
D_IN = int(sum(IN_WIDTHS))


def rms_norm_2(x, g):
    xf = x.astype(jnp.float32)
    y = xf * lax.rsqrt(jnp.mean(xf * xf, axis=-1, keepdims=True) + RMS_EPS)
    return (y * g.astype(jnp.float32)).astype(x.dtype)

def masked_softmax(s, mask):
    return jax.nn.softmax(jnp.where(mask, s, NEG_INF), axis=-1)

def t5_bucket(dist):
    n = jnp.maximum(dist, 0)
    max_exact = N_BUCKETS // 2
    nf = jnp.maximum(n, 1).astype(jnp.float32)
    large = max_exact + (jnp.log(nf / max_exact) / math.log(MAX_DISTANCE / max_exact)
                         * (N_BUCKETS - max_exact)).astype(jnp.int32)
    large = jnp.minimum(large, N_BUCKETS - 1)
    return jnp.where(n < max_exact, n, large)

def pool_mixer(u, w_grp, scale):
    B, T, _ = u.shape
    c = jnp.cumsum(u.astype(jnp.float32), axis=1)
    t_idx = jnp.arange(T)
    outs = []
    for g, w in enumerate(POOL_WINDOWS):
        sl = slice(g * POOL_GROUP_DIM, (g + 1) * POOL_GROUP_DIM)
        cg = c[..., sl]
        shifted = jnp.pad(cg, ((0, 0), (w, 0), (0, 0)))[:, :T]
        cnt = jnp.minimum(t_idx + 1, w).astype(jnp.float32)[None, :, None]
        outs.append((cg - shifted) / cnt - u[..., sl].astype(jnp.float32))
    pooled = jnp.stack(outs, axis=2)
    mixed = jnp.einsum('btgc,gcd->btgd', pooled, w_grp.astype(jnp.float32))
    return (mixed.reshape(B, T, POOL_WIDTH) * scale.astype(jnp.float32)).astype(u.dtype)

def nsa_attention(q, k_cmp_tok, v_cmp_tok, k_sel, v_sel, k_win, v_win,
                  w_cmp_k, w_cmp_v, pe_k, pe_v, rel_bias):
    B, T = q.shape[:2]
    G, R, dh = NSA_KV_HEADS, NSA_GROUP, HEAD_DIM
    QB = NSA_Q_BLOCK
    n_cmp = (T - CMP_LEN) // CMP_STRIDE + 1
    n_sel = T // SEL_BLOCK
    n_top = min(N_SELECT, n_sel)

    cmp_start = jnp.arange(n_cmp) * CMP_STRIDE
    cmp_end = cmp_start + CMP_LEN - 1
    tok_idx = cmp_start[:, None] + jnp.arange(CMP_LEN)[None, :]

    def compress(tok, pe, w):
        blk = tok[:, tok_idx] + pe[None, None, :, None, :]
        blk = blk.transpose(0, 1, 3, 2, 4).reshape(B, n_cmp, G, CMP_LEN * dh)
        return blk @ w

    kc = compress(k_cmp_tok, pe_k, w_cmp_k)
    vc = compress(v_cmp_tok, pe_v, w_cmp_v)

    sel_start = jnp.arange(n_sel) * SEL_BLOCK
    overlap = ((cmp_start[:, None] < sel_start[None, :] + SEL_BLOCK) &
               (cmp_start[:, None] + CMP_LEN > sel_start[None, :])).astype(jnp.float32)

    ks_blk = k_sel.reshape(B, n_sel, SEL_BLOCK, G, dh).transpose(0, 3, 1, 2, 4)
    vs_blk = v_sel.reshape(B, n_sel, SEL_BLOCK, G, dh).transpose(0, 3, 1, 2, 4)
    kw_pad = jnp.pad(k_win, ((0, 0), (WINDOW, 0), (0, 0), (0, 0)))
    vw_pad = jnp.pad(v_win, ((0, 0), (WINDOW, 0), (0, 0), (0, 0)))

    qg = q.reshape(B, T, G, R, dh) * (dh ** -0.5)
    table_gr = rel_bias.astype(jnp.float32).reshape(N_BUCKETS, G, R)
    bi = jnp.arange(B)[:, None, None, None]
    gi = jnp.arange(G)[None, :, None, None]
    gi5 = jnp.arange(G)[None, :, None, None, None]
    sel_ids = jnp.arange(n_sel)
    win_off = jnp.arange(WINDOW + QB)

    def head_bias(dist):
        return table_gr[t5_bucket(dist)].transpose(2, 3, 0, 1)

    def block(t0):
        qb = lax.dynamic_slice_in_dim(qg, t0, QB, axis=1)
        tq = t0 + jnp.arange(QB)

        dist_c = tq[:, None] - cmp_end[None, :]
        mask_c = dist_c >= 0
        s_c = jnp.einsum('bqgrd,bcgd->bgrqc', qb, kc).astype(jnp.float32) + head_bias(dist_c)
        has = jnp.any(mask_c, axis=-1).astype(jnp.float32)
        p_c = masked_softmax(s_c, mask_c) * has[None, None, None, :, None]
        o_c = jnp.einsum('bgrqc,bcgd->bqgrd', p_c.astype(vc.dtype), vc)

        imp = jnp.einsum('bgrqc,cs->bgqs', p_c, overlap)
        blk_q = tq // SEL_BLOCK
        forced = ((sel_ids[None, :] == 0) | (sel_ids[None, :] == blk_q[:, None]) |
                  (sel_ids[None, :] == blk_q[:, None] - 1))
        causal_blk = sel_ids[None, :] <= blk_q[:, None]
        imp = jnp.where(forced, FORCE, jnp.where(causal_blk, imp, -FORCE))
        _, idx = lax.top_k(imp, n_top)

        k_g = ks_blk[bi, gi, idx]
        v_g = vs_blk[bi, gi, idx]
        pos = idx[..., None] * SEL_BLOCK + jnp.arange(SEL_BLOCK)
        dist_s = tq[None, None, :, None, None] - pos
        bias_s = jnp.moveaxis(table_gr[t5_bucket(dist_s), gi5], -1, 2)
        nk = n_top * SEL_BLOCK
        s_s = jnp.einsum('bqgrd,bgqkld->bgrqkl', qb, k_g).astype(jnp.float32) + bias_s
        s_s = s_s.reshape(B, G, R, QB, nk)
        mask_s = (dist_s >= 0).reshape(B, G, 1, QB, nk)
        p_s = masked_softmax(s_s, mask_s)
        o_s = jnp.einsum('bgrqn,bgqnd->bqgrd', p_s.astype(v_g.dtype), v_g.reshape(B, G, QB, nk, dh))

        k_w = lax.dynamic_slice_in_dim(kw_pad, t0, WINDOW + QB, axis=1)
        v_w = lax.dynamic_slice_in_dim(vw_pad, t0, WINDOW + QB, axis=1)
        pos_w = t0 - WINDOW + win_off
        dist_w = tq[:, None] - pos_w[None, :]
        mask_w = (dist_w >= 0) & (dist_w < WINDOW) & (pos_w[None, :] >= 0)
        s_w = jnp.einsum('bqgrd,bkgd->bgrqk', qb, k_w).astype(jnp.float32) + head_bias(dist_w)
        p_w = masked_softmax(s_w, mask_w)
        o_w = jnp.einsum('bgrqk,bkgd->bqgrd', p_w.astype(v_w.dtype), v_w)
        return (o_c, o_s, o_w)

    o_c, o_s, o_w = lax.map(block, jnp.arange(T // QB) * QB)

    def unblock(o):
        return o.transpose(1, 0, 2, 3, 4, 5).reshape(B, T, NSA_HEADS, dh).astype(q.dtype)

    return unblock(o_c), unblock(o_s), unblock(o_w)

def memory_cross_attention(q_x, mem, g_mem, w_mem_kv):
    B, T, _ = q_x.shape
    M = mem.shape[1]
    kv = rms_norm_2(mem, g_mem) @ w_mem_kv
    k, v = jnp.split(kv, 2, axis=-1)
    q = q_x.reshape(B, T, X_HEADS, X_HEAD_DIM) * (X_HEAD_DIM ** -0.5)
    k = k.reshape(B, M, X_HEADS, X_HEAD_DIM)
    v = v.reshape(B, M, X_HEADS, X_HEAD_DIM)
    s = jnp.einsum('bthd,bmhd->bhtm', q, k).astype(jnp.float32)
    p = jax.nn.softmax(s, axis=-1).astype(v.dtype)
    return jnp.einsum('bhtm,bmhd->bthd', p, v).reshape(B, T, X_WIDTH)

def peer_ffn(h, w_q, sub_keys, u, v):
    B, T, D = h.shape
    tokens = h.reshape(-1, D)
    blocks = tokens.reshape(-1, PEER_TOKEN_BLOCK, D)
    n = PEER_TOKEN_BLOCK

    def block(xb):
        q = (xb @ w_q).reshape(n, PEER_HEADS, 2, PEER_HALF)
        s = jnp.einsum('nhpc,hpkc->nhpk', q, sub_keys).astype(jnp.float32)
        s_top, i_top = lax.top_k(s, PEER_TOPK)
        cand_s = (s_top[:, :, 0, :, None] + s_top[:, :, 1, None, :]).reshape(n, PEER_HEADS, -1)
        cand_i = (i_top[:, :, 0, :, None] * N_KEYS + i_top[:, :, 1, None, :]).reshape(n, PEER_HEADS, -1)
        best_s, best_pos = lax.top_k(cand_s, PEER_TOPK)
        ids = jnp.take_along_axis(cand_i, best_pos, axis=-1)
        gate = jax.nn.softmax(best_s, axis=-1)
        u_e = u[ids]
        act = jax.nn.gelu(jnp.einsum('nd,nhkd->nhk', xb, u_e).astype(jnp.float32), approximate=False)
        wgt = (gate * act).astype(xb.dtype)
        return jnp.einsum('nhk,nhkd->nd', wgt, v[ids])

    return lax.map(block, blocks).reshape(B, T, D)

def second_inputs(seed: int = 0) -> dict:
    key = jax.random.key(seed)
    ks = jax.random.split(key, 24)

    def nrm(k, shape, scale):
        return jax.random.normal(k, shape, jnp.float32) * scale

    D = D_MODEL
    return {
        "x": nrm(ks[0], (BATCH, SEQ, D), 1.0),
        "mem": nrm(ks[1], (BATCH, MEM_LEN, D), 1.0),
        "rel_bias": nrm(ks[2], (N_BUCKETS, NSA_HEADS), 0.5),
        "g_mix": 1.0 + nrm(ks[3], (DEPTH_2, D), 0.05),
        "w_in": nrm(ks[4], (DEPTH_2, D, D_IN), D ** -0.5),
        "w_pool_grp": nrm(ks[5], (DEPTH_2, POOL_GROUPS, POOL_GROUP_DIM, POOL_GROUP_DIM), POOL_GROUP_DIM ** -0.5),
        "pool_scale": 1.0 + nrm(ks[6], (DEPTH_2, POOL_WIDTH), 0.1),
        "w_pool_out": nrm(ks[7], (DEPTH_2, POOL_WIDTH, D), POOL_WIDTH ** -0.5),
        "w_cmp_k": nrm(ks[8], (DEPTH_2, CMP_LEN * HEAD_DIM, HEAD_DIM), (CMP_LEN * HEAD_DIM) ** -0.5),
        "w_cmp_v": nrm(ks[9], (DEPTH_2, CMP_LEN * HEAD_DIM, HEAD_DIM), (CMP_LEN * HEAD_DIM) ** -0.5),
        "pe_k": nrm(ks[10], (DEPTH_2, CMP_LEN, HEAD_DIM), 0.5),
        "pe_v": nrm(ks[11], (DEPTH_2, CMP_LEN, HEAD_DIM), 0.5),
        "w_nsa_out": nrm(ks[12], (DEPTH_2, NSA_WIDTH, D), NSA_WIDTH ** -0.5),
        "g_mem": 1.0 + nrm(ks[13], (DEPTH_2, D), 0.05),
        "w_mem_kv": nrm(ks[14], (DEPTH_2, D, 2 * X_WIDTH), D ** -0.5),
        "w_x_out": nrm(ks[15], (DEPTH_2, X_WIDTH, D), X_WIDTH ** -0.5),
        "w_o": nrm(ks[16], (DEPTH_2, D, D), D ** -0.5),
        "g_ffn": 1.0 + nrm(ks[17], (DEPTH_2, D), 0.05),
        "w_peer_q": nrm(ks[18], (DEPTH_2, D, PEER_HEADS * PEER_QDIM), D ** -0.5),
        "peer_sub_keys": nrm(ks[19], (DEPTH_2, PEER_HEADS, 2, N_KEYS, PEER_HALF), PEER_HALF ** -0.5),
        "peer_u": nrm(ks[20], (DEPTH_2, N_EXPERTS, D), D ** -0.5),
        "peer_v": nrm(ks[21], (DEPTH_2, N_EXPERTS, D), 0.1),
        "g_final": 1.0 + nrm(ks[22], (D,), 0.05),
    }

def second_block(x, mem, rel_bias, g_mix, w_in, w_pool_grp, pool_scale, w_pool_out,
              w_cmp_k, w_cmp_v, pe_k, pe_v, w_nsa_out, g_mem, w_mem_kv, w_x_out, w_o,
              g_ffn, w_peer_q, peer_sub_keys, peer_u, peer_v, g_final):
    B, T, D = x.shape
    for l in range(DEPTH_2):
        hn = rms_norm_2(x, g_mix[l])
        z = hn @ w_in[l]
        u_pool, q_nsa, kv_nsa, g_nsa, q_x, g_merge = jnp.split(z, IN_SPLITS, axis=-1)

        y_pool = pool_mixer(u_pool, w_pool_grp[l], pool_scale[l]) @ w_pool_out[l]

        kv = kv_nsa.reshape(B, T, 6, NSA_KV_HEADS, HEAD_DIM)
        o_c, o_s, o_w = nsa_attention(q_nsa.reshape(B, T, NSA_HEADS, HEAD_DIM),
                                      kv[:, :, 0], kv[:, :, 1], kv[:, :, 2], kv[:, :, 3],
                                      kv[:, :, 4], kv[:, :, 5],
                                      w_cmp_k[l], w_cmp_v[l], pe_k[l], pe_v[l], rel_bias)
        bg = jax.nn.sigmoid(g_nsa.reshape(B, T, 3, NSA_HEADS))[..., None]
        o_nsa = (bg[:, :, 0] * o_c + bg[:, :, 1] * o_s + bg[:, :, 2] * o_w).reshape(B, T, NSA_WIDTH)
        y_nsa = o_nsa @ w_nsa_out[l]

        y_mem = memory_cross_attention(q_x, mem, g_mem[l], w_mem_kv[l]) @ w_x_out[l]

        gm = jax.nn.sigmoid(g_merge.reshape(B, T, N_BRANCHES, D))
        merged = gm[:, :, 0] * y_pool + gm[:, :, 1] * y_nsa + gm[:, :, 2] * y_mem
        x = x + merged @ w_o[l]

        x = x + peer_ffn(rms_norm_2(x, g_ffn[l]), w_peer_q[l], peer_sub_keys[l], peer_u[l], peer_v[l])
    return rms_norm_2(x, g_final)


def setup_inputs(seed=0):
    out = dict(first_inputs(seed))
    for name, value in second_inputs(seed + 1).items():
        if name != "x":
            out[name + "_2"] = value
    return out


def reference(
    x, c, w_ada, b_ada, g_pre_mix, g_post_mix, g_pre_mlp, g_post_mlp, w_in, w_conv_m, b_conv_m,
    w_q, w_k, w_v, w_gates, b_gates, g_mh, w_dw, b_dw, g_cn, b_cn, w_out, w_ff1, w_ff2, mem_2,
    rel_bias_2, g_mix_2, w_in_2, w_pool_grp_2, pool_scale_2, w_pool_out_2, w_cmp_k_2, w_cmp_v_2,
    pe_k_2, pe_v_2, w_nsa_out_2, g_mem_2, w_mem_kv_2, w_x_out_2, w_o_2, g_ffn_2, w_peer_q_2,
    peer_sub_keys_2, peer_u_2, peer_v_2, g_final_2,
):
    x = first_block(
        x, c, w_ada, b_ada, g_pre_mix, g_post_mix, g_pre_mlp, g_post_mlp, w_in, w_conv_m,
        b_conv_m, w_q, w_k, w_v, w_gates, b_gates, g_mh, w_dw, b_dw, g_cn, b_cn, w_out, w_ff1,
        w_ff2,
    )
    return second_block(
        x, mem_2, rel_bias_2, g_mix_2, w_in_2, w_pool_grp_2, pool_scale_2, w_pool_out_2,
        w_cmp_k_2, w_cmp_v_2, pe_k_2, pe_v_2, w_nsa_out_2, g_mem_2, w_mem_kv_2, w_x_out_2,
        w_o_2, g_ffn_2, w_peer_q_2, peer_sub_keys_2, peer_u_2, peer_v_2, g_final_2,
    )


_drawn_inputs = setup_inputs


def setup_inputs(seed=0):
    import zlib

    import numpy as np

    out = dict(_drawn_inputs(seed))
    spreads = {}
    factors = {'b_conv_m': 5.224,
     'g_mh': 3.716,
     'b_dw': 3.966,
     'g_cn': 2.967,
     'b_cn': 8.0,
     'pe_k_2': 64.0,
     'g_mem_2': 8.0,
     'g_ffn_2': 5.874,
     'rel_bias_2': 3.061,
     'pool_scale_2': 3.895}
    for name, (base, spread) in spreads.items():
        noise = np.random.default_rng([zlib.crc32(name.encode()), seed]).standard_normal(out[name].shape)
        drawn = base * np.exp(spread * noise) if base else spread * noise
        out[name] = __import__('jax').numpy.asarray(drawn.astype(out[name].dtype))
    for name, factor in factors.items():
        out[name] = (out[name] * factor).astype(out[name].dtype)
    return out
```

```python
from contextlib import ExitStack

import concourse.bass as bass
from concourse import mybir

ALU = mybir.AluOpType
ACT = mybir.ActivationFunctionType
AX = mybir.AxisListType
F32 = mybir.dt.float32
U32 = mybir.dt.uint32

P = 128
T = 256
D = 1024
CT = D // P
DEPTH = 2
H = 4
DH = 256
FF = 4 * D
KM = 4
KC = 31
NEG = -1e30
EPS = 1e-6

SLOT = 2048
RING = 4
ADA_CHUNKS = 24

B_ADA, G_PRE_MIX, G_PRE_MLP, G_POST_MIX, G_POST_MLP = 0, 48, 56, 64, 72
B_CONV_M, G_MH, B_DW, G_CN, B_CN, C_COL = 80, 88, 96, 104, 112, 120
W_DW, W_CONV = 128, 376
NPC = 408


NH, G, R, HD = 16, 4, 4, 64
N_BUCKETS = 32
CMP_LEN, CMP_STRIDE = 32, 16
NCMP = (T - CMP_LEN) // CMP_STRIDE + 1
POOL_WINDOWS = (2, 4, 8, 16)
XH = 4
KV0, GN0, QX0, GM0 = 1536, 3072, 3120, 3632
PH, TOPK = 8, 16
NBUF = 8
LAG = 20
G_MIX2, G_MEM2, G_FFN2, POOL_SC2 = 0, 8, 16, 24
UNITS = [(g, s) for g in range(G) for s in range(2)] + [("x", 0), ("x", 1)]
FILL = [["pool0", "pool1"], ["gm0", "gm1"], ["gm2", "gm3"], ["gm4", "gm5"], ["gm6", "gm7"], ["gm8", "gm9"],
        ["gm10", "gm11"], ["mix"], ["pool_out0", "pool_out1"], []]


def weight_jobs():
    jobs = []
    for l in range(DEPTH):
        for j in list(range(8, 16)) + list(range(0, 8)):
            jobs.append(("w_in", l, j))
        for j in range(8):
            jobs.append(("w_out", l, j))
        for j in range(16):
            jobs.append(("w_ff1", l, j))
        for j in range(16):
            jobs.append(("w_ff2", l, j))
    for j in ("kcmp", "vcmp", "q0", "q1", "q2", "q3", "ksel", "vsel", "kwin", "vwin", "qx0", "qx1",
              "memk0", "memk1", "memv0", "memv1"):
        jobs.append((j, 2, 0))
    for names in FILL:
        jobs += [(j, 2, 0) for j in names if j != "mix"]
    for name, n in (("nsa_out", 4), ("x_out", 2), ("w_o", 4), ("peer_q", 8)):
        jobs += [(f"{name}{j}", 2, 0) for j in range(n)]
    return jobs


def second_weight(a, name):
    w_in = a["w_in_2"][0].rearrange("(k p) n -> p k n", p=P)
    parts = ("kcmp", "vcmp", "ksel", "vsel", "kwin", "vwin")
    if name in parts:
        c = KV0 + 256 * parts.index(name)
        return w_in[:, :, c:c + 256]
    base = name.rstrip("0123456789")
    j = int(name[len(base):])
    if base == "pool":
        return w_in[:, :, 256 * j:256 * j + 256]
    if base == "qx":
        return w_in[:, :, QX0 + 256 * j:QX0 + 256 * j + 256]
    if base == "gm":
        return w_in[:, :, GM0 + 256 * j:GM0 + 256 * j + 256]
    if base in ("memk", "memv"):
        c = 512 * (base == "memv") + 256 * j
        return a["w_mem_kv_2"][0].rearrange("(k p) n -> p k n", p=P)[:, :, c:c + 256]
    if base in ("pool_out", "x_out"):
        return a[f"w_{base}_2"][0].rearrange("(k p) n -> p k n", p=P)[:, :, 512 * j:512 * j + 512]
    w = {"nsa_out": "w_nsa_out_2", "w_o": "w_o_2", "peer_q": "w_peer_q_2"}[base]
    return a[w][0].rearrange("(k p) n -> p k n", p=P)[:, :, 256 * j:256 * j + 256]


def top_of(dve, link, values, top, where, groups):
    v = dve
    for c in range(groups):
        i = v.max(top[:, c, 0:8], values[:, c, :])
    link(i)
    for c in range(groups):
        i = v.max_index(where[:, c, 0:8], top[:, c, 0:8], values[:, c, :])
    link(i)
    for c in range(groups):
        i = v.match_replace(values[:, c, :], top[:, c, 0:8], values[:, c, :], -3.0e38)
    link(i)
    for c in range(groups):
        i = v.max(top[:, c, 8:16], values[:, c, :])
    link(i)
    for c in range(groups):
        i = v.max_index(where[:, c, 8:16], top[:, c, 8:16], values[:, c, :])
    link(i)


def build_program(nc, a, out):
    ctx = ExitStack()
    with ctx:
        def sb(name, shape, dt=F32):
            return ctx.enter_context(nc.sbuf_tensor(name, shape, dt))

        ring = sb("ring", [P, RING, SLOT])
        xT = sb("xT", [P, CT, T])
        hT = sb("hT", [P, CT, T])
        tmp = sb("tmp", [P, CT, T])
        region = sb("region", [P, 32768])
        at = 0

        def cut(n):
            nonlocal at
            at += n
            return region[:, at - n:at]

        U = cut(8192).rearrange("p (c t) -> p c t", t=T)
        xc = cut(2048).rearrange("p (c t) -> p c t", t=T)
        qT = cut(2048).rearrange("p (c t) -> p c t", t=T)
        kT = cut(2048).rearrange("p (c t) -> p c t", t=T)
        vtok = cut(2048).rearrange("p (s e) -> p s e", s=2)
        wqkv = cut(6144).rearrange("p (m c e) -> p m c e", m=3, c=2 * H)
        ada_in = cut(4096).rearrange("p (b k n) -> p b k n", b=2, k=CT)
        ada_acc = cut(6144)
        x_tok = tmp[:, :, :].rearrange("p c t -> p (c t)").rearrange("p (s d) -> p s d", s=2)
        def piece(lo, n):
            return region[:, lo:lo + n]

        gm = piece(0, 6144).rearrange("p (c t) -> p c t", t=T)
        poolT = piece(6144, 1024).rearrange("p (c t) -> p c t", t=T)
        qxT = piece(7168, 1024).rearrange("p (c t) -> p c t", t=T)
        wcmp = piece(8192, 4096).rearrange("p (m i e) -> p m i e", m=2, i=CMP_LEN)
        oT = piece(8192, 2048).rearrange("p (c t) -> p c t", t=T)
        merged = piece(10240, 2048).rearrange("p (c t) -> p c t", t=T)
        q2T = piece(12288, 2048).rearrange("p (c t) -> p c t", t=T)
        cmpT = piece(14336, 1024).rearrange("p (m c t) -> p m c t", m=2, t=T)
        oxT = piece(14336, 1024).rearrange("p (c t) -> p c t", t=T)
        kselT = piece(15360, 1024).rearrange("p (m c t) -> p m c t", m=2, t=T)
        onehot = piece(16384, 512)
        bias_w = piece(16896, 512)
        rel = piece(17408, NH)
        wqkv_free = piece(18432, 1024)
        v2 = piece(16384, 1024).rearrange("p (m s e) -> p m s e", m=2, s=2)
        kxT = piece(17408, 1024).rearrange("p (c t) -> p c t", t=T)
        vx = piece(18432, 1024).rearrange("p (s e) -> p s e", s=2)
        probs = [piece(19456, 2048).rearrange("p (m r t) -> p m r t", m=2, r=R),
                 piece(24576, 2048).rearrange("p (m r t) -> p m r t", m=2, r=R)]
        probsT = piece(21504, 2048).rearrange("p (m j r t) -> p m j r t", m=2, j=2, r=R)
        memtok = piece(22528, 2048).rearrange("p (s d) -> p s d", s=2)
        memT = piece(24576, 2048).rearrange("p (c t) -> p c t", t=T)
        bias = [piece(26624, 2048).rearrange("p (h t) -> p h t", h=NH), piece(28672, 4096).rearrange("p (h t) -> p h t", h=NH)]
        blk = tmp[:, :, :].rearrange("p c t -> p (c t)")[:, 0:1920].rearrange("p (m g c i) -> p m g c i", m=2, g=2, i=CMP_LEN)
        win = [tmp[:, 0:4, :], tmp[:, 4:8, :]]
        qpT = piece(0, 4096).rearrange("p (c t) -> p c t", t=T)
        subT = piece(4096, 2048).rearrange("p (c t) -> p c t", t=P)
        s_sb = piece(6144, 2048).rearrange("p (c t) -> p c t", t=P)
        acc = piece(8192, 2048).rearrange("p (s d) -> p s d", s=2)
        h_tok = piece(10240, 2048).rearrange("p (s d) -> p s d", s=2)
        ubuf = piece(12288, 8192).rearrange("p (b d) -> p b d", b=NBUF)
        vbuf = piece(20480, 8192).rearrange("p (b d) -> p b d", b=NBUF)
        eq = piece(28672, 2048)
        sub_raw = piece(30720, 2048).rearrange("p (c t) -> p c t", t=P)
        cand = tmp[:, :, :]
        g_fin = ring[:, 0, 0:D]

        vT = tmp
        y = hT

        prow = qT.rearrange("p c t -> p (c t)")[:, 0:DEPTH * 4 * P].rearrange("p (l k q) -> p l k q", l=DEPTH, k=4)
        small = sb("small", [P, 3072])

        def small_piece(lo, n, rows=P):
            return small[0:rows, lo:lo + n]

        pc = sb("pc", [P, DEPTH, NPC])
        modc = sb("modc", [P, 48])
        mod_scale = sb("mod_scale", [P, 4, CT])
        c_act = sb("c_act", [P, CT])
        wg = sb("wg", [P, 6, H * 2 * H])
        bg = sb("bg", [2 * H, 1])
        ident = sb("ident", [P, P])
        ones = sb("ones", [P, P])
        eps_col = sb("eps_col", [P, 1])
        causal = sb("causal", [P, 2, T])
        wpg = small_piece(1504, 512).rearrange("p (g d) -> p g d", g=4)
        pick = small_piece(2048, 512, H).rearrange("p (h q) -> p h q", h=H)
        rstd = sb("rstd", [P, T])
        gates = small_piece(2816, 256, 2 * H)
        fgr = hT[0:H, 0:3, :]
        lrow = hT[0:H, 3:7, :]
        zrow = small_piece(2560, 256, H)
        rows = small_piece(1536, 512, H).rearrange("p (s t) -> p s t", s=2)
        rcol = sb("rcol", [P, 2, H])
        wlog = small_piece(0, 512).rearrange("p (s t) -> p s t", s=2)
        sT = small_piece(512, 512).rearrange("p (s t) -> p s t", s=2)
        en_b = small_piece(1024, 256)
        den = small_piece(1280, 256)
        prow2 = kT.rearrange("p c t -> p (c t)")[:, 0:P]
        pc2 = sb("pc2", [P, 28])
        pe_T = sb("pe_T", [P, 2, CMP_LEN])
        pe_raw = kT.rearrange("p c t -> p (c t)")[0:CMP_LEN, 256:512].rearrange("p (m h d) -> p m h d", m=2, h=2)
        wgn = small_piece(0, 384).rearrange("p (k n) -> p k n", k=CT)
        bgate = small_piece(448, 96).rearrange("p (s n) -> p s n", s=2)
        has = sb("has", [P, 1])
        cmpc = small_piece(384, 60).rearrange("p (m g c) -> p m g c", m=2, g=2)
        vc = small_piece(544, 256, NCMP).rearrange("p (g e) -> p g e", g=2)
        pcmp = small_piece(800, 120).rearrange("p (b r c) -> p b r c", b=2, r=R)
        pcmpT = small_piece(920, 512, NCMP).rearrange("p (r t) -> p r t", r=R)
        stat = small_piece(1432, 72).rearrange("p (b n m r) -> p b n m r", b=2, n=3, m=3)
        rc = piece(19456 + 2048 + 2048 + 0, 1024).rearrange("p (g t) -> p g t", g=4)
        mstat = sb("mstat", [P, 2, 2])
        top_v = small_piece(0, 256).rearrange("p (c k) -> p c k", k=TOPK)
        top_i = small_piece(256, 256).bitcast(U32).rearrange("p (c k) -> p c k", k=TOPK)
        top_f = small_piece(512, 256).rearrange("p (c k) -> p c k", k=TOPK)
        best = small_piece(768, 128).rearrange("p (c k) -> p c k", k=TOPK)
        pos = small_piece(896, 128).bitcast(U32).rearrange("p (c k) -> p c k", k=TOPK)
        half = small_piece(1024, 256).bitcast(U32).rearrange("p (c k) -> p c k", c=2)
        half_f = small_piece(1280, 256).rearrange("p (c k) -> p c k", c=2)
        part = small_piece(1536, 256).rearrange("p (c k) -> p c k", c=2)
        ids = small_piece(1792, 256).bitcast(U32).rearrange("p (c k) -> p c k", c=2)
        gate = small_piece(2048, 256).rearrange("p (s h k) -> p s h k", s=2, k=TOPK)
        gsum = sb("gsum", [P, PH])
        dots = small_piece(2304, 256).rearrange("p (s h k) -> p s h k", s=2, k=TOPK)
        wgt = small_piece(2560, 256).rearrange("p (s h k) -> p s h k", s=2, k=TOPK)
        iota16 = sb("iota16", [P, TOPK])
        bias_dram = nc.dram_tensor("bias_dram", (P, NH, 512), F32, kind="Internal").ap()

        pj = [ctx.enter_context(nc.psum_tensor(f"pj{i}", [P, 2, T], F32)) for i in range(2)]
        st = ctx.enter_context(nc.psum_tensor("st", [P, CT, T], F32))
        ms = [ctx.enter_context(nc.psum_tensor(f"ms{i}", [P, 2, T], F32)) for i in range(2)]

        sems = {}

        def sem(name):
            if name not in sems:
                sems[name] = ctx.enter_context(nc.semaphore(name))
            return sems[name]

        ring_full = [sem(f"ring_full{i}") for i in range(RING)]
        jobs = weight_jobs()
        job_at = {j: n for n, j in enumerate(jobs)}
        full_at = []
        for n, j in enumerate(jobs):
            before = full_at[n - RING] if n >= RING else 0
            full_at.append(before + (64 if j[0] in ("q0", "q1", "q2", "q3") else 16))

        MERGE_BANKS, GATE_BANK, banks = [], None, 64 * DEPTH
        for j in jobs[job_at[("kcmp", 2, 0)]:job_at[("vwin", 2, 0)] + 1]:
            banks += 1
        banks += 1
        GATE_BANK = banks
        banks += 6
        for (g, s), names in zip(UNITS, FILL):
            for name in names:
                if name[:8] == "pool_out":
                    MERGE_BANKS += [banks % 2, (banks + 1) % 2]
                    banks += 2
                else:
                    banks += 2 if name == "mix" else 1
            banks += 3 if g == "x" else 2 * (s + 1) + 2
        MERGE_BANKS += [(banks + k) % 2 for k in range(12)]

        block = ctx.enter_context(nc.Block())

        @block.sync
        def _(sp):
            def load_params(l):
                r = prow[:, l]
                for dst, n, src in (
                    (B_ADA, 48, a["b_ada"]), (G_PRE_MIX, 8, a["g_pre_mix"]), (G_PRE_MLP, 8, a["g_pre_mlp"]),
                    (G_POST_MIX, 8, a["g_post_mix"]), (G_POST_MLP, 8, a["g_post_mlp"]), (B_CONV_M, 8, a["b_conv_m"]),
                    (G_MH, 8, a["g_mh"]), (B_DW, 8, a["b_dw"]), (G_CN, 8, a["g_cn"]), (B_CN, 8, a["b_cn"]),
                ):
                    sp.dma_start(r[dst:dst + n, 0, :], src[l].rearrange("(r q) -> r q", q=P)).then_inc(sem("params_in"), 16)
                sp.dma_start(r[C_COL:C_COL + 8, 0, :], a["c"][0].rearrange("(r q) -> r q", q=P)).then_inc(sem("params_in"), 16)
                wdw = a["w_dw"][l].rearrange("k (c q) -> (k c) q", q=P)
                sp.dma_start(r[:, 1, :], wdw[0:P, :]).then_inc(sem("params_in"), 16)
                sp.dma_start(r[0:120, 2, :], wdw[P:248, :]).then_inc(sem("params_in"), 16)
                sp.dma_start(r[0:32, 3, :], a["w_conv_m"][l].rearrange("k (c q) -> (k c) q", q=P)).then_inc(sem("params_in"), 16)

            sp.dma_start(x_tok, a["x"][0].rearrange("(s p) d -> p s d", p=P)).then_inc(sem("x_in"), 16)
            for l in range(DEPTH):
                load_params(l)

            def load_layer(l):
                if l:
                    sp.wait_ge(sem("qkv_made"), 16 * l)
                    sp.wait_ge(sem("gates_made"), l)
                for m, w in enumerate((a["w_q"], a["w_k"], a["w_v"])):
                    sp.dma_start(wqkv[:, m], w[l].rearrange("h (c p) e -> p (h c) e", p=P)).then_inc(sem("wqkv_in"), 16)
                sp.dma_start(wg[:, :, :], a["w_gates"][l].rearrange("(j p h) g -> p j (h g)", p=P, h=H)).then_inc(sem("wg_in"), 16)
                sp.dma_start(bg[:, :], a["b_gates"][l].rearrange("(g o) -> g o", o=1)).then_inc(sem("wg_in"), 16)

            for lo, n, src in ((G_MIX2, 8, a["g_mix_2"][0]), (G_MEM2, 8, a["g_mem_2"][0]), (G_FFN2, 8, a["g_ffn_2"][0]),
                               (POOL_SC2, 4, a["pool_scale_2"][0])):
                sp.dma_start(prow2[lo:lo + n, :], src.rearrange("(r q) -> r q", q=P)).then_inc(sem("params2_in"), 16)
            for m, src in enumerate((a["pe_k_2"][0], a["pe_v_2"][0])):
                for h in range(2):
                    sp.dma_start(pe_raw[:, m, h, :], src).then_inc(sem("params2_in"), 16)

            for n, (name, l, j) in enumerate(jobs):
                if n >= RING:
                    sp.wait_ge(sem("slot_used"), n - RING + 1)
                dst = ring[:, n % RING, :]
                if name in ("w_in", "w_ff1"):
                    src = a[name][l].rearrange("(k p) n -> p k n", p=P)[:, :, 256 * j:256 * j + 256]
                    dst = dst.rearrange("p (k n) -> p k n", n=256)
                elif name == "w_out":
                    src = a[name][l].rearrange("(k p) n -> p k n", p=P)[:, :, P * j:P * j + P]
                    dst = dst.rearrange("p (k n) -> p k n", n=P)
                elif name in ("q0", "q1", "q2", "q3"):
                    gp, rp = divmod(int(name[1]), 2)
                    w = a["w_in_2"][0].rearrange("(k p) n -> p k n", p=P)
                    dst = dst.rearrange("p (k r h d) -> p k r h d", r=2, h=2, d=HD)
                    for r in range(2):
                        for hf in range(2):
                            c = 512 + 256 * (2 * gp + hf) + P * rp + HD * r
                            sp.dma_start(dst[:, :, r, hf, :], w[:, :, c:c + HD]).then_inc(ring_full[n % RING], 16)
                    continue
                elif l == 2:
                    src = second_weight(a, name)
                    dst = dst.rearrange("p (k n) -> p k n", n=src.shape[2])
                else:
                    src = a[name][l].rearrange("(k p) n -> p k n", p=P)[:, 16 * (j % 2):16 * (j % 2) + 16, P * (j // 2):P * (j // 2) + P]
                    dst = dst.rearrange("p (k n) -> p k n", n=P)
                sp.dma_start(dst, src).then_inc(ring_full[n % RING], 16)
                if name == "w_in" and j == 11:
                    load_layer(l)

            sp.wait_ge(sem("slot_used"), len(jobs))
            sp.dma_start(g_fin, a["g_final_2"].partition_broadcast(P)).then_inc(sem("g_fin_in"), 16)
            for s in range(2):
                sp.wait_ge(sem("out_ready"), s + 1)
                sp.dma_start(out[0, P * s:P * s + P, :], h_tok[:, s, :]).then_inc(sem("out_done"), 16)
            sp.wait_ge(sem("out_done"), 32)

        @block.gpsimd
        def _(pool):
            nc.gpsimd.memset(ident[:, :], 0.0).then_inc(sem("pool_c"), 1)
            nc.gpsimd.memset(causal[:, :, :], 0.0).then_inc(sem("pool_c"), 1)
            nc.gpsimd.memset(pick[:, :, :], 0.0).then_inc(sem("pool_c"), 1)
            nc.gpsimd.memset(ones[:, :], 1.0)
            nc.gpsimd.memset(eps_col[:, :], EPS)
            nc.gpsimd.memset(zrow[:, :], 0.0).then_inc(sem("pool_c"), 1)
            pool.wait_ge(sem("pool_c"), 4)
            nc.gpsimd.affine_select(out=ident[:, :], in_=ident[:, :], compare_op=ALU.not_equal, fill=1.0, base=0,
                                    pattern=[[-1, P]], channel_multiplier=1)
            nc.gpsimd.affine_select(out=causal[:, :, :], in_=causal[:, :, :], compare_op=ALU.is_ge, fill=NEG, base=0,
                                    pattern=[[-P, 2], [1, T]], channel_multiplier=-1)
            nc.gpsimd.affine_select(out=pick[:, :, :], in_=pick[:, :, :], compare_op=ALU.not_equal, fill=1.0, base=0,
                                    pattern=[[-1, H], [0, P]], channel_multiplier=1).then_inc(sem("consts"), 1)

            nc.gpsimd.memset(has[:, :], 1.0).then_inc(sem("pool_c"), 1)
            pool.wait_ge(sem("pool_c"), 5)
            nc.gpsimd.affine_select(out=has[:, :], in_=has[:, :], compare_op=ALU.is_ge, fill=0.0, base=-(CMP_LEN - 1),
                                    pattern=[[0, 1]], channel_multiplier=1)
            nc.gpsimd.iota(iota16[:, :], pattern=[[1, TOPK]], base=0, channel_multiplier=0,
                           allow_small_or_imprecise_dtypes=True).then_inc(sem("consts2"), 1)

            def load(n):
                l, j = divmod(n, ADA_CHUNKS)
                src = a["w_ada"][l].rearrange("(k p) n -> p k n", p=P)[:, :, 256 * j:256 * j + 256]
                pool.dma_start(ada_in[:, n % 2], src).then_inc(sem(f"ada_full{n % 2}"), 16)

            total = DEPTH * ADA_CHUNKS
            load(0)
            pool.wait_ge(sem("c_ready"), 1)
            step = 0
            for n in range(total):
                if n + 1 < total:
                    load(n + 1)
                l, j = divmod(n, ADA_CHUNKS)
                pool.wait_ge(sem(f"ada_full{n % 2}"), 16 * (n // 2 + 1))
                if l and j == 0:
                    pool.wait_ge(sem("mod_summed"), l)
                acc = ada_acc[:, 256 * j:256 * j + 256]
                w = ada_in[:, n % 2]
                c_wide = c_act[:, :].unsqueeze(2).broadcast_to([P, CT, 256])
                for dst, x0, x1, op in ((w, w, c_wide, ALU.mult), (w[:, 0:4], w[:, 0:4], w[:, 4:8], ALU.add),
                                        (w[:, 0:2], w[:, 0:2], w[:, 2:4], ALU.add), (acc, w[:, 0], w[:, 1], ALU.add)):
                    nc.gpsimd.tensor_tensor(dst, x0, x1, op).then_inc(sem("ada_step"), 1)
                    step += 1
                    pool.wait_ge(sem("ada_step"), step)

            pool.wait_ge(sem("mod_summed"), DEPTH)
            pool.dma_start(memtok, a["mem_2"][0].rearrange("(s p) d -> p s d", p=P)).then_inc(sem("mem_in"), 16)
            pool.wait_ge(sem("qkv_made"), 16 * DEPTH)
            pool.dma_start(onehot[0:N_BUCKETS, :], a["onehot"]).then_inc(sem("bias_in"), 16)
            pool.dma_start(rel[0:N_BUCKETS, :], a["rel_bias_2"]).then_inc(sem("bias_in"), 16)
            pool.wait_ge(sem("mix_ready"), DEPTH)
            pool.dma_start(wgn[:, :, :], a["w_in_2"][0].rearrange("(k p) n -> p k n", p=P)[:, :, GN0:GN0 + 48]).then_inc(sem("wgn_in"), 16)
            for m, w in enumerate((a["w_cmp_k_2"], a["w_cmp_v_2"])):
                for h in range(2):
                    pool.dma_start(wcmp[HD * h:HD * h + HD, m], w[0].rearrange("(i d) e -> d i e", d=HD)).then_inc(sem("wcmp_in"), 16)
            pool.wait_ge(sem("bias_masked"), 1)
            pool.wait_ge(sem("bias_copied"), 1)
            pool.dma_start(bias_dram.rearrange("p h u -> h p u"), bias_w[0:NH, :].unsqueeze(1).broadcast_to([NH, P, 512])).then_inc(sem("bias_out"), 16)
            pool.wait_ge(sem("bias_out"), 16)
            for s in range(2):
                n = P * (s + 1)
                src = bass.AP(tensor=bias_dram.tensor, offset=255 - P * s, ap=[[NH * 512 - 1, P], [512, NH], [1, n]])
                pool.dma_start(bias[s], src).then_inc(sem("toeplitz_in"), 16)
            pool.wait_ge(sem("memT_ready"), 1)
            pool.dma_start(rc, a["rcount"].partition_broadcast(P)).then_inc(sem("rcount_in"), 16)
            pool.wait_ge(sem("x_ready"), 2 * DEPTH)
            pool.dma_start(wpg[:, :, :], a["w_pool_grp_2"][0].rearrange("g c d -> c g d")).then_inc(sem("wpg_in"), 16)
            pool.wait_ge(sem("attention_done"), 1)
            pool.dma_start(sub_raw, a["peer_sub_keys_2"][0].rearrange("h p k c -> k (h p) c")).then_inc(sem("sub_in"), 16)

            total = 2 * PH * TOPK
            for n in range(total + LAG):
                for table, buf, name, m in ((a["peer_u_2"], ubuf, "u", n), (a["peer_v_2"], vbuf, "v", n - LAG)):
                    if not 0 <= m < total:
                        continue
                    s, k = divmod(m, PH * TOPK)
                    if name == "u" and k == 0:
                        pool.wait_ge(sem("ids_ready"), s + 1)
                    if m >= NBUF:
                        pool.wait_ge(sem(f"{name}_used"), m - NBUF + 1)
                    nc.gpsimd.indirect_dma_start(
                        out=buf[:, m % NBUF, :], out_offset=None, in_=table[0],
                        in_offset=bass.IndirectOffsetOnAxis(ap=ids[:, s, k:k + 1], axis=0)).then_inc(sem(f"{name}_row{m % NBUF}"), 16)

        @block.tensor
        def _(pe):
            bank = 0
            emptied = {"proj_drained": 0, "merge_drained": 0}
            emptied_at = []

            def take_bank(by="proj_drained"):
                nonlocal bank
                if bank >= 2:
                    pe.wait_ge(sem(emptied_at[bank - 2][0]), emptied_at[bank - 2][1])
                emptied[by] += 1
                emptied_at.append((by, emptied[by]))
                bank += 1
                return pj[(bank - 1) % 2]

            def ring_slot(job):
                n = job_at[job]
                pe.wait_ge(ring_full[n % RING], full_at[n])
                return ring[:, n % RING, :]

            pe.wait_ge(sem("consts"), 1)
            pe.wait_ge(sem("x_in"), 16)
            for c in range(CT):
                for s in range(2):
                    i = nc.tensor.transpose(st[:, c, P * s:P * s + P], x_tok[:, s, P * c:P * c + P], ident[:, :])
            i.then_inc(sem("x_turned"), 1)
            pe.wait_ge(sem("params_in"), 16 * 14 * DEPTH)
            for l in range(DEPTH):
                b = ms[l][:, :, :].rearrange("p s t -> p (s t)")
                for k, n, c0 in ((0, P, 0), (1, P, W_DW), (2, 120, W_DW + P), (3, 32, W_CONV)):
                    i = nc.tensor.transpose(b[:, c0:c0 + n], prow[0:n, l, k, :], ident[0:n, 0:n])
                i.then_inc(sem("params_turned"), 1)

            pe.wait_ge(sem("params2_in"), 16 * 8)
            pe.wait_ge(sem("params_kept"), 1)
            nc.tensor.transpose(ms[0][:, 0, 0:28], prow2[0:28, :], ident[0:28, 0:28])
            for m in range(2):
                i = nc.tensor.transpose(ms[0][:, 1, CMP_LEN * m:CMP_LEN * m + CMP_LEN], pe_raw[:, m].rearrange("p h d -> p (h d)"),
                                        ident[0:CMP_LEN, 0:CMP_LEN])
            i.then_inc(sem("params2_turned"), 1)
            norms = 0

            def norm_sum():
                nonlocal norms
                pe.wait_ge(sem("squares"), norms + 1)
                for c in range(CT):
                    i = nc.tensor.matmul(ms[0][:, 0, :], ones[:, :], tmp[:, c, :], start=(c == 0), stop=(c == CT - 1))
                i.then_inc(sem("norm_summed"), 1)
                norms += 1

            h_waits = 0

            def wide(name, l, js, first_wait):
                for j in js:
                    w = ring_slot((name, l, j)).rearrange("p (k n) -> p k n", n=256)
                    b = take_bank()
                    for m in range(2):
                        for k in range(CT):
                            if j == js[0] and m == 0:
                                pe.wait_ge(sem("h_ready"), first_wait + k + 1)
                            i = nc.tensor.matmul(b[:, m, :], w[:, k, P * m:P * m + P], hT[:, k, :], start=(k == 0), stop=(k == CT - 1))
                            if m == 1 and k == CT - 1:
                                i.then_inc(sem("slot_used"), 1)

            for l in range(DEPTH):
                pe.wait_ge(sem("ada_step"), 4 * ADA_CHUNKS * (l + 1))
                if l == 0:
                    pe.wait_ge(sem("params_kept"), 2)
                if l:
                    pe.wait_ge(sem("x_ready"), 2 * l)
                for m in range(48):
                    i = nc.tensor.matmul(ms[1][:, 0, m:m + 1], ada_acc[:, P * m:P * m + P], ones[:, 0:1], start=True, stop=True)
                i.then_inc(sem("mod_summed"), 1)
                norm_sum()
                wide("w_in", l, list(range(8, 16)) + list(range(0, 8)), 16 * l)

                pe.wait_ge(sem("wqkv_in"), 48 * (l + 1))
                pe.wait_ge(sem("proj_drained"), bank)
                for m in (2, 0, 1):
                    if m == 0:
                        pe.wait_ge(sem("xc_ready"), l + 1)
                    for h in range(H):
                        b = take_bank()
                        for e in range(2):
                            for d in range(2):
                                src = U if m == 2 else xc
                                i = nc.tensor.matmul(b[:, e, :], wqkv[:, m, 2 * h + d, P * e:P * e + P], src[:, 2 * h + d, :],
                                                     start=(d == 0), stop=(d == 1))
                        i.then_inc(sem("qkv_made"), 1)
                    if m == 2:
                        for s in range(2):
                            for hp in range(2):
                                b = take_bank()
                                for h in range(2):
                                    for d in range(2):
                                        c = 2 * (2 * hp + h) + d
                                        i = nc.tensor.matmul(b[:, h, :], U[:, c, P * s:P * s + P], wqkv[:, 2, c, :],
                                                             start=(d == 0), stop=(d == 1))
                                i.then_inc(sem("qkv_made"), 1)

                pe.wait_ge(sem("wg_in"), 32 * (l + 1))
                pe.wait_ge(sem("proj_drained"), bank)
                n = 0
                for m, src in enumerate((qT, kT, vT)):
                    for e in range(2):
                        for h in range(H):
                            i = nc.tensor.matmul(ms[0][0:2 * H, 0, :], wg[:, 2 * m + e, 8 * h:8 * h + 8], src[:, 2 * h + e, :],
                                                 start=(n == 0), stop=(n == 23))
                            n += 1
                i.then_inc(sem("gates_made"), 1)
                pe.wait_ge(sem("gates_kept"), l + 1)
                nc.tensor.matmul(ms[0][0:H, 1, :], ident[0:2 * H, H:2 * H], gates[:, :], start=True, stop=True).then_inc(sem("fg_moved"), 1)

                pe.wait_ge(sem("rows_ready"), l + 1)
                for s in range(2):
                    i = nc.tensor.transpose(ms[0][:, 0, H * s:H * s + H], lrow[:, 2, P * s:P * s + P], ident[0:H, 0:H])
                i.then_inc(sem("r_turned"), 1)

                def group_sum(src, name):
                    for c in range(CT):
                        i = nc.tensor.matmul(st[:, c, :], ones[:, :], src[:, c, :], start=True, stop=True)
                    i.then_inc(sem(name), 1)

                for h in range(H):
                    hn = l * H + h
                    if hn:
                        pe.wait_ge(sem("head_done"), hn)
                    if h == 0:
                        pe.wait_ge(sem("rcol_kept"), l + 1)
                        if l:
                            pe.wait_ge(sem("gn_centred"), 4 * l)
                    nc.tensor.matmul(ms[0][:, :, :].rearrange("p a t -> p (a t)"), pick[:, h, :],
                                     rows[:, :, :].rearrange("p a t -> p (a t)"), start=True, stop=True).then_inc(sem("rows_spread"), 1)
                    for s in range(2):
                        t0 = P * s
                        for d in range(2):
                            i = nc.tensor.matmul(ms[1][:, s, t0:T], kT[:, 2 * h + d, P * s:P * s + P], qT[:, 2 * h + d, t0:T],
                                                 start=(d == 0), stop=(d == 1))
                    i.then_inc(sem("scores_made"), 1)
                    pe.wait_ge(sem("s_ready"), hn + 1)
                    for s in range(2):
                        i = nc.tensor.matmul(st[:, 4, P * s:T], ones[:, :], sT[:, s, P * s:T], start=(s == 0), stop=(s == 1))
                    for e in range(2):
                        for s in range(2):
                            i = nc.tensor.matmul(st[:, 6 + e, P * s:T], vtok[:, s, DH * h + P * e:DH * h + P * e + P], sT[:, s, P * s:T],
                                                 start=(s == 0), stop=(s == 1))
                    i.then_inc(sem("num_made"), 1)

                pe.wait_ge(sem("head_done"), (l + 1) * H)
                for h in range(H):
                    for e in range(2):
                        i = nc.tensor.matmul(st[:, h, :], ones[:, :], tmp[:, 2 * h + e, :], start=(e == 0), stop=(e == 1))
                i.then_inc(sem("hm_summed"), 1)
                pe.wait_ge(sem("hm_squared"), l + 1)
                for h in range(H):
                    for e in range(2):
                        i = nc.tensor.matmul(st[:, H + h, :], ones[:, :], hT[:, 2 * h + e, :], start=(e == 0), stop=(e == 1))
                i.then_inc(sem("hm_summed"), 1)
                pe.wait_ge(sem("hm_done"), l + 1)

                pe.wait_ge(sem("conv_ready"), l + 1)
                group_sum(U[:, 16:24], "gn_summed")
                pe.wait_ge(sem("gn_squared"), l + 1)
                group_sum(tmp, "gn_summed")

                pe.wait_ge(sem("mix_ready"), l + 1)
                for j in range(8):
                    w = ring_slot(("w_out", l, j)).rearrange("p (k n) -> p k n", n=P)
                    b = take_bank()
                    for k in range(16):
                        i = nc.tensor.matmul(b[:, 0, :], w[:, k, :], U[:, 8 + k, :], start=(k == 0), stop=(k == 15))
                    i.then_inc(sem("slot_used"), 1)
                norm_sum()
                norm_sum()
                wide("w_ff1", l, list(range(16)), 16 * l + 8)
                pe.wait_ge(sem("proj_drained"), bank)
                for j in range(16):
                    w = ring_slot(("w_ff2", l, j)).rearrange("p (k n) -> p k n", n=P)
                    if j % 2 == 0:
                        b = take_bank()
                    for k in range(16):
                        kk = 16 * (j % 2) + k
                        i = nc.tensor.matmul(b[:, 0, :], w[:, k, :], U[:, kk, :], start=(kk == 0), stop=(kk == 31))
                    i.then_inc(sem("slot_used"), 1)
                if l == DEPTH - 1:
                    pe.wait_ge(sem("mem_scaled"), 1)
                    for c in range(CT):
                        for s in range(2):
                            i = nc.tensor.transpose(st[:, c, P * s:P * s + P], memtok[:, s, P * c:P * c + P], ident[:, :])
                    i.then_inc(sem("mem_turned"), 1)
                    pe.wait_ge(sem("bias_in"), 32)
                    nc.tensor.matmul(ms[1][0:NH, :, :].rearrange("p a t -> p (a t)"), rel[0:N_BUCKETS, :], onehot[0:N_BUCKETS, :],
                                     start=True, stop=True).then_inc(sem("bias_made"), 1)
                norm_sum()

            def second_slot(name):
                return ring_slot((name, 2, 0))

            def columns(name, src, h_first=False, by="proj_drained", k_tiles=CT, tiles=(0, 1), last=True):
                w = second_slot(name).rearrange("p (k n) -> p k n", k=k_tiles)
                b = take_bank(by)
                for n, m in enumerate(tiles):
                    for k in range(k_tiles):
                        if h_first and n == 0:
                            pe.wait_ge(sem("h_ready"), 4 * CT + k + 1)
                        i = nc.tensor.matmul(b[:, n, :], w[:, k, P * m:P * m + P], src[:, k, :], start=(k == 0), stop=(k == k_tiles - 1))
                if last:
                    i.then_inc(sem("slot_used"), 1)
                else:
                    i.then_inc(sem("half_slot"), 1)

            def tokens(name, src):
                w = second_slot(name).rearrange("p (k n) -> p k n", k=CT)
                b = take_bank()
                for n in range(2):
                    for k in range(CT):
                        i = nc.tensor.matmul(b[:, n, :], src[:, k, P * n:P * n + P], w[:, k, :], start=(k == 0), stop=(k == CT - 1))
                i.then_inc(sem("slot_used"), 1)

            norm_sum()
            columns("kcmp", hT, h_first=True)
            columns("vcmp", hT)
            for j in range(4):
                w = second_slot(f"q{j}").rearrange("p (k r n) -> p k r n", k=CT, r=2)
                b = take_bank()
                for r in range(2):
                    for k in range(CT):
                        i = nc.tensor.matmul(b[:, r, :], w[:, k, r, :], hT[:, k, :], start=(k == 0), stop=(k == CT - 1))
                i.then_inc(sem("slot_used"), 1)
            columns("ksel", hT)
            tokens("vsel", hT)
            columns("kwin", hT)
            tokens("vwin", hT)
            pe.wait_ge(sem("wgn_in"), 16)
            b = take_bank()
            for s in range(2):
                for k in range(CT):
                    i = nc.tensor.matmul(b[:, 0, 48 * s:48 * s + 48], hT[:, k, P * s:P * s + P], wgn[:, k, :], start=(k == 0), stop=(k == CT - 1))
            i.then_inc(sem("bgate_made"), 1)
            pe.wait_ge(sem("wcmp_in"), 64)
            pe.wait_ge(sem("blk_ready"), 1)
            for m in range(2):
                for h in range(2):
                    lo = HD * h
                    for i_ in range(CMP_LEN):
                        i = nc.tensor.matmul(ms[1][lo:lo + HD, 0, 32 * m:32 * m + 2 * NCMP].rearrange("p (g c) -> p g c", g=2),
                                             wcmp[lo:lo + HD, m, i_, :], blk[lo:lo + HD, m, :, :, i_],
                                             start=(i_ == 0), stop=(i_ == CMP_LEN - 1))
            i.then_inc(sem("cmp_made"), 1)
            columns("qx0", hT)
            columns("qx1", hT)
            pe.wait_ge(sem("cmp_kept"), 1)
            for g in range(2):
                i = nc.tensor.transpose(ms[1][0:NCMP, 1, P * g:P * g + P], cmpc[:, 1, g, :], ident[:, :])
            i.then_inc(sem("vc_turned"), 1)
            pe.wait_ge(sem("memT_ready"), 1)
            columns("memk0", memT)
            columns("memk1", memT)
            tokens("memv0", memT)
            tokens("memv1", memT)

            def scores(u):
                g, s = UNITS[u]
                if u:
                    pe.wait_ge(sem("scores_kept"), u)
                if g == "x":
                    for h in range(XH):
                        i = nc.tensor.matmul(st[:, h, :], qxT[:, h, P * s:P * s + P], kxT[:, h, :], start=True, stop=True)
                    i.then_inc(sem("scores2_made"), 1)
                    return
                gp, lo, n = g // 2, HD * (g % 2), P * (s + 1)
                for m in range(2):
                    for r in range(R):
                        nc.tensor.matmul(st[:, R * m + r, 0:n], q2T[lo:lo + HD, R * gp + r, P * s:P * s + P], kselT[lo:lo + HD, m, gp, 0:n],
                                         start=True, stop=True)
                for r in range(R):
                    i = nc.tensor.matmul(ms[0][:, 0, 16 * r:16 * r + NCMP], q2T[lo:lo + HD, R * gp + r, P * s:P * s + P],
                                         cmpc[lo:lo + HD, 0, gp, :], start=True, stop=True)
                i.then_inc(sem("scores2_made"), 1)

            def turn(u):
                g, s = UNITS[u]
                pb = probs[u % 2]
                pe.wait_ge(sem("probs_ready"), u + 1)
                for m in range(1 if g == "x" else 2):
                    for j in range(2 if g == "x" else s + 1):
                        b = take_bank().rearrange("p a t -> p (a t)")
                        for r in range(R):
                            i = nc.tensor.transpose(b[:, P * r:P * r + P], pb[:, m, r, P * j:P * j + P], ident[:, :])
                        i.then_inc(sem("turned"), 1)
                if g != "x":
                    nb = NCMP if s else NCMP // 2
                    b = take_bank().rearrange("p a t -> p (a t)")
                    for r in range(R):
                        i = nc.tensor.transpose(b[0:nb, P * r:P * r + P], pcmp[:, u % 2, r, 0:nb], ident[:, :])
                    i.then_inc(sem("turned"), 1)

            def values(u):
                g, s = UNITS[u]
                b = take_bank()
                pe.wait_ge(sem("turned_kept"), u + 1)
                if g == "x":
                    o = b.rearrange("p a t -> p (a t)")
                    for h in range(XH):
                        for j in range(2):
                            i = nc.tensor.matmul(o[:, P * h:P * h + P], vx[:, j, P * h:P * h + P], probsT[:, 0, j, h, :], start=(j == 0), stop=(j == 1))
                    i.then_inc(sem("o_made"), 1)
                    return
                nb = NCMP if s else NCMP // 2
                gp, lo = g // 2, HD * (g % 2)
                for hf in range(2):
                    o = b[HD * hf:HD * hf + HD, 0, :].rearrange("p (a t) -> p a t", a=2)
                    for m in range(2):
                        for j in range(s + 1):
                            nc.tensor.matmul(o, v2[:, m, j, HD * g:HD * g + HD], probsT[:, m, j, hf:R:2, :], start=(m == 0 and j == 0), stop=False)
                    i = nc.tensor.matmul(o, vc[0:nb, gp, lo:lo + HD], pcmpT[0:nb, hf:R:2, :], start=False, stop=True)
                i.then_inc(sem("o_made"), 1)

            pe.wait_ge(sem("vc_kept"), 1)
            pe.wait_ge(sem("vx_kept"), 1)
            scores(0)
            for u in range(len(UNITS)):
                if u + 1 < len(UNITS):
                    scores(u + 1)
                for name in FILL[u]:
                    if name == "mix":
                        pe.wait_ge(sem("wpg_in"), 16)
                        pe.wait_ge(sem("pooled"), 1)
                        for m in range(2):
                            b = take_bank()
                            for k in range(2):
                                i = nc.tensor.matmul(b[:, k, :], wpg[:, 2 * m + k, :], win[0][:, 2 * m + k, :], start=True, stop=True)
                            i.then_inc(sem("mixed"), 1)
                    elif name[:8] == "pool_out":
                        pe.wait_ge(sem("mix_kept"), 1)
                        columns(name, poolT, by="merge_drained", k_tiles=4, last=False)
                        columns(name, poolT, by="merge_drained", k_tiles=4, tiles=(2, 3))
                    else:
                        columns(name, hT)
                turn(u)
                values(u)
            pe.wait_ge(sem("o_kept"), len(UNITS))
            for j in range(4):
                columns(f"nsa_out{j}", oT, by="merge_drained")
            for j in range(2):
                columns(f"x_out{j}", oxT, by="merge_drained", k_tiles=4, last=False)
                columns(f"x_out{j}", oxT, by="merge_drained", k_tiles=4, tiles=(2, 3))
            pe.wait_ge(sem("merge_drained"), 12)
            for j in range(4):
                columns(f"w_o{j}", merged, by="merge_drained")
            pe.wait_ge(sem("sub_in"), 16)
            for c in range(2 * PH):
                i = nc.tensor.transpose(st[:, c // 2, P * (c % 2):P * (c % 2) + P], sub_raw[:, c, :], ident[:, :])
            i.then_inc(sem("sub_turned"), 1)
            norm_sum()
            for j in range(8):
                w = second_slot(f"peer_q{j}").rearrange("p (k n) -> p k n", k=CT)
                b = take_bank()
                for m in range(2):
                    for k in range(CT):
                        if j == 0 and m == 0:
                            pe.wait_ge(sem("h_ready"), 5 * CT + k + 1)
                        i = nc.tensor.matmul(b[:, m, :], w[:, k, P * m:P * m + P], hT[:, k, :], start=(k == 0), stop=(k == CT - 1))
                i.then_inc(sem("slot_used"), 1)
            pe.wait_ge(sem("sub_kept"), 1)
            pe.wait_ge(sem("qp_kept"), 1)
            for s in range(2):
                if s:
                    pe.wait_ge(sem("sub_scores_kept"), s)
                for c in range(2 * PH):
                    i = nc.tensor.matmul(st[:, c // 2, P * (c % 2):P * (c % 2) + P], qpT[:, c, P * s:P * s + P], subT[:, c, :], start=True, stop=True)
                i.then_inc(sem("sub_scores"), 1)
            pe.wait_ge(sem("sub_scores_kept"), 2)
            for n, src in enumerate((hT, xT)):
                if n:
                    pe.wait_ge(sem("tok_kept"), 1)
                for s in range(2):
                    for c in range(CT):
                        i = nc.tensor.transpose(st[:, 4 * s + c // 2, P * (c % 2):P * (c % 2) + P], src[:, c, P * s:P * s + P], ident[:, :])
                i.then_inc(sem("tok_turned"), 1)

        @block.scalar
        def _(act):
            steps = 0

            def link(i):
                nonlocal steps
                steps += 1
                i.then_inc(sem("act_step"), 1)
                act.wait_ge(sem("act_step"), steps)

            act.wait_ge(sem("x_turned"), 1)
            nc.scalar.copy(xT[:, :, :], st[:, :, :]).then_inc(sem("x_kept"), 1)
            for l in range(DEPTH):
                act.wait_ge(sem("params_turned"), l + 1)
                b = ms[l][:, :, :].rearrange("p s t -> p (s t)")
                nc.scalar.copy(pc[:, l, :], b[:, 0:NPC]).then_inc(sem("params_kept"), 1)
            act.wait_ge(sem("params_kept"), 2)
            nc.scalar.activation(c_act[:, :], pc[:, 0, C_COL:C_COL + 8], ACT.Silu).then_inc(sem("c_ready"), 1)
            act.wait_ge(sem("x_kept"), 1)
            act.wait_ge(sem("params2_turned"), 1)
            nc.scalar.copy(pc2[:, :], ms[0][:, 0, 0:28])
            nc.scalar.copy(pe_T[:, :, :].rearrange("p m i -> p (m i)"), ms[0][:, 1, 0:2 * CMP_LEN]).then_inc(sem("params2_kept"), 1)
            act.wait_ge(sem("params2_kept"), 1)

            norms = 0
            bank = 0
            qkv = 0

            def drain(dst, func, n=2, job=None):
                nonlocal bank, qkv
                if job:
                    act.wait_ge(sem("slot_used"), job_at[job] + 1)
                else:
                    qkv += 1
                    act.wait_ge(sem("qkv_made"), qkv)
                i = nc.scalar.activation(dst, pj[bank % 2][:, 0:n, :], func)
                i.then_inc(sem("proj_drained"), 1)
                bank += 1
                return i

            def norm(src):
                nonlocal norms
                nc.scalar.activation(tmp[:, :, :], src[:, :, :], ACT.Square).then_inc(sem("squares"), 1)
                norms += 1
                act.wait_ge(sem("norm_summed"), norms)
                if norms > 1:
                    act.wait_ge(sem("rstd_used"), norms - 1)
                nc.scalar.activation(rstd[:, :], ms[0][:, 0, :], ACT.Sqrt, bias=eps_col[:, 0:1], scale=1.0 / D).then_inc(sem("std_ready"), 1)

            for l in range(DEPTH):
                if l:
                    act.wait_ge(sem("x_ready"), 2 * l)
                norm(xT)
                for j in range(16):
                    c = (16 + 2 * j) % 32
                    drain(U[:, c:c + 2, :], ACT.Sigmoid if c >= 24 or 8 <= c < 16 else ACT.Copy, job=("w_in", l, c // 2))
                for h in range(H):
                    drain(vT[:, 2 * h:2 * h + 2, :], ACT.Copy)
                for s in range(2):
                    for hp in range(2):
                        drain(vtok[:, s, 512 * hp:512 * hp + 512].rearrange("p (a t) -> p a t", a=2), ACT.Copy)
                act.wait_ge(sem("conv_m_ready"), l + 1)
                nc.scalar.activation(xc[:, :, :], xc[:, :, :], ACT.Silu).then_inc(sem("xc_ready"), 1)
                for dst in (qT, kT):
                    for h in range(H):
                        drain(dst[:, 2 * h:2 * h + 2, :], ACT.Copy)

                act.wait_ge(sem("gates_made"), l + 1)
                nc.scalar.activation(gates[:, :], ms[0][0:2 * H, 0, :], ACT.Identity, bias=bg[:, 0:1]).then_inc(sem("gates_kept"), 1)
                act.wait_ge(sem("fg_moved"), l + 1)
                link(nc.scalar.activation(fgr[:, 0, :], ms[0][0:H, 1, :], ACT.Copy))
                link(nc.scalar.activation(fgr[:, 1, :], fgr[:, 0, :], ACT.Abs))
                link(nc.scalar.activation(fgr[:, 1, :], fgr[:, 1, :], ACT.Exp, scale=-1.0))
                nc.scalar.activation(fgr[:, 2, :], fgr[:, 1, :], ACT.Ln, bias=ones[0:H, 0:1]).then_inc(sem("softplus"), 1)
                act.wait_ge(sem("m_ready"), l + 1)
                nc.scalar.activation(rows[:, 1, :], lrow[:, 1, :], ACT.Exp, scale=-1.0).then_inc(sem("rows_ready"), 1)
                act.wait_ge(sem("r_turned"), l + 1)
                nc.scalar.copy(rcol[:, :, :].rearrange("p s h -> p (s h)"), ms[0][:, 0, 0:2 * H]).then_inc(sem("rcol_kept"), 1)

                for h in range(H):
                    hn = l * H + h
                    act.wait_ge(sem("rows_spread"), hn + 1)
                    if hn:
                        act.wait_ge(sem("head_done"), hn)
                    nc.scalar.copy(en_b[:, :], ms[0][:, 1, :]).then_inc(sem("en_kept"), 1)
                    act.wait_ge(sem("wlog_ready"), hn + 1)
                    act.wait_ge(sem("en_kept"), hn + 1)
                    nc.scalar.activation(wlog[:, 0, :], wlog[:, 0, :], ACT.Exp)
                    nc.scalar.activation(wlog[:, 1, P:T], wlog[:, 1, P:T], ACT.Exp).then_inc(sem("w_ready"), 1)

                act.wait_ge(sem("hm_centred"), l + 1)
                nc.scalar.activation(hT[:, :, :], tmp[:, :, :], ACT.Square).then_inc(sem("hm_squared"), 1)
                act.wait_ge(sem("hm_summed"), 2 * l + 2)
                nc.scalar.activation(xc[:, 0:H, :], st[:, H:2 * H, :], ACT.Sqrt, bias=eps_col[:, 0:1], scale=1.0 / DH).then_inc(sem("hm_std"), 1)

                act.wait_ge(sem("gn_centred"), 4 * l + 4)
                nc.scalar.activation(tmp[:, :, :], U[:, 16:24, :], ACT.Square).then_inc(sem("gn_squared"), 1)
                act.wait_ge(sem("gn_summed"), 2 * l + 2)
                nc.scalar.activation(xc[:, :, :], st[:, :, :], ACT.Sqrt, bias=eps_col[:, 0:1], scale=1.0 / P).then_inc(sem("gn_std"), 1)
                act.wait_ge(sem("gn_scaled"), l + 1)
                for c in range(CT):
                    i = nc.scalar.activation(U[:, 16 + c, :], U[:, 16 + c, :], ACT.Silu, bias=pc[:, l, B_CN + c:B_CN + c + 1],
                                             scale=pc[:, l, G_CN + c:G_CN + c + 1])
                i.then_inc(sem("mix_ready"), 1)

                for c in range(CT):
                    drain(y[:, c:c + 1, :], ACT.Copy, 1, ("w_out", l, c))
                act.wait_ge(sem("proj_drained"), bank)
                norm(y)
                act.wait_ge(sem("x_ready"), 2 * l + 1)
                norm(xT)
                for j in range(16):
                    link_dst = U[:, 2 * j:2 * j + 2, :]
                    act.wait_ge(sem("slot_used"), job_at[("w_ff1", l, j)] + 1)
                    link(nc.scalar.activation(link_dst, pj[bank % 2][:, :, :], ACT.Relu))
                    nc.scalar.activation(link_dst, link_dst, ACT.Square).then_inc(sem("proj_drained"), 1)
                    bank += 1
                if l == DEPTH - 1:
                    act.wait_ge(sem("mem_in"), 16)
                    for t in range(2):
                        link(nc.scalar.activation(wqkv_free[:, :], memtok[:, t, :], ACT.Square, accum_out=mstat[:, 0, t:t + 1]))
                    nc.scalar.activation(mstat[:, 1, :], mstat[:, 0, :], ACT.Sqrt, bias=eps_col[:, 0:1], scale=1.0 / D).then_inc(sem("mem_std"), 1)
                for c in range(CT):
                    drain(y[:, c:c + 1, :], ACT.Copy, 1, ("w_ff2", l, 2 * c + 1))
                act.wait_ge(sem("proj_drained"), bank)
                if l == DEPTH - 1:
                    act.wait_ge(sem("mem_turned"), 1)
                    for c in range(CT):
                        i = nc.scalar.activation(memT[:, c, :], st[:, c, :], ACT.Copy, scale=pc2[:, G_MEM2 + c:G_MEM2 + c + 1])
                    i.then_inc(sem("memT_ready"), 1)
                    act.wait_ge(sem("bias_made"), 1)
                    nc.scalar.copy(bias_w[0:NH, 0:T], ms[1][0:NH, 0, :]).then_inc(sem("bias_copied"), 1)
                norm(y)

            def drain2(dst, name, func=ACT.Copy, shape=None):
                nonlocal bank
                act.wait_ge(sem("slot_used"), job_at[(name, 2, 0)] + 1)
                src = pj[bank_of()][:, :, :]
                if shape:
                    src = src.rearrange("p a t -> p (a t)")
                bank += 1
                return nc.scalar.activation(dst, src, func).then_inc(sem("proj_drained"), 1)

            merged_banks = 0

            def bank_of():
                return (bank + merged_banks) % 2

            act.wait_ge(sem("x_ready"), 2 * DEPTH)
            norm(xT)
            drain2(cmpT[:, 0], "kcmp")
            drain2(cmpT[:, 1], "vcmp")
            act.wait_ge(sem("proj_drained"), bank)
            act.sem_inc(sem("cmpT_kept"), 1)
            for j in range(4):
                drain2(q2T[:, 2 * j:2 * j + 2, :], f"q{j}")
            act.wait_ge(sem("bias_out"), 16)
            drain2(kselT[:, 0], "ksel")
            drain2(v2[:, 0], "vsel")
            drain2(kselT[:, 1], "kwin")
            drain2(v2[:, 1], "vwin")
            act.wait_ge(sem("bgate_made"), 1)
            nc.scalar.activation(bgate[:, :, :].rearrange("p s n -> p (s n)"), pj[bank_of()][:, 0, 0:96], ACT.Sigmoid).then_inc(sem("proj_drained"), 1)
            bank += 1
            act.wait_ge(sem("cmp_made"), 1)
            nc.scalar.copy(cmpc[:, 0].rearrange("p g c -> p (g c)"), ms[1][:, 0, 0:2 * NCMP])
            nc.scalar.copy(cmpc[:, 1].rearrange("p g c -> p (g c)"), ms[1][:, 0, 32:32 + 2 * NCMP]).then_inc(sem("cmp_kept"), 1)
            drain2(qxT[:, 0:2, :], "qx0")
            drain2(qxT[:, 2:4, :], "qx1")
            act.wait_ge(sem("vc_turned"), 1)
            nc.scalar.copy(vc[:, :, :].rearrange("p g e -> p (g e)"), ms[1][0:NCMP, 1, :]).then_inc(sem("vc_kept"), 1)
            drain2(kxT[:, 0:2, :], "memk0")
            drain2(kxT[:, 2:4, :], "memk1")
            drain2(vx[:, :, 0:256], "memv0")
            drain2(vx[:, :, 256:512], "memv1")
            act.wait_ge(sem("proj_drained"), bank)
            act.sem_inc(sem("vx_kept"), 1)

            turned = 0
            for u, (g, s) in enumerate(UNITS):
                act.wait_ge(sem("max_ready"), u + 1)
                pb, sv = probs[u % 2], stat[:, u % 2]
                n = P * (s + 1)
                if g == "x":
                    for h in range(XH):
                        i = nc.scalar.activation(pb[:, 0, h, :], pb[:, 0, h, :], ACT.Exp, bias=sv[:, 0, 1, h:h + 1], accum_out=sv[:, 1, 1, h:h + 1])
                else:
                    nb = NCMP if s else NCMP // 2
                    for r in range(R):
                        nc.scalar.activation(pcmp[:, u % 2, r, 0:nb], pcmp[:, u % 2, r, 0:nb], ACT.Exp, bias=sv[:, 0, 0, r:r + 1], accum_out=sv[:, 1, 0, r:r + 1])
                        for m in range(2):
                            i = nc.scalar.activation(pb[:, m, r, 0:n], pb[:, m, r, 0:n], ACT.Exp, bias=sv[:, 0, 1 + m, r:r + 1], accum_out=sv[:, 1, 1 + m, r:r + 1])
                i.then_inc(sem("exp_done"), 1)
                for name in FILL[u]:
                    if name[:2] == "gm":
                        j = int(name[2:])
                        drain2(gm[:, 2 * j:2 * j + 2, :], name, ACT.Sigmoid)
                    elif name == "mix":
                        for m in range(2):
                            act.wait_ge(sem("mixed"), m + 1)
                            for k in range(2):
                                c = 2 * m + k
                                i = nc.scalar.activation(poolT[:, c, :], pj[bank_of()][:, k, :], ACT.Copy, scale=pc2[:, POOL_SC2 + c:POOL_SC2 + c + 1])
                            i.then_inc(sem("proj_drained"), 1)
                            bank += 1
                        act.wait_ge(sem("proj_drained"), bank)
                        act.sem_inc(sem("mix_kept"), 1)
                    elif name[:8] == "pool_out":
                        merged_banks += 2
                    else:
                        j = int(name[4:])
                        drain2(poolT[:, 2 * j:2 * j + 2, :], name)
                        if j == 1:
                            act.wait_ge(sem("proj_drained"), bank)
                            act.sem_inc(sem("pool_kept"), 1)
                for m in range(1 if g == "x" else 2):
                    for j in range(2 if g == "x" else s + 1):
                        turned += 1
                        act.wait_ge(sem("turned"), turned)
                        nc.scalar.copy(probsT[:, m, j].rearrange("p r t -> p (r t)"), pj[bank_of()][:, :, :].rearrange("p a t -> p (a t)")).then_inc(sem("proj_drained"), 1)
                        bank += 1
                if g != "x":
                    turned += 1
                    act.wait_ge(sem("turned"), turned)
                    nc.scalar.copy(pcmpT[0:nb, :, :].rearrange("p r t -> p (r t)"), pj[bank_of()][0:nb, :, :].rearrange("p a t -> p (a t)")).then_inc(sem("proj_drained"), 1)
                    bank += 1
                act.wait_ge(sem("proj_drained"), bank)
                act.sem_inc(sem("turned_kept"), 1)
                act.wait_ge(sem("o_made"), u + 1)
                o = pj[bank_of()]
                if g == "x":
                    i = nc.scalar.copy(oxT[:, :, P * s:P * s + P], o[:, :, :].rearrange("p a t -> p (a t)").rearrange("p (h t) -> p h t", h=XH))
                else:
                    i = nc.scalar.copy(oT[:, 2 * g:2 * g + 2, P * s:P * s + P], o[:, 0, :].rearrange("p (a t) -> p a t", a=2))
                i.then_inc(sem("proj_drained"), 1)
                bank += 1
                act.wait_ge(sem("proj_drained"), bank)
                act.sem_inc(sem("o_kept"), 1)
            act.sem_inc(sem("attention_done"), 1)
            merged_banks += 12
            act.wait_ge(sem("sub_turned"), 1)
            nc.scalar.copy(subT.rearrange("p c t -> p (c t)"), st[:, :, :].rearrange("p c t -> p (c t)")).then_inc(sem("sub_kept"), 1)
            act.wait_ge(sem("x2_ready"), 1)
            norm(xT)
            for j in range(8):
                drain2(qpT[:, 2 * j:2 * j + 2, :], f"peer_q{j}")
            act.wait_ge(sem("proj_drained"), bank)
            act.sem_inc(sem("qp_kept"), 1)
            for s in range(2):
                act.wait_ge(sem("sub_scores"), s + 1)
                if s:
                    act.wait_ge(sem("top_done"), s)
                nc.scalar.copy(s_sb.rearrange("p c t -> p (c t)"), st[:, :, :].rearrange("p c t -> p (c t)")).then_inc(sem("sub_scores_kept"), 1)
                if s == 0:
                    act.wait_ge(sem("best_ready"), 1)
                    nc.scalar.activation(gate[:, 0], gate[:, 0], ACT.Exp).then_inc(sem("gate_exp"), 1)
            for n, dst in enumerate((h_tok, acc)):
                act.wait_ge(sem("tok_turned"), n + 1)
                nc.scalar.copy(dst.rearrange("p s d -> p (s d)"), st[:, :, :].rearrange("p c t -> p (c t)")).then_inc(sem("tok_kept"), 1)
            act.wait_ge(sem("best_ready"), 2)
            nc.scalar.activation(gate[:, 1], gate[:, 1], ACT.Exp).then_inc(sem("gate_exp"), 1)
            for n in range(2 * PH):
                s, h = divmod(n, PH)
                act.wait_ge(sem("dots_ready"), n + 1)
                nc.scalar.activation(wgt[:, s, h, :], dots[:, s, h, :], ACT.Gelu).then_inc(sem("gelu_done"), 1)
            for s in range(2):
                act.wait_ge(sem("acc_ready"), s + 1)
                link(nc.scalar.activation(h_tok[:, s, :], acc[:, s, :], ACT.Square, accum_out=mstat[:, 0, s:s + 1]))
                nc.scalar.activation(mstat[:, 1, s:s + 1], mstat[:, 0, s:s + 1], ACT.Sqrt, bias=eps_col[:, 0:1], scale=1.0 / D).then_inc(sem("last_std"), 1)

        @block.vector
        def _(dve):
            steps = 0
            norms = 0

            def count(i):
                nonlocal steps
                steps += 1
                i.then_inc(sem("dve_step"), 1)
                return steps

            def link(i):
                dve.wait_ge(sem("dve_step"), count(i))

            def rsqrt_finish():
                nonlocal norms
                norms += 1
                dve.wait_ge(sem("std_ready"), norms)
                link(nc.vector.reciprocal(rstd[:, :], rstd[:, :]))

            def over_channels(t):
                return t.unsqueeze(1).broadcast_to([P, CT, T])

            def col(l, at, c):
                return pc[:, l, at + c:at + c + 1]

            def pre_norm(l, which, shift):
                rsqrt_finish()
                link(nc.vector.tensor_tensor(hT[:, :, :], xT[:, :, :], over_channels(rstd[:, :]), ALU.mult))
                for c in range(CT):
                    i = nc.vector.tensor_scalar(hT[:, c, :], hT[:, c, :], mod_scale[:, which, c:c + 1], modc[:, shift + c:shift + c + 1],
                                                ALU.mult, ALU.add)
                    i.then_inc(sem("h_ready"), 1)
                dve.wait_ge(sem("h_ready"), (2 * l + (which == 1) + 1) * CT)
                dve.sem_inc(sem("rstd_used"), 1)

            def post_norm(l, which):
                rsqrt_finish()
                for c in range(CT):
                    i = nc.vector.scalar_tensor_tensor(y[:, c, :], y[:, c, :], mod_scale[:, which, c:c + 1], rstd[:, :], ALU.mult, ALU.mult)
                link(i)
                dve.sem_inc(sem("rstd_used"), 1)
                nc.vector.tensor_tensor(xT[:, :, :], xT[:, :, :], y[:, :, :], ALU.add).then_inc(sem("x_ready"), 1)

            def conv(l, dst, src, taps, w, bias):
                for c in range(CT):
                    i = nc.vector.tensor_scalar(dst[:, c, :], src[:, c, :], col(l, w, (taps - 1) * CT + c), col(l, bias, c), ALU.mult, ALU.add)
                    last = count(i)
                for k in range(taps - 2, -1, -1):
                    s = taps - 1 - k
                    for c in range(CT):
                        dve.wait_ge(sem("dve_step"), last - CT + 1)
                        i = nc.vector.scalar_tensor_tensor(dst[:, c, s:T], src[:, c, 0:T - s], col(l, w, k * CT + c), dst[:, c, s:T], ALU.mult, ALU.add)
                        if k == 0 and c == CT - 1:
                            return i
                        last = count(i)

            dve.wait_ge(sem("consts"), 1)
            dve.wait_ge(sem("consts2"), 1)
            dve.wait_ge(sem("params2_kept"), 1)
            dve.wait_ge(sem("params_kept"), 2)
            dve.wait_ge(sem("x_kept"), 1)
            for l in range(DEPTH):
                dve.wait_ge(sem("mod_summed"), l + 1)
                link(nc.vector.tensor_tensor(modc[:, :], ms[1][:, 0, 0:48], pc[:, l, B_ADA:B_ADA + 48], ALU.add))
                for n, (src, g, one) in enumerate(((8, G_PRE_MIX, 1.0), (32, G_PRE_MLP, 1.0), (16, G_POST_MIX, 0.0), (40, G_POST_MLP, 0.0))):
                    i = nc.vector.scalar_tensor_tensor(mod_scale[:, n, :], modc[:, src:src + 8], one, pc[:, l, g:g + 8], ALU.add, ALU.mult)
                link(i)
                pre_norm(l, 0, 0)

                dve.wait_ge(sem("proj_drained"), 64 * l + 8)
                link(nc.vector.tensor_tensor(U[:, 24:32, :], U[:, 16:24, :], U[:, 24:32, :], ALU.mult))
                glu_done = steps
                dve.wait_ge(sem("proj_drained"), 64 * l + 12)
                conv(l, xc, U[:, 0:8], KM, W_CONV, B_CONV_M).then_inc(sem("conv_m_ready"), 1)
                conv(l, U[:, 16:24], U[:, 24:32], KC, W_DW, B_DW).then_inc(sem("conv_ready"), 1)

                dve.wait_ge(sem("softplus"), l + 1)
                link(nc.vector.scalar_tensor_tensor(lrow[:, 0, :], fgr[:, 0, :], 0.0, fgr[:, 2, :], ALU.min, ALU.subtract))
                link(nc.vector.tensor_tensor_scan(lrow[:, 3, :], lrow[:, 0, :], zrow[:, :], 0.0, ALU.add, ALU.add))
                link(nc.vector.tensor_tensor(lrow[:, 2, :], gates[0:H, :], lrow[:, 3, :], ALU.subtract))
                link(nc.vector.tensor_tensor_scan(lrow[:, 0, :], lrow[:, 2, :], zrow[:, :], 0.0, ALU.max, ALU.add))
                nc.vector.tensor_scalar(rows[:, 0, :], lrow[:, 0, :], -1.0, None, ALU.mult)
                nc.vector.tensor_tensor(lrow[:, 1, :], lrow[:, 3, :], lrow[:, 0, :], ALU.add).then_inc(sem("m_ready"), 1)

                dve.wait_ge(sem("rcol_kept"), l + 1)
                for h in range(H):
                    hn = l * H + h
                    dve.wait_ge(sem("en_kept"), hn + 1)
                    for s in range(2):
                        i = nc.vector.scalar_tensor_tensor(wlog[:, s, P * s:T], ms[0][:, 0, P * s:T], rcol[:, s, h:h + 1], causal[:, s, P * s:T], ALU.add, ALU.add)
                    i.then_inc(sem("wlog_ready"), 1)
                    dve.wait_ge(sem("w_ready"), hn + 1)
                    dve.wait_ge(sem("scores_made"), hn + 1)
                    for s in range(2):
                        i = nc.vector.scalar_tensor_tensor(sT[:, s, P * s:T], ms[1][:, s, P * s:T], DH ** -0.5, wlog[:, s, P * s:T], ALU.mult, ALU.mult)
                    i.then_inc(sem("s_ready"), 1)
                    dve.wait_ge(sem("num_made"), hn + 1)
                    link(nc.vector.tensor_scalar(den[:, :], st[:, 4, :], -1.0, None, ALU.mult))
                    link(nc.vector.tensor_tensor(den[:, :], den[:, :], st[:, 4, :], ALU.max))
                    link(nc.vector.tensor_tensor(den[:, :], den[:, :], en_b[:, :], ALU.max))
                    link(nc.vector.reciprocal(den[:, :], den[:, :]))
                    nc.vector.tensor_tensor(tmp[:, 2 * h:2 * h + 2, :], st[:, 6:8, :], den[:, :].unsqueeze(1).broadcast_to([P, 2, T]), ALU.mult).then_inc(sem("head_done"), 1)
                dve.wait_ge(sem("hm_summed"), 2 * l + 1)
                for h in range(H):
                    for e in range(2):
                        i = nc.vector.scalar_tensor_tensor(tmp[:, 2 * h + e, :], st[:, h, :], -1.0 / DH, tmp[:, 2 * h + e, :], ALU.mult, ALU.add)
                i.then_inc(sem("hm_centred"), 1)
                dve.wait_ge(sem("hm_std"), l + 1)
                link(nc.vector.reciprocal(xc[:, 0:H, :], xc[:, 0:H, :]))
                for c in range(CT):
                    i = nc.vector.scalar_tensor_tensor(tmp[:, c, :], tmp[:, c, :], col(l, G_MH, c), xc[:, c // 2, :], ALU.mult, ALU.mult)
                link(i)
                link(nc.vector.tensor_tensor(U[:, 8:16, :], tmp[:, :, :], U[:, 8:16, :], ALU.mult))
                dve.sem_inc(sem("hm_done"), 1)
                dve.wait_ge(sem("gn_summed"), 2 * l + 1)
                for b in range(4):
                    nc.vector.scalar_tensor_tensor(U[:, 16 + 2 * b:18 + 2 * b, :], st[:, 2 * b:2 * b + 2, :], -1.0 / P, U[:, 16 + 2 * b:18 + 2 * b, :],
                                                   ALU.mult, ALU.add).then_inc(sem("gn_centred"), 1)
                dve.wait_ge(sem("gn_std"), l + 1)
                link(nc.vector.reciprocal(xc[:, :, :], xc[:, :, :]))
                nc.vector.tensor_tensor(U[:, 16:24, :], U[:, 16:24, :], xc[:, :, :], ALU.mult).then_inc(sem("gn_scaled"), 1)

                post_norm(l, 2)
                pre_norm(l, 1, 24)
                if l == DEPTH - 1:
                    dve.wait_ge(sem("mem_std"), 1)
                    link(nc.vector.reciprocal(mstat[:, 1, :], mstat[:, 1, :]))
                    for t in range(2):
                        i = nc.vector.tensor_scalar(memtok[:, t, :], memtok[:, t, :], mstat[:, 1, t:t + 1], None, ALU.mult)
                    i.then_inc(sem("mem_scaled"), 1)
                    dve.wait_ge(sem("bias_in"), 32)
                    nc.vector.memset(bias_w[0:NH, T:512], NEG).then_inc(sem("bias_masked"), 1)
                post_norm(l, 3)

            def gain_norm(g, n):
                rsqrt_finish()
                for c in range(CT):
                    i = nc.vector.scalar_tensor_tensor(hT[:, c, :], xT[:, c, :], pc2[:, g + c:g + c + 1], rstd[:, :], ALU.mult, ALU.mult)
                    i.then_inc(sem("h_ready"), 1)
                dve.wait_ge(sem("h_ready"), n * CT)
                dve.sem_inc(sem("rstd_used"), 1)

            dve.wait_ge(sem("x_ready"), 2 * DEPTH)
            gain_norm(G_MIX2, 5)
            dve.wait_ge(sem("cmpT_kept"), 1)
            for m in range(2):
                for g in range(2):
                    for hf in range(2):
                        src = cmpT[:, m, g, 16 * hf:16 * hf + 16 * NCMP].rearrange("p (c i) -> p c i", i=16)
                        i = nc.vector.tensor_tensor(blk[:, m, g, :, 16 * hf:16 * hf + 16], src,
                                                    pe_T[:, m, 16 * hf:16 * hf + 16].unsqueeze(1).broadcast_to([P, NCMP, 16]), ALU.add)
            i.then_inc(sem("blk_ready"), 1)
            dve.wait_ge(sem("proj_drained"), GATE_BANK)
            link(nc.vector.tensor_scalar(bgate[:, 0, 0:NH], bgate[:, 0, 0:NH], has[:, 0:1], None, ALU.mult))
            dve.wait_ge(sem("toeplitz_in"), 32)
            merge_jobs = 0

            def merge(job, tiles, branch, how):
                nonlocal merge_jobs
                sm, v, b = job
                dve.wait_ge(sem(sm), v)
                src = pj[b][:, :, :]
                if how == "x":
                    i = nc.vector.tensor_tensor(xT[:, tiles:tiles + 2, :], xT[:, tiles:tiles + 2, :], src, ALU.add)
                    return i.then_inc(sem("merge_drained"), 1)
                g = gm[:, CT * branch + tiles:CT * branch + tiles + 2, :]
                dst = merged[:, tiles:tiles + 2, :]
                if how == "first":
                    i = nc.vector.tensor_tensor(dst, src, g, ALU.mult)
                    return i.then_inc(sem("merge_drained"), 1)
                link(nc.vector.tensor_tensor(g, src, g, ALU.mult))
                nc.vector.tensor_tensor(dst, dst, g, ALU.add).then_inc(sem("merge_drained"), 1)

            for u, (g, s) in enumerate(UNITS):
                pb, sv = probs[u % 2], stat[:, u % 2]
                n = P * (s + 1)
                dve.wait_ge(sem("scores2_made"), u + 1)
                if u == 1:
                    dve.wait_ge(sem("vx_kept"), 1)
                if g == "x":
                    link(nc.vector.tensor_scalar(pb[:, 0], st[:, 0:R, :], float(P) ** -0.5, None, ALU.mult))
                    dve.sem_inc(sem("scores_kept"), 1)
                    link(nc.vector.tensor_reduce(sv[:, 0, 1, :], pb[:, 0], AX.X, ALU.max))
                    nc.vector.tensor_scalar(sv[:, 0, 1, :], sv[:, 0, 1, :], -1.0, None, ALU.mult).then_inc(sem("max_ready"), 1)
                else:
                    nb = NCMP if s else NCMP // 2
                    bs = bias[s][:, R * g:R * g + R, :]
                    nc.vector.scalar_tensor_tensor(pcmp[:, u % 2, :, 0:nb], ms[0][:, 0, 0:64].rearrange("p (r c) -> p r c", c=16)[:, :, 0:nb],
                                                   HD ** -0.5, bs[:, :, CMP_LEN - 1:CMP_LEN + CMP_STRIDE * (nb - 1):CMP_STRIDE], ALU.mult, ALU.add)
                    for m in range(2):
                        i = nc.vector.scalar_tensor_tensor(pb[:, m, :, 0:n], st[:, R * m:R * m + R, 0:n], HD ** -0.5, bs, ALU.mult, ALU.add)
                    link(i)
                    dve.sem_inc(sem("scores_kept"), 1)
                    nc.vector.tensor_reduce(sv[:, 0, 0, :], pcmp[:, u % 2, :, 0:nb], AX.X, ALU.max)
                    for m in range(2):
                        i = nc.vector.tensor_reduce(sv[:, 0, 1 + m, :], pb[:, m, :, 0:n], AX.X, ALU.max)
                    link(i)
                    nc.vector.tensor_scalar(sv[:, 0], sv[:, 0], -1.0, None, ALU.mult).then_inc(sem("max_ready"), 1)
                dve.wait_ge(sem("exp_done"), u + 1)
                if g == "x":
                    link(nc.vector.reciprocal(sv[:, 2, 1, :], sv[:, 1, 1, :]))
                    nc.vector.tensor_tensor(pb[:, 0], pb[:, 0], sv[:, 2, 1, :].unsqueeze(2).broadcast_to([P, R, T]), ALU.mult).then_inc(sem("probs_ready"), 1)
                else:
                    link(nc.vector.reciprocal(sv[:, 2], sv[:, 1]))
                    gates3 = bgate[:, s, :].rearrange("p (m h) -> p m h", m=3)[:, :, R * g:R * g + R]
                    link(nc.vector.tensor_tensor(sv[:, 2], sv[:, 2], gates3, ALU.mult))
                    nc.vector.tensor_tensor(pcmp[:, u % 2, :, 0:nb], pcmp[:, u % 2, :, 0:nb], sv[:, 2, 0, :].unsqueeze(2).broadcast_to([P, R, nb]), ALU.mult)
                    for m in range(2):
                        i = nc.vector.tensor_tensor(pb[:, m, :, 0:n], pb[:, m, :, 0:n], sv[:, 2, 1 + m, :].unsqueeze(2).broadcast_to([P, R, n]), ALU.mult)
                    i.then_inc(sem("probs_ready"), 1)
                if u == 0:
                    dve.wait_ge(sem("pool_kept"), 1)
                    dve.wait_ge(sem("cmp_made"), 1)
                    dve.wait_ge(sem("rcount_in"), 16)
                    src = poolT
                    for k in range(4):
                        sh, dst = 1 << k, win[k % 2]
                        nc.vector.tensor_copy(dst[:, k:4, 0:sh], src[:, k:4, 0:sh])
                        link(nc.vector.tensor_tensor(dst[:, k:4, sh:T], src[:, k:4, sh:T], src[:, k:4, 0:T - sh], ALU.add))
                        src = dst
                    for k in range(4):
                        i = nc.vector.tensor_tensor(win[k % 2][:, k, :], win[k % 2][:, k, :], rc[:, k, :], ALU.mult)
                    link(i)
                    for k in range(4):
                        i = nc.vector.tensor_tensor(win[0][:, k, :], win[k % 2][:, k, :], poolT[:, k, :], ALU.subtract)
                    i.then_inc(sem("pooled"), 1)
                if FILL[u] and FILL[u][0] == "pool_out0":
                    for j in range(2):
                        for k in range(2):
                            done = ("half_slot", j + 1, MERGE_BANKS[2 * j + k]) if k == 0 else ("slot_used", job_at[(f"pool_out{j}", 2, 0)] + 1, MERGE_BANKS[2 * j + k])
                            merge(done, 4 * j + 2 * k, 0, "first")
            for j in range(4):
                merge(("slot_used", job_at[(f"nsa_out{j}", 2, 0)] + 1, MERGE_BANKS[4 + j]), 2 * j, 1, "more")
            for j in range(2):
                for k in range(2):
                    done = ("half_slot", 2 + j + 1, MERGE_BANKS[8 + 2 * j + k]) if k == 0 else ("slot_used", job_at[(f"x_out{j}", 2, 0)] + 1, MERGE_BANKS[8 + 2 * j + k])
                    merge(done, 4 * j + 2 * k, 2, "more")
            for j in range(4):
                merge(("slot_used", job_at[(f"w_o{j}", 2, 0)] + 1, MERGE_BANKS[12 + j]), 2 * j, 0, "x")
            dve.wait_ge(sem("merge_drained"), 16)
            dve.sem_inc(sem("x2_ready"), 1)
            gain_norm(G_FFN2, 6)
            for s in range(2):
                dve.wait_ge(sem("sub_scores_kept"), s + 1)
                top_of(dve, link, s_sb, top_v, top_i, 2 * PH)
                tv = top_v[:, :, :].rearrange("p (h q) k -> p h q k", q=2)
                cands = cand.rearrange("p h (i j) -> p h i j", i=TOPK)
                link(nc.vector.tensor_tensor(cands, tv[:, :, 0, :].unsqueeze(3).broadcast_to([P, PH, TOPK, TOPK]),
                                             tv[:, :, 1, :].unsqueeze(2).broadcast_to([P, PH, TOPK, TOPK]), ALU.add))
                top_of(dve, link, cand, best, pos, PH)
                dve.sem_inc(sem("top_done"), 1)
                link(nc.vector.tensor_tensor(gate[:, s], best[:, :, :], best[:, :, 0:1].broadcast_to([P, PH, TOPK]), ALU.subtract))
                dve.sem_inc(sem("best_ready"), 1)
                posf = pos[:, :, :].rearrange("p h k -> p (h k)")
                nc.vector.tensor_single_scalar(half[:, 0, :], posf, 4, ALU.logical_shift_right)
                nc.vector.tensor_single_scalar(half[:, 1, :], posf, 15, ALU.bitwise_and)
                link(nc.vector.tensor_copy(top_f[:, :, :], top_i[:, :, :]))
                link(nc.vector.tensor_copy(half_f[:, :, :], half[:, :, :]))
                tf = top_f[:, :, :].rearrange("p (h q) k -> p h q k", q=2)
                for q in range(2):
                    e3 = eq.rearrange("p (n j) -> p n j", j=TOPK)
                    e4 = eq.rearrange("p (h k j) -> p h k j", h=PH, j=TOPK)
                    link(nc.vector.tensor_tensor(e3, half_f[:, q, :].unsqueeze(2).broadcast_to([P, PH * TOPK, TOPK]),
                                                 iota16[:, :].unsqueeze(1).broadcast_to([P, PH * TOPK, TOPK]), ALU.is_equal))
                    link(nc.vector.tensor_tensor(e4, e4, tf[:, :, q, :].unsqueeze(2).broadcast_to([P, PH, TOPK, TOPK]), ALU.mult))
                    link(nc.vector.tensor_reduce(part[:, q, :], e3, AX.X, ALU.add))
                nc.vector.scalar_tensor_tensor(ids[:, s, :], part[:, 0, :], float(P), part[:, 1, :], ALU.mult, ALU.add).then_inc(sem("ids_ready"), 1)
                dve.wait_ge(sem("gate_exp"), s + 1)
                link(nc.vector.tensor_reduce(gsum[:, :], gate[:, s], AX.X, ALU.add))
                link(nc.vector.reciprocal(gsum[:, :], gsum[:, :]))
                link(nc.vector.tensor_tensor(gate[:, s], gate[:, s], gsum[:, :].unsqueeze(2).broadcast_to([P, PH, TOPK]), ALU.mult))

            dve.wait_ge(sem("tok_kept"), 2)
            total = 2 * PH * TOPK
            for n in range(total + LAG):
                if n < total:
                    s, k = divmod(n, PH * TOPK)
                    dve.wait_ge(sem(f"u_row{n % NBUF}"), 16 * (n // NBUF + 1))
                    row = ubuf[:, n % NBUF, :]
                    i = nc.vector.tensor_tensor_reduce(row, row, h_tok[:, s, :], 1.0, 0.0, ALU.mult, ALU.add, dots[:, s, k // TOPK, k % TOPK:k % TOPK + 1])
                    i.then_inc(sem("u_used"), 1)
                    if n % TOPK == TOPK - 1:
                        dve.wait_ge(sem("u_used"), n + 1)
                        dve.sem_inc(sem("dots_ready"), 1)
                m = n - LAG
                if m >= 0:
                    s, k = divmod(m, PH * TOPK)
                    if m % TOPK == 0:
                        dve.wait_ge(sem("gelu_done"), m // TOPK + 1)
                        h = k // TOPK
                        link(nc.vector.tensor_tensor(wgt[:, s, h, :], wgt[:, s, h, :], gate[:, s, h, :], ALU.mult))
                    dve.wait_ge(sem(f"v_row{m % NBUF}"), 16 * (m // NBUF + 1))
                    if k:
                        dve.wait_ge(sem("v_used"), m)
                    nc.vector.scalar_tensor_tensor(acc[:, s, :], vbuf[:, m % NBUF, :], wgt[:, s, k // TOPK, k % TOPK:k % TOPK + 1], acc[:, s, :],
                                                   ALU.mult, ALU.add).then_inc(sem("v_used"), 1)
                    if k == PH * TOPK - 1:
                        dve.wait_ge(sem("v_used"), m + 1)
                        if s == 1:
                            dve.sem_inc(sem("acc_ready"), 2)
            dve.wait_ge(sem("g_fin_in"), 16)
            for s in range(2):
                dve.wait_ge(sem("last_std"), s + 1)
                link(nc.vector.reciprocal(mstat[:, 1, s:s + 1], mstat[:, 1, s:s + 1]))
                nc.vector.scalar_tensor_tensor(h_tok[:, s, :], acc[:, s, :], mstat[:, 1, s:s + 1], g_fin, ALU.mult, ALU.mult).then_inc(sem("out_ready"), 1)


def kernel(**inputs):
    import numpy as _np
    import concourse.bacc as _bacc
    from concourse.bass_utils import run_bass_kernel_spmd as _run

    nc = _bacc.Bacc("TRN2", target_bir_lowering=False, num_devices=1)
    arrays, aps = {}, {}
    dist = _np.arange(256)
    large = 16 + (_np.log(_np.maximum(dist, 1) / 16.0) / _np.log(128 / 16.0) * 16).astype(_np.int64)
    bucket = _np.where(dist < 16, dist, _np.minimum(large, N_BUCKETS - 1))
    onehot = _np.zeros((N_BUCKETS, 512), _np.float32)
    onehot[bucket, 255 - dist] = 1.0
    t = _np.arange(T)
    rcount = _np.stack([1.0 / _np.minimum(t + 1, w) for w in POOL_WINDOWS]).astype(_np.float32)
    for name, v in list(inputs.items()) + [("onehot", onehot), ("rcount", rcount)]:
        v = _np.ascontiguousarray(v)
        arrays[f"in_{name}"] = v
        aps[name] = nc.dram_tensor(f"in_{name}", v.shape, mybir.dt.from_np(v.dtype), kind="ExternalInput").ap()
    out = nc.dram_tensor("out_0", (1, T, D), F32, kind="ExternalOutput").ap()
    build_program(nc, aps, out)
    r = _run(nc, [arrays], core_ids=[0])
    return r.results[0]["out_0"]
```

```python
from contextlib import ExitStack

import concourse.bass as bass
from concourse import mybir

ALU = mybir.AluOpType
ACT = mybir.ActivationFunctionType
AX = mybir.AxisListType
F32 = mybir.dt.float32
U32 = mybir.dt.uint32

P = 128
T = 256
D = 1024
CT = D // P
DEPTH = 2
H = 4
DH = 256
FF = 4 * D
KM = 4
KC = 31
NEG = -1e30
EPS = 1e-6

SLOT = 2048
RING = 4
ADA_CHUNKS = 24

FIRST_CHUNKS = 8
W_IN_ORDER = [0, 1, 2, 3] + list(range(8, 16)) + [4, 5, 6, 7]

B_ADA, G_PRE_MIX, G_PRE_MLP, G_POST_MIX, G_POST_MLP = 0, 48, 56, 64, 72
B_CONV_M, G_MH, B_DW, G_CN, B_CN, C_COL = 80, 88, 96, 104, 112, 120
W_DW, W_CONV = 128, 376
NPC = 408


NH, G, R, HD = 16, 4, 4, 64
N_BUCKETS = 32
CMP_LEN, CMP_STRIDE = 32, 16
NCMP = (T - CMP_LEN) // CMP_STRIDE + 1
POOL_WINDOWS = (2, 4, 8, 16)
XH = 4
KV0, GN0, QX0, GM0 = 1536, 3072, 3120, 3632
PH, TOPK = 8, 16
NBUF = 8
LAG = 20
G_MIX2, G_MEM2, G_FFN2, POOL_SC2 = 0, 8, 16, 24
UNITS = [(g, s) for g in range(G) for s in range(2)] + [("x", 0), ("x", 1)]
FILL = [["pool0", "pool1"], ["gm0", "gm1"], ["gm2", "gm3"], ["gm4", "gm5"], ["gm6", "gm7"], ["gm8", "gm9"],
        ["gm10", "gm11"], ["mix"], ["pool_out0", "pool_out1"], []]


def weight_jobs():
    jobs = []
    for l in range(DEPTH):
        for j in W_IN_ORDER:
            jobs.append(("w_in", l, j))
        for j in range(8):
            jobs.append(("w_out", l, j))
        for j in range(16):
            jobs.append(("w_ff1", l, j))
        for j in range(16):
            jobs.append(("w_ff2", l, j))
    for j in ("kcmp", "vcmp", "q0", "q1", "q2", "q3", "ksel", "vsel", "kwin", "vwin", "qx0", "qx1",
              "memk0", "memk1", "memv0", "memv1"):
        jobs.append((j, 2, 0))
    for names in FILL:
        jobs += [(j, 2, 0) for j in names if j != "mix"]
    for name, n in (("nsa_out", 4), ("x_out", 2), ("w_o", 4), ("peer_q", 8)):
        jobs += [(f"{name}{j}", 2, 0) for j in range(n)]
    return jobs


def second_weight(a, name):
    w_in = a["w_in_2"][0].rearrange("(k p) n -> p k n", p=P)
    parts = ("kcmp", "vcmp", "ksel", "vsel", "kwin", "vwin")
    if name in parts:
        c = KV0 + 256 * parts.index(name)
        return w_in[:, :, c:c + 256]
    base = name.rstrip("0123456789")
    j = int(name[len(base):])
    if base == "pool":
        return w_in[:, :, 256 * j:256 * j + 256]
    if base == "qx":
        return w_in[:, :, QX0 + 256 * j:QX0 + 256 * j + 256]
    if base == "gm":
        return w_in[:, :, GM0 + 256 * j:GM0 + 256 * j + 256]
    if base in ("memk", "memv"):
        c = 512 * (base == "memv") + 256 * j
        return a["w_mem_kv_2"][0].rearrange("(k p) n -> p k n", p=P)[:, :, c:c + 256]
    if base in ("pool_out", "x_out"):
        return a[f"w_{base}_2"][0].rearrange("(k p) n -> p k n", p=P)[:, :, 512 * j:512 * j + 512]
    w = {"nsa_out": "w_nsa_out_2", "w_o": "w_o_2", "peer_q": "w_peer_q_2"}[base]
    return a[w][0].rearrange("(k p) n -> p k n", p=P)[:, :, 256 * j:256 * j + 256]


def top_of(dve, link, values, top, where, groups):
    v = dve
    for c in range(groups):
        i = v.max(top[:, c, 0:8], values[:, c, :])
    link(i)
    for c in range(groups):
        i = v.max_index(where[:, c, 0:8], top[:, c, 0:8], values[:, c, :])
    link(i)
    for c in range(groups):
        i = v.match_replace(values[:, c, :], top[:, c, 0:8], values[:, c, :], -3.0e38)
    link(i)
    for c in range(groups):
        i = v.max(top[:, c, 8:16], values[:, c, :])
    link(i)
    for c in range(groups):
        i = v.max_index(where[:, c, 8:16], top[:, c, 8:16], values[:, c, :])
    link(i)


def build_program(nc, a, out):
    ctx = ExitStack()
    with ctx:
        def sb(name, shape, dt=F32):
            return ctx.enter_context(nc.sbuf_tensor(name, shape, dt))

        ring = sb("ring", [P, RING, SLOT])
        xT = sb("xT", [P, CT, T])
        hT = sb("hT", [P, CT, T])
        tmp = sb("tmp", [P, CT, T])
        region = sb("region", [P, 32768])
        at = 0

        def cut(n):
            nonlocal at
            at += n
            return region[:, at - n:at]

        U = cut(8192).rearrange("p (c t) -> p c t", t=T)
        xc = cut(2048).rearrange("p (c t) -> p c t", t=T)
        qT = cut(2048).rearrange("p (c t) -> p c t", t=T)
        kT = cut(2048).rearrange("p (c t) -> p c t", t=T)
        vtok = cut(2048).rearrange("p (s e) -> p s e", s=2)
        wqkv = cut(6144).rearrange("p (m c e) -> p m c e", m=3, c=2 * H)
        ada_in = cut(4096).rearrange("p (b k n) -> p b k n", b=2, k=CT)
        ada_acc = cut(6144)
        x_tok = tmp[:, :, :].rearrange("p c t -> p (c t)").rearrange("p (s d) -> p s d", s=2)
        def piece(lo, n):
            return region[:, lo:lo + n]

        gm = piece(0, 6144).rearrange("p (c t) -> p c t", t=T)
        poolT = piece(6144, 1024).rearrange("p (c t) -> p c t", t=T)
        qxT = piece(7168, 1024).rearrange("p (c t) -> p c t", t=T)
        wcmp = piece(8192, 4096).rearrange("p (m i e) -> p m i e", m=2, i=CMP_LEN)
        oT = piece(8192, 2048).rearrange("p (c t) -> p c t", t=T)
        merged = piece(10240, 2048).rearrange("p (c t) -> p c t", t=T)
        q2T = piece(12288, 2048).rearrange("p (c t) -> p c t", t=T)
        cmpT = piece(14336, 1024).rearrange("p (m c t) -> p m c t", m=2, t=T)
        oxT = piece(14336, 1024).rearrange("p (c t) -> p c t", t=T)
        kselT = piece(15360, 1024).rearrange("p (m c t) -> p m c t", m=2, t=T)
        onehot = piece(16384, 512)
        bias_w = piece(16896, 512)
        rel = piece(17408, NH)
        wqkv_free = piece(18432, 1024)
        v2 = piece(16384, 1024).rearrange("p (m s e) -> p m s e", m=2, s=2)
        kxT = piece(17408, 1024).rearrange("p (c t) -> p c t", t=T)
        vx = piece(18432, 1024).rearrange("p (s e) -> p s e", s=2)
        probs = [piece(19456, 2048).rearrange("p (m r t) -> p m r t", m=2, r=R),
                 piece(24576, 2048).rearrange("p (m r t) -> p m r t", m=2, r=R)]
        probsT = piece(21504, 2048).rearrange("p (m j r t) -> p m j r t", m=2, j=2, r=R)
        memtok = piece(22528, 2048).rearrange("p (s d) -> p s d", s=2)
        memT = piece(24576, 2048).rearrange("p (c t) -> p c t", t=T)
        bias = [piece(26624, 2048).rearrange("p (h t) -> p h t", h=NH), piece(28672, 4096).rearrange("p (h t) -> p h t", h=NH)]
        blk = tmp[:, :, :].rearrange("p c t -> p (c t)")[:, 0:1920].rearrange("p (m g c i) -> p m g c i", m=2, g=2, i=CMP_LEN)
        win = [tmp[:, 0:4, :], tmp[:, 4:8, :]]
        qpT = piece(0, 4096).rearrange("p (c t) -> p c t", t=T)
        subT = piece(4096, 2048).rearrange("p (c t) -> p c t", t=P)
        s_sb = piece(6144, 2048).rearrange("p (c t) -> p c t", t=P)
        acc = piece(8192, 2048).rearrange("p (s d) -> p s d", s=2)
        h_tok = piece(10240, 2048).rearrange("p (s d) -> p s d", s=2)
        ubuf = piece(12288, 8192).rearrange("p (b d) -> p b d", b=NBUF)
        vbuf = piece(20480, 8192).rearrange("p (b d) -> p b d", b=NBUF)
        eq = piece(28672, 2048)
        sub_raw = piece(30720, 2048).rearrange("p (c t) -> p c t", t=P)
        cand = tmp[:, :, :]
        g_fin = ring[:, 0, 0:D]

        vT = tmp
        y = hT

        prow = qT.rearrange("p c t -> p (c t)")[:, 0:DEPTH * 4 * P].rearrange("p (l k q) -> p l k q", l=DEPTH, k=4)
        small = sb("small", [P, 3584])

        def small_piece(lo, n, rows=P):
            return small[0:rows, lo:lo + n]

        pc = sb("pc", [P, DEPTH, NPC])
        modc = sb("modc", [P, 48])
        mod_scale = sb("mod_scale", [P, 4, CT])
        c_act = sb("c_act", [P, CT])
        wg = sb("wg", [P, 6, H * 2 * H])
        bg = sb("bg", [2 * H, 1])
        ident = sb("ident", [P, P])
        ones = sb("ones", [P, P])
        eps_col = sb("eps_col", [P, 1])
        causal = sb("causal", [P, 2, T])
        wpg = small_piece(1504, 512).rearrange("p (g d) -> p g d", g=4)
        pick = small_piece(2048, 1024, CT).rearrange("p (h q) -> p h q", h=CT)
        rstd = sb("rstd", [P, T])
        gates = small_piece(3328, 256, 2 * H)
        vrow = small_piece(0, 256, CT)
        to_row = sb("to_row", [P, CT, CT])
        grow = wqkv.rearrange("p m c e -> p (m c e)")[0:H, 0:7 * T].rearrange("p (n t) -> p n t", t=T)
        fgr = grow[:, 0:3, :]
        lrow = grow[:, 3:7, :]
        ada_first = [region[:, 0:8192].rearrange("p (k n) -> p k n", k=CT), region[:, 14336:22528].rearrange("p (k n) -> p k n", k=CT)]
        zrow = small_piece(3072, 256, H)
        rows = small_piece(1536, 512, H).rearrange("p (s t) -> p s t", s=2)
        rcol = sb("rcol", [P, 2, H])
        wlog = small_piece(0, 512).rearrange("p (s t) -> p s t", s=2)
        sT = small_piece(512, 512).rearrange("p (s t) -> p s t", s=2)
        en_b = small_piece(1024, 256)
        den = small_piece(1280, 256)
        prow2 = kT.rearrange("p c t -> p (c t)")[:, 0:P]
        pc2 = sb("pc2", [P, 28])
        pe_T = sb("pe_T", [P, 2, CMP_LEN])
        pe_raw = kT.rearrange("p c t -> p (c t)")[0:CMP_LEN, 256:512].rearrange("p (m h d) -> p m h d", m=2, h=2)
        wgn = small_piece(0, 384).rearrange("p (k n) -> p k n", k=CT)
        bgate = small_piece(448, 96).rearrange("p (s n) -> p s n", s=2)
        has = sb("has", [P, 1])
        cmpc = small_piece(384, 60).rearrange("p (m g c) -> p m g c", m=2, g=2)
        vc = small_piece(544, 256, NCMP).rearrange("p (g e) -> p g e", g=2)
        pcmp = small_piece(800, 120).rearrange("p (b r c) -> p b r c", b=2, r=R)
        pcmpT = small_piece(920, 512, NCMP).rearrange("p (r t) -> p r t", r=R)
        stat = small_piece(1432, 72).rearrange("p (b n m r) -> p b n m r", b=2, n=3, m=3)
        rc = piece(19456 + 2048 + 2048 + 0, 1024).rearrange("p (g t) -> p g t", g=4)
        mstat = sb("mstat", [P, 2, 2])
        top_v = small_piece(0, 256).rearrange("p (c k) -> p c k", k=TOPK)
        top_i = small_piece(256, 256).bitcast(U32).rearrange("p (c k) -> p c k", k=TOPK)
        top_f = small_piece(512, 256).rearrange("p (c k) -> p c k", k=TOPK)
        best = small_piece(768, 128).rearrange("p (c k) -> p c k", k=TOPK)
        pos = small_piece(896, 128).bitcast(U32).rearrange("p (c k) -> p c k", k=TOPK)
        half = small_piece(1024, 256).bitcast(U32).rearrange("p (c k) -> p c k", c=2)
        half_f = small_piece(1280, 256).rearrange("p (c k) -> p c k", c=2)
        part = small_piece(1536, 256).rearrange("p (c k) -> p c k", c=2)
        ids = small_piece(1792, 256).bitcast(U32).rearrange("p (c k) -> p c k", c=2)
        gate = small_piece(2048, 256).rearrange("p (s h k) -> p s h k", s=2, k=TOPK)
        gsum = sb("gsum", [P, PH])
        dots = small_piece(2304, 256).rearrange("p (s h k) -> p s h k", s=2, k=TOPK)
        wgt = small_piece(2560, 256).rearrange("p (s h k) -> p s h k", s=2, k=TOPK)
        iota16 = sb("iota16", [P, TOPK])
        bias_dram = nc.dram_tensor("bias_dram", (P, NH, 512), F32, kind="Internal").ap()

        pj = [ctx.enter_context(nc.psum_tensor(f"pj{i}", [P, 2, T], F32)) for i in range(2)]
        st = ctx.enter_context(nc.psum_tensor("st", [P, CT, T], F32))
        ms = [ctx.enter_context(nc.psum_tensor(f"ms{i}", [P, 2, T], F32)) for i in range(2)]

        sems = {}

        def sem(name):
            if name not in sems:
                sems[name] = ctx.enter_context(nc.semaphore(name))
            return sems[name]

        ring_full = [sem(f"ring_full{i}") for i in range(RING)]
        jobs = weight_jobs()
        job_at = {j: n for n, j in enumerate(jobs)}
        full_at = []
        for n, j in enumerate(jobs):
            before = full_at[n - RING] if n >= RING else 0
            full_at.append(before + (64 if j[0] in ("q0", "q1", "q2", "q3") else 16))

        MERGE_BANKS, GATE_BANK, banks = [], None, 64 * DEPTH
        for j in jobs[job_at[("kcmp", 2, 0)]:job_at[("vwin", 2, 0)] + 1]:
            banks += 1
        banks += 1
        GATE_BANK = banks
        banks += 6
        for (g, s), names in zip(UNITS, FILL):
            for name in names:
                if name[:8] == "pool_out":
                    MERGE_BANKS += [banks % 2, (banks + 1) % 2]
                    banks += 2
                else:
                    banks += 2 if name == "mix" else 1
            banks += 3 if g == "x" else 2 * (s + 1) + 2
        MERGE_BANKS += [(banks + k) % 2 for k in range(12)]

        block = ctx.enter_context(nc.Block())

        @block.sync
        def _(sp):
            def load_params(l):
                r = prow[:, l]
                for dst, n, src in (
                    (B_ADA, 48, a["b_ada"]), (G_PRE_MIX, 8, a["g_pre_mix"]), (G_PRE_MLP, 8, a["g_pre_mlp"]),
                    (G_POST_MIX, 8, a["g_post_mix"]), (G_POST_MLP, 8, a["g_post_mlp"]), (B_CONV_M, 8, a["b_conv_m"]),
                    (G_MH, 8, a["g_mh"]), (B_DW, 8, a["b_dw"]), (G_CN, 8, a["g_cn"]), (B_CN, 8, a["b_cn"]),
                ):
                    sp.dma_start(r[dst:dst + n, 0, :], src[l].rearrange("(r q) -> r q", q=P)).then_inc(sem("params_in"), 16)
                sp.dma_start(r[C_COL:C_COL + 8, 0, :], a["c"][0].rearrange("(r q) -> r q", q=P)).then_inc(sem("params_in"), 16)
                wdw = a["w_dw"][l].rearrange("k (c q) -> (k c) q", q=P)
                sp.dma_start(r[:, 1, :], wdw[0:P, :]).then_inc(sem("params_in"), 16)
                sp.dma_start(r[0:120, 2, :], wdw[P:248, :]).then_inc(sem("params_in"), 16)
                sp.dma_start(r[0:32, 3, :], a["w_conv_m"][l].rearrange("k (c q) -> (k c) q", q=P)).then_inc(sem("params_in"), 16)

            sp.dma_start(x_tok, a["x"][0].rearrange("(s p) d -> p s d", p=P)).then_inc(sem("x_in"), 16)
            for j in range(2):
                sp.dma_start(ada_first[j], a["w_ada"][0].rearrange("(k p) n -> p k n", p=P)[:, :, 1024 * j:1024 * j + 1024]).then_inc(sem(f"ada_first{j}"), 16)
            for l in range(DEPTH):
                load_params(l)

            def load_layer(l):
                sp.wait_ge(sem("mod_first"), 1)
                if l:
                    sp.wait_ge(sem("head_done"), H * l)
                for m, w in enumerate((a["w_q"], a["w_k"], a["w_v"])):
                    sp.dma_start(wqkv[:, m], w[l].rearrange("h (c p) e -> p (h c) e", p=P)).then_inc(sem("wqkv_in"), 16)
                sp.dma_start(wg[:, :, :], a["w_gates"][l].rearrange("(j p h) g -> p j (h g)", p=P, h=H)).then_inc(sem("wg_in"), 16)
                sp.dma_start(bg[:, :], a["b_gates"][l].rearrange("(g o) -> g o", o=1)).then_inc(sem("wg_in"), 16)

            for lo, n, src in ((G_MIX2, 8, a["g_mix_2"][0]), (G_MEM2, 8, a["g_mem_2"][0]), (G_FFN2, 8, a["g_ffn_2"][0]),
                               (POOL_SC2, 4, a["pool_scale_2"][0])):
                sp.dma_start(prow2[lo:lo + n, :], src.rearrange("(r q) -> r q", q=P)).then_inc(sem("params2_in"), 16)
            for m, src in enumerate((a["pe_k_2"][0], a["pe_v_2"][0])):
                for h in range(2):
                    sp.dma_start(pe_raw[:, m, h, :], src).then_inc(sem("params2_in"), 16)

            for n, (name, l, j) in enumerate(jobs):
                if n >= RING:
                    sp.wait_ge(sem("slot_used"), n - RING + 1)
                dst = ring[:, n % RING, :]
                if name in ("w_in", "w_ff1"):
                    src = a[name][l].rearrange("(k p) n -> p k n", p=P)[:, :, 256 * j:256 * j + 256]
                    dst = dst.rearrange("p (k n) -> p k n", n=256)
                elif name == "w_out":
                    src = a[name][l].rearrange("(k p) n -> p k n", p=P)[:, :, P * j:P * j + P]
                    dst = dst.rearrange("p (k n) -> p k n", n=P)
                elif name in ("q0", "q1", "q2", "q3"):
                    gp, rp = divmod(int(name[1]), 2)
                    w = a["w_in_2"][0].rearrange("(k p) n -> p k n", p=P)
                    dst = dst.rearrange("p (k r h d) -> p k r h d", r=2, h=2, d=HD)
                    for r in range(2):
                        for hf in range(2):
                            c = 512 + 256 * (2 * gp + hf) + P * rp + HD * r
                            sp.dma_start(dst[:, :, r, hf, :], w[:, :, c:c + HD]).then_inc(ring_full[n % RING], 16)
                    continue
                elif l == 2:
                    src = second_weight(a, name)
                    dst = dst.rearrange("p (k n) -> p k n", n=src.shape[2])
                else:
                    src = a[name][l].rearrange("(k p) n -> p k n", p=P)[:, 16 * (j % 2):16 * (j % 2) + 16, P * (j // 2):P * (j // 2) + P]
                    dst = dst.rearrange("p (k n) -> p k n", n=P)
                sp.dma_start(dst, src).then_inc(ring_full[n % RING], 16)
                if name == "w_in" and j == (3 if l == 0 else 11):
                    load_layer(l)

            sp.wait_ge(sem("slot_used"), len(jobs))
            sp.dma_start(g_fin, a["g_final_2"].partition_broadcast(P)).then_inc(sem("g_fin_in"), 16)
            for s in range(2):
                sp.wait_ge(sem("out_ready"), s + 1)
                sp.dma_start(out[0, P * s:P * s + P, :], h_tok[:, s, :]).then_inc(sem("out_done"), 16)
            sp.wait_ge(sem("out_done"), 32)

        @block.gpsimd
        def _(pool):
            nc.gpsimd.memset(ident[:, :], 0.0).then_inc(sem("pool_c"), 1)
            nc.gpsimd.memset(causal[:, :, :], 0.0).then_inc(sem("pool_c"), 1)
            nc.gpsimd.memset(pick[:, :, :], 0.0).then_inc(sem("pool_c"), 1)
            nc.gpsimd.memset(to_row[:, :, :], 0.0)
            nc.gpsimd.memset(ones[:, :], 1.0)
            nc.gpsimd.memset(eps_col[:, :], EPS)
            nc.gpsimd.memset(zrow[:, :], 0.0).then_inc(sem("pool_c"), 1)
            pool.wait_ge(sem("pool_c"), 4)
            nc.gpsimd.affine_select(out=ident[:, :], in_=ident[:, :], compare_op=ALU.not_equal, fill=1.0, base=0,
                                    pattern=[[-1, P]], channel_multiplier=1)
            nc.gpsimd.affine_select(out=causal[:, :, :], in_=causal[:, :, :], compare_op=ALU.is_ge, fill=NEG, base=0,
                                    pattern=[[-P, 2], [1, T]], channel_multiplier=-1)
            nc.gpsimd.affine_select(out=to_row[:, :, :], in_=to_row[:, :, :], compare_op=ALU.not_equal, fill=1.0, base=0,
                                    pattern=[[1, CT], [-1, CT]], channel_multiplier=0)
            nc.gpsimd.affine_select(out=pick[:, :, :], in_=pick[:, :, :], compare_op=ALU.not_equal, fill=1.0, base=0,
                                    pattern=[[-1, CT], [0, P]], channel_multiplier=1).then_inc(sem("consts"), 1)

            nc.gpsimd.memset(has[:, :], 1.0).then_inc(sem("pool_c"), 1)
            pool.wait_ge(sem("pool_c"), 5)
            nc.gpsimd.affine_select(out=has[:, :], in_=has[:, :], compare_op=ALU.is_ge, fill=0.0, base=-(CMP_LEN - 1),
                                    pattern=[[0, 1]], channel_multiplier=1)
            nc.gpsimd.iota(iota16[:, :], pattern=[[1, TOPK]], base=0, channel_multiplier=0,
                           allow_small_or_imprecise_dtypes=True).then_inc(sem("consts2"), 1)

            def load(n):
                l, j = divmod(n, ADA_CHUNKS)
                src = a["w_ada"][l].rearrange("(k p) n -> p k n", p=P)[:, :, 256 * j:256 * j + 256]
                pool.dma_start(ada_in[:, n % 2], src).then_inc(sem(f"ada_full{n % 2}"), 16)

            total = DEPTH * ADA_CHUNKS
            load(FIRST_CHUNKS)
            pool.wait_ge(sem("c_ready"), 1)
            step = 0
            for n in range(FIRST_CHUNKS, total):
                if n + 1 < total:
                    load(n + 1)
                l, j = divmod(n, ADA_CHUNKS)
                pool.wait_ge(sem(f"ada_full{n % 2}"), 16 * ((n - FIRST_CHUNKS) // 2 + 1))
                if l and j == 0:
                    pool.wait_ge(sem("mod_summed"), l)
                acc = ada_acc[:, 256 * j:256 * j + 256]
                w = ada_in[:, n % 2]
                c_wide = c_act[:, :].unsqueeze(2).broadcast_to([P, CT, 256])
                for dst, x0, x1, op in ((w, w, c_wide, ALU.mult), (w[:, 0:4], w[:, 0:4], w[:, 4:8], ALU.add),
                                        (w[:, 0:2], w[:, 0:2], w[:, 2:4], ALU.add), (acc, w[:, 0], w[:, 1], ALU.add)):
                    nc.gpsimd.tensor_tensor(dst, x0, x1, op).then_inc(sem("ada_step"), 1)
                    step += 1
                    pool.wait_ge(sem("ada_step"), step)

            pool.wait_ge(sem("mod_summed"), DEPTH)
            pool.dma_start(memtok, a["mem_2"][0].rearrange("(s p) d -> p s d", p=P)).then_inc(sem("mem_in"), 16)
            pool.wait_ge(sem("head_done"), H * DEPTH)
            pool.dma_start(onehot[0:N_BUCKETS, :], a["onehot"]).then_inc(sem("bias_in"), 16)
            pool.dma_start(rel[0:N_BUCKETS, :], a["rel_bias_2"]).then_inc(sem("bias_in"), 16)
            pool.wait_ge(sem("mix_ready"), DEPTH * CT)
            pool.dma_start(wgn[:, :, :], a["w_in_2"][0].rearrange("(k p) n -> p k n", p=P)[:, :, GN0:GN0 + 48]).then_inc(sem("wgn_in"), 16)
            for m, w in enumerate((a["w_cmp_k_2"], a["w_cmp_v_2"])):
                for h in range(2):
                    pool.dma_start(wcmp[HD * h:HD * h + HD, m], w[0].rearrange("(i d) e -> d i e", d=HD)).then_inc(sem("wcmp_in"), 16)
            pool.wait_ge(sem("bias_masked"), 1)
            pool.wait_ge(sem("bias_copied"), 1)
            pool.dma_start(bias_dram.rearrange("p h u -> h p u"), bias_w[0:NH, :].unsqueeze(1).broadcast_to([NH, P, 512])).then_inc(sem("bias_out"), 16)
            pool.wait_ge(sem("bias_out"), 16)
            for s in range(2):
                n = P * (s + 1)
                src = bass.AP(tensor=bias_dram.tensor, offset=255 - P * s, ap=[[NH * 512 - 1, P], [512, NH], [1, n]])
                pool.dma_start(bias[s], src).then_inc(sem("toeplitz_in"), 16)
            pool.wait_ge(sem("memT_ready"), 1)
            pool.dma_start(rc, a["rcount"].partition_broadcast(P)).then_inc(sem("rcount_in"), 16)
            pool.wait_ge(sem("x_ready"), 2 * DEPTH * CT)
            pool.dma_start(wpg[:, :, :], a["w_pool_grp_2"][0].rearrange("g c d -> c g d")).then_inc(sem("wpg_in"), 16)
            pool.wait_ge(sem("attention_done"), 1)
            pool.dma_start(sub_raw, a["peer_sub_keys_2"][0].rearrange("h p k c -> k (h p) c")).then_inc(sem("sub_in"), 16)

            total = 2 * PH * TOPK
            for n in range(total + LAG):
                for table, buf, name, m in ((a["peer_u_2"], ubuf, "u", n), (a["peer_v_2"], vbuf, "v", n - LAG)):
                    if not 0 <= m < total:
                        continue
                    s, k = divmod(m, PH * TOPK)
                    if name == "u" and k == 0:
                        pool.wait_ge(sem("ids_ready"), s + 1)
                    if m >= NBUF:
                        pool.wait_ge(sem(f"{name}_used"), m - NBUF + 1)
                    nc.gpsimd.indirect_dma_start(
                        out=buf[:, m % NBUF, :], out_offset=None, in_=table[0],
                        in_offset=bass.IndirectOffsetOnAxis(ap=ids[:, s, k:k + 1], axis=0)).then_inc(sem(f"{name}_row{m % NBUF}"), 16)

        @block.tensor
        def _(pe):
            bank = 0
            emptied = {"proj_drained": 0, "merge_drained": 0}
            emptied_at = []

            def take_bank(by="proj_drained"):
                nonlocal bank
                if bank >= 2:
                    pe.wait_ge(sem(emptied_at[bank - 2][0]), emptied_at[bank - 2][1])
                emptied[by] += 1
                emptied_at.append((by, emptied[by]))
                bank += 1
                return pj[(bank - 1) % 2]

            def ring_slot(job):
                n = job_at[job]
                pe.wait_ge(ring_full[n % RING], full_at[n])
                return ring[:, n % RING, :]

            pe.wait_ge(sem("consts"), 1)
            pe.wait_ge(sem("x_in"), 16)
            for c in range(CT):
                for s in range(2):
                    i = nc.tensor.transpose(st[:, c, P * s:P * s + P], x_tok[:, s, P * c:P * c + P], ident[:, :])
            i.then_inc(sem("x_turned"), 1)
            pe.wait_ge(sem("params_in"), 16 * 14 * DEPTH)
            for l in range(DEPTH):
                b = ms[l][:, :, :].rearrange("p s t -> p (s t)")
                for k, n, c0 in ((0, P, 0), (1, P, W_DW), (2, 120, W_DW + P), (3, 32, W_CONV)):
                    i = nc.tensor.transpose(b[:, c0:c0 + n], prow[0:n, l, k, :], ident[0:n, 0:n])
                i.then_inc(sem("params_turned"), 1)

            pe.wait_ge(sem("params2_in"), 16 * 8)
            pe.wait_ge(sem("params_kept"), 1)
            nc.tensor.transpose(ms[0][:, 0, 0:28], prow2[0:28, :], ident[0:28, 0:28])
            for m in range(2):
                i = nc.tensor.transpose(ms[0][:, 1, CMP_LEN * m:CMP_LEN * m + CMP_LEN], pe_raw[:, m].rearrange("p h d -> p (h d)"),
                                        ident[0:CMP_LEN, 0:CMP_LEN])
            i.then_inc(sem("params2_turned"), 1)
            norms = 0

            def norm_sum():
                nonlocal norms
                for c in range(CT):
                    pe.wait_ge(sem("squares"), CT * norms + c + 1)
                    i = nc.tensor.matmul(ms[0][:, 0, :], ones[:, :], tmp[:, c, :], start=(c == 0), stop=(c == CT - 1))
                i.then_inc(sem("norm_summed"), 1)
                norms += 1

            def wide_tile(job, m, b, first_wait=None):
                w = ring_slot(job).rearrange("p (k n) -> p k n", n=256)
                for k in range(CT):
                    if first_wait is not None and m == 0:
                        pe.wait_ge(sem("h_ready"), first_wait + k + 1)
                    i = nc.tensor.matmul(b[:, m, :], w[:, k, P * m:P * m + P], hT[:, k, :], start=(k == 0), stop=(k == CT - 1))
                if m == 1:
                    i.then_inc(sem("slot_used"), 1)

            def wide(name, l, js, first_wait=None):
                for j in js:
                    b = take_bank()
                    for m in range(2):
                        wide_tile((name, l, j), m, b, first_wait if j == js[0] else None)

            def sum_modulation(l, first):
                pe.wait_ge(sem("ada_step"), 4 * (ADA_CHUNKS * (l + 1) - FIRST_CHUNKS))
                for m in range(first, 48):
                    i = nc.tensor.matmul(ms[1][:, 0, m:m + 1], ada_acc[:, P * m:P * m + P], ones[:, 0:1], start=True, stop=True)
                i.then_inc(sem("mod_summed"), 1)

            for l in range(DEPTH):
                if l == 0:
                    pe.wait_ge(sem("params_kept"), 2)
                    pe.wait_ge(sem("params2_kept"), 1)
                    pe.wait_ge(sem("c_ready"), 1)
                    for m in range(2 * FIRST_CHUNKS):
                        if m % 8 == 0:
                            pe.wait_ge(sem(f"ada_first{m // 8}"), 16)
                        for k in range(CT):
                            i = nc.tensor.matmul(ms[1][:, 0, m:m + 1], ada_first[m // 8][:, k, P * (m % 8):P * (m % 8) + P], c_act[:, k:k + 1],
                                                 start=(k == 0), stop=(k == CT - 1))
                    i.then_inc(sem("mod_first"), 1)
                else:
                    sum_modulation(l, 0)
                norm_sum()
                wide("w_in", l, W_IN_ORDER[:12], 16 * l)

                pe.wait_ge(sem("wqkv_in"), 48 * (l + 1))
                pe.wait_ge(sem("proj_drained"), bank)
                for m in (2, 0, 1):
                    if m == 0:
                        pe.wait_ge(sem("xc_ready"), l + 1)
                    for h in range(H):
                        b = take_bank()
                        for e in range(2):
                            for d in range(2):
                                src = U if m == 2 else xc
                                i = nc.tensor.matmul(b[:, e, :], wqkv[:, m, 2 * h + d, P * e:P * e + P], src[:, 2 * h + d, :],
                                                     start=(d == 0), stop=(d == 1))
                        i.then_inc(sem("qkv_made"), 1)
                    if m == 2:
                        for s in range(2):
                            for hp in range(2):
                                b = take_bank()
                                for h in range(2):
                                    for d in range(2):
                                        c = 2 * (2 * hp + h) + d
                                        i = nc.tensor.matmul(b[:, h, :], U[:, c, P * s:P * s + P], wqkv[:, 2, c, :],
                                                             start=(d == 0), stop=(d == 1))
                                i.then_inc(sem("qkv_made"), 1)

                pe.wait_ge(sem("wg_in"), 32 * (l + 1))
                pe.wait_ge(sem("proj_drained"), bank)
                n = 0
                for m, src in enumerate((qT, kT, vT)):
                    for e in range(2):
                        for h in range(H):
                            i = nc.tensor.matmul(ms[0][0:2 * H, 0, :], wg[:, 2 * m + e, 8 * h:8 * h + 8], src[:, 2 * h + e, :],
                                                 start=(n == 0), stop=(n == 23))
                            n += 1
                i.then_inc(sem("gates_made"), 1)
                pe.wait_ge(sem("gates_kept"), l + 1)
                nc.tensor.matmul(ms[0][0:H, 1, :], ident[0:2 * H, H:2 * H], gates[:, :], start=True, stop=True).then_inc(sem("fg_moved"), 1)

                if l == 0:
                    sum_modulation(0, 2 * FIRST_CHUNKS)
                wide("w_in", l, [4])
                pe.wait_ge(sem("rows_ready"), l + 1)
                for s in range(2):
                    i = nc.tensor.transpose(ms[0][:, 0, H * s:H * s + H], lrow[:, 2, P * s:P * s + P], ident[0:H, 0:H])
                i.then_inc(sem("r_turned"), 1)

                for h in range(H):
                    hn = l * H + h
                    if h == 0:
                        pe.wait_ge(sem("rcol_kept"), l + 1)
                        pe.wait_ge(sem("mod_kept"), l + 1)
                    else:
                        pe.wait_ge(sem("head_done"), hn)
                    nc.tensor.matmul(ms[0][:, :, :].rearrange("p a t -> p (a t)"), pick[0:H, h, :],
                                     rows[:, :, :].rearrange("p a t -> p (a t)"), start=True, stop=True).then_inc(sem("rows_spread"), 1)
                    for s in range(2):
                        t0 = P * s
                        for d in range(2):
                            i = nc.tensor.matmul(ms[1][:, s, t0:T], kT[:, 2 * h + d, P * s:P * s + P], qT[:, 2 * h + d, t0:T],
                                                 start=(d == 0), stop=(d == 1))
                    i.then_inc(sem("scores_made"), 1)
                    z = ("w_in", l, 5 + h)
                    if h < 3:
                        b = take_bank()
                        wide_tile(z, 0, b)
                    pe.wait_ge(sem("s_ready"), hn + 1)
                    for s in range(2):
                        i = nc.tensor.matmul(st[:, 4, P * s:T], ones[:, :], sT[:, s, P * s:T], start=(s == 0), stop=(s == 1))
                    for e in range(2):
                        for s in range(2):
                            i = nc.tensor.matmul(st[:, 6 + e, P * s:T], vtok[:, s, DH * h + P * e:DH * h + P * e + P], sT[:, s, P * s:T],
                                                 start=(s == 0), stop=(s == 1))
                    i.then_inc(sem("num_made"), 1)
                    if h < 3:
                        wide_tile(z, 1, b)

                pe.wait_ge(sem("head_done"), (l + 1) * H)
                for h in range(H):
                    for e in range(2):
                        i = nc.tensor.matmul(st[:, h, :], ones[:, :], tmp[:, 2 * h + e, :], start=(e == 0), stop=(e == 1))
                i.then_inc(sem("hm_summed"), 1)
                pe.wait_ge(sem("hm_squared"), l + 1)
                for c in range(CT):
                    i = nc.tensor.matmul(ms[0][0:CT, 0, :], to_row[:, c // 2, :], hT[:, c, :], start=(c == 0), stop=(c == CT - 1))
                i.then_inc(sem("hm_summed"), 1)
                pe.wait_ge(sem("hm_inverse"), l + 1)
                for h in range(H):
                    i = nc.tensor.matmul(st[:, h, :], pick[:, h, :], vrow, start=True, stop=True)
                i.then_inc(sem("hm_spread"), 1)
                pe.wait_ge(sem("conv_ready"), l + 1)
                pe.wait_ge(sem("hm_done"), l + 1)
                for c in range(CT):
                    i = nc.tensor.matmul(st[:, c, :], ones[:, :], U[:, 16 + c, :], start=True, stop=True)
                    if c % 2:
                        i.then_inc(sem("gn_summed"), 1)
                for c in range(CT):
                    if c % 2 == 0:
                        pe.wait_ge(sem("gn_squared"), 4 * l + c // 2 + 1)
                    i = nc.tensor.matmul(ms[0][0:CT, 0, :], to_row[:, c, :], tmp[:, c, :], start=(c == 0), stop=(c == CT - 1))
                i.then_inc(sem("gn_var"), 1)
                pe.wait_ge(sem("gn_inverse"), l + 1)
                for c in range(CT):
                    i = nc.tensor.matmul(st[:, c, :], pick[:, c, :], vrow, start=True, stop=True)
                    if c % 2:
                        i.then_inc(sem("gn_spread"), 1)

                for j in range(8):
                    w = ring_slot(("w_out", l, j)).rearrange("p (k n) -> p k n", n=P)
                    b = take_bank()
                    for k in range(16):
                        if j == 0 and k >= 8:
                            pe.wait_ge(sem("mix_ready"), CT * l + k - 7)
                        i = nc.tensor.matmul(b[:, 0, :], w[:, k, :], U[:, 8 + k, :], start=(k == 0), stop=(k == 15))
                    i.then_inc(sem("slot_used"), 1)
                norm_sum()
                norm_sum()
                wide("w_ff1", l, list(range(16)), 16 * l + 8)
                pe.wait_ge(sem("proj_drained"), bank)
                for j in range(16):
                    w = ring_slot(("w_ff2", l, j)).rearrange("p (k n) -> p k n", n=P)
                    if j % 2 == 0:
                        b = take_bank()
                    for k in range(16):
                        kk = 16 * (j % 2) + k
                        i = nc.tensor.matmul(b[:, 0, :], w[:, k, :], U[:, kk, :], start=(kk == 0), stop=(kk == 31))
                    i.then_inc(sem("slot_used"), 1)
                if l == DEPTH - 1:
                    pe.wait_ge(sem("mem_scaled"), 1)
                    for c in range(CT):
                        for s in range(2):
                            i = nc.tensor.transpose(st[:, c, P * s:P * s + P], memtok[:, s, P * c:P * c + P], ident[:, :])
                    i.then_inc(sem("mem_turned"), 1)
                    pe.wait_ge(sem("bias_in"), 32)
                    nc.tensor.matmul(ms[1][0:NH, :, :].rearrange("p a t -> p (a t)"), rel[0:N_BUCKETS, :], onehot[0:N_BUCKETS, :],
                                     start=True, stop=True).then_inc(sem("bias_made"), 1)
                norm_sum()

            def second_slot(name):
                return ring_slot((name, 2, 0))

            def columns(name, src, h_first=False, by="proj_drained", k_tiles=CT, tiles=(0, 1), last=True):
                w = second_slot(name).rearrange("p (k n) -> p k n", k=k_tiles)
                b = take_bank(by)
                for n, m in enumerate(tiles):
                    for k in range(k_tiles):
                        if h_first and n == 0:
                            pe.wait_ge(sem("h_ready"), 4 * CT + k + 1)
                        i = nc.tensor.matmul(b[:, n, :], w[:, k, P * m:P * m + P], src[:, k, :], start=(k == 0), stop=(k == k_tiles - 1))
                if last:
                    i.then_inc(sem("slot_used"), 1)
                else:
                    i.then_inc(sem("half_slot"), 1)

            def tokens(name, src):
                w = second_slot(name).rearrange("p (k n) -> p k n", k=CT)
                b = take_bank()
                for n in range(2):
                    for k in range(CT):
                        i = nc.tensor.matmul(b[:, n, :], src[:, k, P * n:P * n + P], w[:, k, :], start=(k == 0), stop=(k == CT - 1))
                i.then_inc(sem("slot_used"), 1)

            norm_sum()
            columns("kcmp", hT, h_first=True)
            columns("vcmp", hT)
            for j in range(4):
                w = second_slot(f"q{j}").rearrange("p (k r n) -> p k r n", k=CT, r=2)
                b = take_bank()
                for r in range(2):
                    for k in range(CT):
                        i = nc.tensor.matmul(b[:, r, :], w[:, k, r, :], hT[:, k, :], start=(k == 0), stop=(k == CT - 1))
                i.then_inc(sem("slot_used"), 1)
            columns("ksel", hT)
            tokens("vsel", hT)
            columns("kwin", hT)
            tokens("vwin", hT)
            pe.wait_ge(sem("wgn_in"), 16)
            b = take_bank()
            for s in range(2):
                for k in range(CT):
                    i = nc.tensor.matmul(b[:, 0, 48 * s:48 * s + 48], hT[:, k, P * s:P * s + P], wgn[:, k, :], start=(k == 0), stop=(k == CT - 1))
            i.then_inc(sem("bgate_made"), 1)
            pe.wait_ge(sem("wcmp_in"), 64)
            pe.wait_ge(sem("blk_ready"), 1)
            for m in range(2):
                for h in range(2):
                    lo = HD * h
                    for i_ in range(CMP_LEN):
                        i = nc.tensor.matmul(ms[1][lo:lo + HD, 0, 32 * m:32 * m + 2 * NCMP].rearrange("p (g c) -> p g c", g=2),
                                             wcmp[lo:lo + HD, m, i_, :], blk[lo:lo + HD, m, :, :, i_],
                                             start=(i_ == 0), stop=(i_ == CMP_LEN - 1))
            i.then_inc(sem("cmp_made"), 1)
            columns("qx0", hT)
            columns("qx1", hT)
            pe.wait_ge(sem("cmp_kept"), 1)
            for g in range(2):
                i = nc.tensor.transpose(ms[1][0:NCMP, 1, P * g:P * g + P], cmpc[:, 1, g, :], ident[:, :])
            i.then_inc(sem("vc_turned"), 1)
            pe.wait_ge(sem("memT_ready"), 1)
            columns("memk0", memT)
            columns("memk1", memT)
            tokens("memv0", memT)
            tokens("memv1", memT)

            def scores(u):
                g, s = UNITS[u]
                if u:
                    pe.wait_ge(sem("scores_kept"), u)
                if g == "x":
                    for h in range(XH):
                        i = nc.tensor.matmul(st[:, h, :], qxT[:, h, P * s:P * s + P], kxT[:, h, :], start=True, stop=True)
                    i.then_inc(sem("scores2_made"), 1)
                    return
                gp, lo, n = g // 2, HD * (g % 2), P * (s + 1)
                for m in range(2):
                    for r in range(R):
                        nc.tensor.matmul(st[:, R * m + r, 0:n], q2T[lo:lo + HD, R * gp + r, P * s:P * s + P], kselT[lo:lo + HD, m, gp, 0:n],
                                         start=True, stop=True)
                for r in range(R):
                    i = nc.tensor.matmul(ms[0][:, 0, 16 * r:16 * r + NCMP], q2T[lo:lo + HD, R * gp + r, P * s:P * s + P],
                                         cmpc[lo:lo + HD, 0, gp, :], start=True, stop=True)
                i.then_inc(sem("scores2_made"), 1)

            def turn(u):
                g, s = UNITS[u]
                pb = probs[u % 2]
                pe.wait_ge(sem("probs_ready"), u + 1)
                for m in range(1 if g == "x" else 2):
                    for j in range(2 if g == "x" else s + 1):
                        b = take_bank().rearrange("p a t -> p (a t)")
                        for r in range(R):
                            i = nc.tensor.transpose(b[:, P * r:P * r + P], pb[:, m, r, P * j:P * j + P], ident[:, :])
                        i.then_inc(sem("turned"), 1)
                if g != "x":
                    nb = NCMP if s else NCMP // 2
                    b = take_bank().rearrange("p a t -> p (a t)")
                    for r in range(R):
                        i = nc.tensor.transpose(b[0:nb, P * r:P * r + P], pcmp[:, u % 2, r, 0:nb], ident[:, :])
                    i.then_inc(sem("turned"), 1)

            def values(u):
                g, s = UNITS[u]
                b = take_bank()
                pe.wait_ge(sem("turned_kept"), u + 1)
                if g == "x":
                    o = b.rearrange("p a t -> p (a t)")
                    for h in range(XH):
                        for j in range(2):
                            i = nc.tensor.matmul(o[:, P * h:P * h + P], vx[:, j, P * h:P * h + P], probsT[:, 0, j, h, :], start=(j == 0), stop=(j == 1))
                    i.then_inc(sem("o_made"), 1)
                    return
                nb = NCMP if s else NCMP // 2
                gp, lo = g // 2, HD * (g % 2)
                for hf in range(2):
                    o = b[HD * hf:HD * hf + HD, 0, :].rearrange("p (a t) -> p a t", a=2)
                    for m in range(2):
                        for j in range(s + 1):
                            nc.tensor.matmul(o, v2[:, m, j, HD * g:HD * g + HD], probsT[:, m, j, hf:R:2, :], start=(m == 0 and j == 0), stop=False)
                    i = nc.tensor.matmul(o, vc[0:nb, gp, lo:lo + HD], pcmpT[0:nb, hf:R:2, :], start=False, stop=True)
                i.then_inc(sem("o_made"), 1)

            pe.wait_ge(sem("vc_kept"), 1)
            pe.wait_ge(sem("vx_kept"), 1)
            scores(0)
            for u in range(len(UNITS)):
                if u + 1 < len(UNITS):
                    scores(u + 1)
                for name in FILL[u]:
                    if name == "mix":
                        pe.wait_ge(sem("wpg_in"), 16)
                        pe.wait_ge(sem("pooled"), 1)
                        for m in range(2):
                            b = take_bank()
                            for k in range(2):
                                i = nc.tensor.matmul(b[:, k, :], wpg[:, 2 * m + k, :], win[0][:, 2 * m + k, :], start=True, stop=True)
                            i.then_inc(sem("mixed"), 1)
                    elif name[:8] == "pool_out":
                        pe.wait_ge(sem("mix_kept"), 1)
                        columns(name, poolT, by="merge_drained", k_tiles=4, last=False)
                        columns(name, poolT, by="merge_drained", k_tiles=4, tiles=(2, 3))
                    else:
                        columns(name, hT)
                turn(u)
                values(u)
            pe.wait_ge(sem("o_kept"), len(UNITS))
            for j in range(4):
                columns(f"nsa_out{j}", oT, by="merge_drained")
            for j in range(2):
                columns(f"x_out{j}", oxT, by="merge_drained", k_tiles=4, last=False)
                columns(f"x_out{j}", oxT, by="merge_drained", k_tiles=4, tiles=(2, 3))
            pe.wait_ge(sem("merge_drained"), 12)
            for j in range(4):
                columns(f"w_o{j}", merged, by="merge_drained")
            pe.wait_ge(sem("sub_in"), 16)
            for c in range(2 * PH):
                i = nc.tensor.transpose(st[:, c // 2, P * (c % 2):P * (c % 2) + P], sub_raw[:, c, :], ident[:, :])
            i.then_inc(sem("sub_turned"), 1)
            norm_sum()
            for j in range(8):
                w = second_slot(f"peer_q{j}").rearrange("p (k n) -> p k n", k=CT)
                b = take_bank()
                for m in range(2):
                    for k in range(CT):
                        if j == 0 and m == 0:
                            pe.wait_ge(sem("h_ready"), 5 * CT + k + 1)
                        i = nc.tensor.matmul(b[:, m, :], w[:, k, P * m:P * m + P], hT[:, k, :], start=(k == 0), stop=(k == CT - 1))
                i.then_inc(sem("slot_used"), 1)
            pe.wait_ge(sem("sub_kept"), 1)
            pe.wait_ge(sem("qp_kept"), 1)
            for s in range(2):
                if s:
                    pe.wait_ge(sem("sub_scores_kept"), s)
                for c in range(2 * PH):
                    i = nc.tensor.matmul(st[:, c // 2, P * (c % 2):P * (c % 2) + P], qpT[:, c, P * s:P * s + P], subT[:, c, :], start=True, stop=True)
                i.then_inc(sem("sub_scores"), 1)
            pe.wait_ge(sem("sub_scores_kept"), 2)
            for n, src in enumerate((hT, xT)):
                if n:
                    pe.wait_ge(sem("tok_kept"), 1)
                for s in range(2):
                    for c in range(CT):
                        i = nc.tensor.transpose(st[:, 4 * s + c // 2, P * (c % 2):P * (c % 2) + P], src[:, c, P * s:P * s + P], ident[:, :])
                i.then_inc(sem("tok_turned"), 1)

        @block.scalar
        def _(act):
            steps = 0

            def link(i):
                nonlocal steps
                steps += 1
                i.then_inc(sem("act_step"), 1)
                act.wait_ge(sem("act_step"), steps)

            act.wait_ge(sem("x_turned"), 1)
            nc.scalar.copy(xT[:, :, :], st[:, :, :]).then_inc(sem("x_kept"), 1)
            for l in range(DEPTH):
                act.wait_ge(sem("params_turned"), l + 1)
                b = ms[l][:, :, :].rearrange("p s t -> p (s t)")
                nc.scalar.copy(pc[:, l, :], b[:, 0:NPC]).then_inc(sem("params_kept"), 1)
            act.wait_ge(sem("params_kept"), 2)
            nc.scalar.activation(c_act[:, :], pc[:, 0, C_COL:C_COL + 8], ACT.Silu).then_inc(sem("c_ready"), 1)
            act.wait_ge(sem("x_kept"), 1)
            act.wait_ge(sem("params2_turned"), 1)
            nc.scalar.copy(pc2[:, :], ms[0][:, 0, 0:28])
            nc.scalar.copy(pe_T[:, :, :].rearrange("p m i -> p (m i)"), ms[0][:, 1, 0:2 * CMP_LEN]).then_inc(sem("params2_kept"), 1)
            act.wait_ge(sem("params2_kept"), 1)

            norms = 0
            bank = 0
            qkv = 0

            def drain(dst, func, n=2, job=None):
                nonlocal bank, qkv
                if job:
                    act.wait_ge(sem("slot_used"), job_at[job] + 1)
                else:
                    qkv += 1
                    act.wait_ge(sem("qkv_made"), qkv)
                i = nc.scalar.activation(dst, pj[bank % 2][:, 0:n, :], func)
                i.then_inc(sem("proj_drained"), 1)
                bank += 1
                return i

            def norm(src, x_at=None):
                nonlocal norms
                if src is xT:
                    for c in range(CT):
                        if norms and x_at is not None:
                            act.wait_ge(sem("x_ready"), x_at + c + 1)
                        nc.scalar.activation(tmp[:, c, :], src[:, c, :], ACT.Square).then_inc(sem("squares"), 1)
                norms += 1
                act.wait_ge(sem("norm_summed"), norms)
                if norms > 1:
                    act.wait_ge(sem("rstd_used"), norms - 1)
                nc.scalar.activation(rstd[:, :], ms[0][:, 0, :], ACT.Sqrt, bias=eps_col[:, 0:1], scale=1.0 / D).then_inc(sem("std_ready"), 1)

            h_tiles = 0

            def finish_h(shift):
                nonlocal h_tiles
                for c in range(CT):
                    h_tiles += 1
                    act.wait_ge(sem("h_scaled"), h_tiles)
                    nc.scalar.activation(hT[:, c, :], hT[:, c, :], ACT.Identity, bias=modc[:, shift + c:shift + c + 1]).then_inc(sem("h_ready"), 1)

            def drain_y(c, job):
                i = drain(y[:, c:c + 1, :], ACT.Copy, 1, job)
                act.wait_ge(sem("proj_drained"), bank)
                nc.scalar.activation(tmp[:, c, :], y[:, c, :], ACT.Square).then_inc(sem("squares"), 1)

            def drain_u(l, js):
                for j in js:
                    drain(U[:, 2 * j:2 * j + 2, :], ACT.Sigmoid if j >= 12 or 4 <= j < 8 else ACT.Copy, job=("w_in", l, j))

            for l in range(DEPTH):
                norm(xT, CT * (2 * l - 1) if l else None)
                finish_h(0)
                drain_u(l, W_IN_ORDER[:12])
                for h in range(H):
                    drain(vT[:, 2 * h:2 * h + 2, :], ACT.Copy)
                for s in range(2):
                    for hp in range(2):
                        drain(vtok[:, s, 512 * hp:512 * hp + 512].rearrange("p (a t) -> p a t", a=2), ACT.Copy)
                act.wait_ge(sem("conv_m_ready"), l + 1)
                nc.scalar.activation(xc[:, :, :], xc[:, :, :], ACT.Silu).then_inc(sem("xc_ready"), 1)
                for dst in (qT, kT):
                    for h in range(H):
                        drain(dst[:, 2 * h:2 * h + 2, :], ACT.Copy)

                act.wait_ge(sem("gates_made"), l + 1)
                nc.scalar.activation(gates[:, :], ms[0][0:2 * H, 0, :], ACT.Identity, bias=bg[:, 0:1]).then_inc(sem("gates_kept"), 1)
                act.wait_ge(sem("qkv_made"), 16 * (l + 1))
                act.wait_ge(sem("fg_moved"), l + 1)
                link(nc.scalar.activation(fgr[:, 0, :], ms[0][0:H, 1, :], ACT.Copy))
                link(nc.scalar.activation(fgr[:, 1, :], fgr[:, 0, :], ACT.Abs))
                link(nc.scalar.activation(fgr[:, 1, :], fgr[:, 1, :], ACT.Exp, scale=-1.0))
                nc.scalar.activation(fgr[:, 2, :], fgr[:, 1, :], ACT.Ln, bias=ones[0:H, 0:1]).then_inc(sem("softplus"), 1)
                drain_u(l, [4])
                act.wait_ge(sem("m_ready"), l + 1)
                nc.scalar.activation(rows[:, 1, :], lrow[:, 1, :], ACT.Exp, scale=-1.0).then_inc(sem("rows_ready"), 1)
                act.wait_ge(sem("r_turned"), l + 1)
                nc.scalar.copy(rcol[:, :, :].rearrange("p s h -> p (s h)"), ms[0][:, 0, 0:2 * H]).then_inc(sem("rcol_kept"), 1)

                for h in range(H):
                    hn = l * H + h
                    act.wait_ge(sem("rows_spread"), hn + 1)
                    if hn:
                        act.wait_ge(sem("head_done"), hn)
                    nc.scalar.copy(en_b[:, :], ms[0][:, 1, :]).then_inc(sem("en_kept"), 1)
                    act.wait_ge(sem("wlog_ready"), hn + 1)
                    nc.scalar.activation(wlog[:, 0, :], wlog[:, 0, :], ACT.Exp)
                    nc.scalar.activation(wlog[:, 1, P:T], wlog[:, 1, P:T], ACT.Exp).then_inc(sem("w_ready"), 1)
                    if h < 3:
                        drain_u(l, [5 + h])

                act.wait_ge(sem("hm_centred"), l + 1)
                nc.scalar.activation(hT[:, :, :], tmp[:, :, :], ACT.Square).then_inc(sem("hm_squared"), 1)
                act.wait_ge(sem("hm_summed"), 2 * l + 2)
                nc.scalar.activation(vrow, ms[0][0:CT, 0, :], ACT.Sqrt, bias=eps_col[0:CT, 0:1], scale=1.0 / DH).then_inc(sem("hm_std"), 1)

                for b in range(4):
                    act.wait_ge(sem("gn_centred"), 4 * l + b + 1)
                    nc.scalar.activation(tmp[:, 2 * b:2 * b + 2, :], U[:, 16 + 2 * b:18 + 2 * b, :], ACT.Square).then_inc(sem("gn_squared"), 1)
                act.wait_ge(sem("gn_var"), l + 1)
                nc.scalar.activation(vrow, ms[0][0:CT, 0, :], ACT.Sqrt, bias=eps_col[0:CT, 0:1], scale=1.0 / P).then_inc(sem("gn_std"), 1)
                for c in range(CT):
                    if c % 2 == 0:
                        act.wait_ge(sem("gn_scaled"), 4 * l + c // 2 + 1)
                    nc.scalar.activation(U[:, 16 + c, :], U[:, 16 + c, :], ACT.Silu, bias=pc[:, l, B_CN + c:B_CN + c + 1],
                                         scale=pc[:, l, G_CN + c:G_CN + c + 1]).then_inc(sem("mix_ready"), 1)

                for c in range(CT):
                    drain_y(c, ("w_out", l, c))
                norm(y)
                norm(xT, CT * 2 * l)
                finish_h(24)
                for j in range(16):
                    link_dst = U[:, 2 * j:2 * j + 2, :]
                    act.wait_ge(sem("slot_used"), job_at[("w_ff1", l, j)] + 1)
                    link(nc.scalar.activation(link_dst, pj[bank % 2][:, :, :], ACT.Relu))
                    nc.scalar.activation(link_dst, link_dst, ACT.Square).then_inc(sem("proj_drained"), 1)
                    bank += 1
                if l == DEPTH - 1:
                    act.wait_ge(sem("mem_in"), 16)
                    for t in range(2):
                        link(nc.scalar.activation(wqkv_free[:, :], memtok[:, t, :], ACT.Square, accum_out=mstat[:, 0, t:t + 1]))
                    nc.scalar.activation(mstat[:, 1, :], mstat[:, 0, :], ACT.Sqrt, bias=eps_col[:, 0:1], scale=1.0 / D).then_inc(sem("mem_std"), 1)
                for c in range(CT):
                    drain_y(c, ("w_ff2", l, 2 * c + 1))
                if l == DEPTH - 1:
                    act.wait_ge(sem("mem_turned"), 1)
                    for c in range(CT):
                        i = nc.scalar.activation(memT[:, c, :], st[:, c, :], ACT.Copy, scale=pc2[:, G_MEM2 + c:G_MEM2 + c + 1])
                    i.then_inc(sem("memT_ready"), 1)
                    act.wait_ge(sem("bias_made"), 1)
                    nc.scalar.copy(bias_w[0:NH, 0:T], ms[1][0:NH, 0, :]).then_inc(sem("bias_copied"), 1)
                norm(y)

            def drain2(dst, name, func=ACT.Copy, shape=None):
                nonlocal bank
                act.wait_ge(sem("slot_used"), job_at[(name, 2, 0)] + 1)
                src = pj[bank_of()][:, :, :]
                if shape:
                    src = src.rearrange("p a t -> p (a t)")
                bank += 1
                return nc.scalar.activation(dst, src, func).then_inc(sem("proj_drained"), 1)

            merged_banks = 0

            def bank_of():
                return (bank + merged_banks) % 2

            norm(xT, CT * (2 * DEPTH - 1))
            drain2(cmpT[:, 0], "kcmp")
            drain2(cmpT[:, 1], "vcmp")
            act.wait_ge(sem("proj_drained"), bank)
            act.sem_inc(sem("cmpT_kept"), 1)
            for j in range(4):
                drain2(q2T[:, 2 * j:2 * j + 2, :], f"q{j}")
            act.wait_ge(sem("bias_out"), 16)
            drain2(kselT[:, 0], "ksel")
            drain2(v2[:, 0], "vsel")
            drain2(kselT[:, 1], "kwin")
            drain2(v2[:, 1], "vwin")
            act.wait_ge(sem("bgate_made"), 1)
            nc.scalar.activation(bgate[:, :, :].rearrange("p s n -> p (s n)"), pj[bank_of()][:, 0, 0:96], ACT.Sigmoid).then_inc(sem("proj_drained"), 1)
            bank += 1
            act.wait_ge(sem("cmp_made"), 1)
            nc.scalar.copy(cmpc[:, 0].rearrange("p g c -> p (g c)"), ms[1][:, 0, 0:2 * NCMP])
            nc.scalar.copy(cmpc[:, 1].rearrange("p g c -> p (g c)"), ms[1][:, 0, 32:32 + 2 * NCMP]).then_inc(sem("cmp_kept"), 1)
            drain2(qxT[:, 0:2, :], "qx0")
            drain2(qxT[:, 2:4, :], "qx1")
            act.wait_ge(sem("vc_turned"), 1)
            nc.scalar.copy(vc[:, :, :].rearrange("p g e -> p (g e)"), ms[1][0:NCMP, 1, :]).then_inc(sem("vc_kept"), 1)
            drain2(kxT[:, 0:2, :], "memk0")
            drain2(kxT[:, 2:4, :], "memk1")
            drain2(vx[:, :, 0:256], "memv0")
            drain2(vx[:, :, 256:512], "memv1")
            act.wait_ge(sem("proj_drained"), bank)
            act.sem_inc(sem("vx_kept"), 1)

            turned = 0
            for u, (g, s) in enumerate(UNITS):
                act.wait_ge(sem("max_ready"), u + 1)
                pb, sv = probs[u % 2], stat[:, u % 2]
                n = P * (s + 1)
                if g == "x":
                    for h in range(XH):
                        i = nc.scalar.activation(pb[:, 0, h, :], pb[:, 0, h, :], ACT.Exp, bias=sv[:, 0, 1, h:h + 1], accum_out=sv[:, 1, 1, h:h + 1])
                else:
                    nb = NCMP if s else NCMP // 2
                    for r in range(R):
                        nc.scalar.activation(pcmp[:, u % 2, r, 0:nb], pcmp[:, u % 2, r, 0:nb], ACT.Exp, bias=sv[:, 0, 0, r:r + 1], accum_out=sv[:, 1, 0, r:r + 1])
                        for m in range(2):
                            i = nc.scalar.activation(pb[:, m, r, 0:n], pb[:, m, r, 0:n], ACT.Exp, bias=sv[:, 0, 1 + m, r:r + 1], accum_out=sv[:, 1, 1 + m, r:r + 1])
                i.then_inc(sem("exp_done"), 1)
                for name in FILL[u]:
                    if name[:2] == "gm":
                        j = int(name[2:])
                        drain2(gm[:, 2 * j:2 * j + 2, :], name, ACT.Sigmoid)
                    elif name == "mix":
                        for m in range(2):
                            act.wait_ge(sem("mixed"), m + 1)
                            for k in range(2):
                                c = 2 * m + k
                                i = nc.scalar.activation(poolT[:, c, :], pj[bank_of()][:, k, :], ACT.Copy, scale=pc2[:, POOL_SC2 + c:POOL_SC2 + c + 1])
                            i.then_inc(sem("proj_drained"), 1)
                            bank += 1
                        act.wait_ge(sem("proj_drained"), bank)
                        act.sem_inc(sem("mix_kept"), 1)
                    elif name[:8] == "pool_out":
                        merged_banks += 2
                    else:
                        j = int(name[4:])
                        drain2(poolT[:, 2 * j:2 * j + 2, :], name)
                        if j == 1:
                            act.wait_ge(sem("proj_drained"), bank)
                            act.sem_inc(sem("pool_kept"), 1)
                for m in range(1 if g == "x" else 2):
                    for j in range(2 if g == "x" else s + 1):
                        turned += 1
                        act.wait_ge(sem("turned"), turned)
                        nc.scalar.copy(probsT[:, m, j].rearrange("p r t -> p (r t)"), pj[bank_of()][:, :, :].rearrange("p a t -> p (a t)")).then_inc(sem("proj_drained"), 1)
                        bank += 1
                if g != "x":
                    turned += 1
                    act.wait_ge(sem("turned"), turned)
                    nc.scalar.copy(pcmpT[0:nb, :, :].rearrange("p r t -> p (r t)"), pj[bank_of()][0:nb, :, :].rearrange("p a t -> p (a t)")).then_inc(sem("proj_drained"), 1)
                    bank += 1
                act.wait_ge(sem("proj_drained"), bank)
                act.sem_inc(sem("turned_kept"), 1)
                act.wait_ge(sem("o_made"), u + 1)
                o = pj[bank_of()]
                if g == "x":
                    i = nc.scalar.copy(oxT[:, :, P * s:P * s + P], o[:, :, :].rearrange("p a t -> p (a t)").rearrange("p (h t) -> p h t", h=XH))
                else:
                    i = nc.scalar.copy(oT[:, 2 * g:2 * g + 2, P * s:P * s + P], o[:, 0, :].rearrange("p (a t) -> p a t", a=2))
                i.then_inc(sem("proj_drained"), 1)
                bank += 1
                act.wait_ge(sem("proj_drained"), bank)
                act.sem_inc(sem("o_kept"), 1)
            act.sem_inc(sem("attention_done"), 1)
            merged_banks += 12
            act.wait_ge(sem("sub_turned"), 1)
            nc.scalar.copy(subT.rearrange("p c t -> p (c t)"), st[:, :, :].rearrange("p c t -> p (c t)")).then_inc(sem("sub_kept"), 1)
            act.wait_ge(sem("x2_ready"), 1)
            norm(xT)
            for j in range(8):
                drain2(qpT[:, 2 * j:2 * j + 2, :], f"peer_q{j}")
            act.wait_ge(sem("proj_drained"), bank)
            act.sem_inc(sem("qp_kept"), 1)
            for s in range(2):
                act.wait_ge(sem("sub_scores"), s + 1)
                if s:
                    act.wait_ge(sem("top_done"), s)
                nc.scalar.copy(s_sb.rearrange("p c t -> p (c t)"), st[:, :, :].rearrange("p c t -> p (c t)")).then_inc(sem("sub_scores_kept"), 1)
                if s == 0:
                    act.wait_ge(sem("best_ready"), 1)
                    nc.scalar.activation(gate[:, 0], gate[:, 0], ACT.Exp).then_inc(sem("gate_exp"), 1)
            for n, dst in enumerate((h_tok, acc)):
                act.wait_ge(sem("tok_turned"), n + 1)
                nc.scalar.copy(dst.rearrange("p s d -> p (s d)"), st[:, :, :].rearrange("p c t -> p (c t)")).then_inc(sem("tok_kept"), 1)
            act.wait_ge(sem("best_ready"), 2)
            nc.scalar.activation(gate[:, 1], gate[:, 1], ACT.Exp).then_inc(sem("gate_exp"), 1)
            for n in range(2 * PH):
                s, h = divmod(n, PH)
                act.wait_ge(sem("dots_ready"), n + 1)
                nc.scalar.activation(wgt[:, s, h, :], dots[:, s, h, :], ACT.Gelu).then_inc(sem("gelu_done"), 1)
            for s in range(2):
                act.wait_ge(sem("acc_ready"), s + 1)
                link(nc.scalar.activation(h_tok[:, s, :], acc[:, s, :], ACT.Square, accum_out=mstat[:, 0, s:s + 1]))
                nc.scalar.activation(mstat[:, 1, s:s + 1], mstat[:, 0, s:s + 1], ACT.Sqrt, bias=eps_col[:, 0:1], scale=1.0 / D).then_inc(sem("last_std"), 1)

        @block.vector
        def _(dve):
            steps = 0
            norms = 0

            def count(i):
                nonlocal steps
                steps += 1
                i.then_inc(sem("dve_step"), 1)
                return steps

            def link(i):
                dve.wait_ge(sem("dve_step"), count(i))

            def rsqrt_finish():
                nonlocal norms
                norms += 1
                dve.wait_ge(sem("std_ready"), norms)
                link(nc.vector.reciprocal(rstd[:, :], rstd[:, :]))

            def over_channels(t):
                return t.unsqueeze(1).broadcast_to([P, CT, T])

            def col(l, at, c):
                return pc[:, l, at + c:at + c + 1]

            def pre_norm(l, which):
                rsqrt_finish()
                for c in range(CT):
                    i = nc.vector.scalar_tensor_tensor(hT[:, c, :], xT[:, c, :], mod_scale[:, which, c:c + 1], rstd[:, :], ALU.mult, ALU.mult)
                    i.then_inc(sem("h_scaled"), 1)
                dve.wait_ge(sem("h_scaled"), (2 * l + (which == 1) + 1) * CT)
                dve.sem_inc(sem("rstd_used"), 1)

            def post_norm(l, which):
                rsqrt_finish()
                scaled = []
                for c in range(CT):
                    scaled.append(count(nc.vector.scalar_tensor_tensor(y[:, c, :], y[:, c, :], mod_scale[:, which, c:c + 1], rstd[:, :],
                                                                       ALU.mult, ALU.mult)))
                    if c:
                        dve.wait_ge(sem("dve_step"), scaled[c - 1])
                        nc.vector.tensor_tensor(xT[:, c - 1, :], xT[:, c - 1, :], y[:, c - 1, :], ALU.add).then_inc(sem("x_ready"), 1)
                dve.wait_ge(sem("dve_step"), scaled[-1])
                nc.vector.tensor_tensor(xT[:, CT - 1, :], xT[:, CT - 1, :], y[:, CT - 1, :], ALU.add).then_inc(sem("x_ready"), 1)
                dve.sem_inc(sem("rstd_used"), 1)

            last = {}

            def tap(l, dst, src, taps, w, bias, back, signal=None):
                for c in range(CT):
                    wc = col(l, w, (taps - 1 - back) * CT + c)
                    if back == 0:
                        i = nc.vector.tensor_scalar(dst[:, c, :], src[:, c, :], wc, col(l, bias, c), ALU.mult, ALU.add)
                    else:
                        dve.wait_ge(sem("dve_step"), last[c])
                        i = nc.vector.scalar_tensor_tensor(dst[:, c, back:T], src[:, c, 0:T - back], wc, dst[:, c, back:T], ALU.mult, ALU.add)
                    if signal and c == CT - 1:
                        i.then_inc(sem(signal), 1)
                    else:
                        last[c] = count(i)

            done_taps = 0

            def long_taps(l, n):
                nonlocal done_taps
                for back in range(done_taps, min(done_taps + n, KC)):
                    tap(l, U[:, 16:24], U[:, 24:32], KC, W_DW, B_DW, back, "conv_ready" if back == KC - 1 else None)
                done_taps = min(done_taps + n, KC)

            dve.wait_ge(sem("consts"), 1)
            dve.wait_ge(sem("consts2"), 1)
            dve.wait_ge(sem("params2_kept"), 1)
            dve.wait_ge(sem("params_kept"), 2)
            dve.wait_ge(sem("x_kept"), 1)
            for l in range(DEPTH):
                def modulation(first, last_col, kinds):
                    link(nc.vector.tensor_tensor(modc[:, first:last_col], ms[1][:, 0, first:last_col], pc[:, l, B_ADA + first:B_ADA + last_col], ALU.add))
                    for n in kinds:
                        src, g, one = ((8, G_PRE_MIX, 1.0), (32, G_PRE_MLP, 1.0), (16, G_POST_MIX, 0.0), (40, G_POST_MLP, 0.0))[n]
                        i = nc.vector.scalar_tensor_tensor(mod_scale[:, n, :], modc[:, src:src + 8], one, pc[:, l, g:g + 8], ALU.add, ALU.mult)
                    link(i)

                if l == 0:
                    dve.wait_ge(sem("mod_first"), 1)
                    modulation(0, 16, (0,))
                else:
                    dve.wait_ge(sem("mod_summed"), l + 1)
                    modulation(0, 48, (0, 1, 2, 3))
                    dve.sem_inc(sem("mod_kept"), 1)
                pre_norm(l, 0)

                dve.wait_ge(sem("proj_drained"), 64 * l + 4)
                for back in range(KM):
                    tap(l, xc, U[:, 0:8], KM, W_CONV, B_CONV_M, back, "conv_m_ready" if back == KM - 1 else None)
                dve.wait_ge(sem("proj_drained"), 64 * l + 12)
                link(nc.vector.tensor_tensor(U[:, 24:32, :], U[:, 16:24, :], U[:, 24:32, :], ALU.mult))
                done_taps = 0
                long_taps(l, 13)

                dve.wait_ge(sem("softplus"), l + 1)
                link(nc.vector.scalar_tensor_tensor(lrow[:, 0, :], fgr[:, 0, :], 0.0, fgr[:, 2, :], ALU.min, ALU.subtract))
                link(nc.vector.tensor_tensor_scan(lrow[:, 3, :], lrow[:, 0, :], zrow[:, :], 0.0, ALU.add, ALU.add))
                link(nc.vector.tensor_tensor(lrow[:, 2, :], gates[0:H, :], lrow[:, 3, :], ALU.subtract))
                link(nc.vector.tensor_tensor_scan(lrow[:, 0, :], lrow[:, 2, :], zrow[:, :], 0.0, ALU.max, ALU.add))
                nc.vector.tensor_scalar(rows[:, 0, :], lrow[:, 0, :], -1.0, None, ALU.mult)
                nc.vector.tensor_tensor(lrow[:, 1, :], lrow[:, 3, :], lrow[:, 0, :], ALU.add).then_inc(sem("m_ready"), 1)

                if l == 0:
                    dve.wait_ge(sem("mod_summed"), 1)
                    modulation(16, 48, (1, 2, 3))
                    dve.sem_inc(sem("mod_kept"), 1)
                dve.wait_ge(sem("rcol_kept"), l + 1)
                for h in range(H):
                    hn = l * H + h
                    dve.wait_ge(sem("en_kept"), hn + 1)
                    for s in range(2):
                        i = nc.vector.scalar_tensor_tensor(wlog[:, s, P * s:T], ms[0][:, 0, P * s:T], rcol[:, s, h:h + 1], causal[:, s, P * s:T], ALU.add, ALU.add)
                    i.then_inc(sem("wlog_ready"), 1)
                    long_taps(l, 1)
                    dve.wait_ge(sem("w_ready"), hn + 1)
                    dve.wait_ge(sem("scores_made"), hn + 1)
                    for s in range(2):
                        i = nc.vector.scalar_tensor_tensor(sT[:, s, P * s:T], ms[1][:, s, P * s:T], DH ** -0.5, wlog[:, s, P * s:T], ALU.mult, ALU.mult)
                    i.then_inc(sem("s_ready"), 1)
                    long_taps(l, 1)
                    dve.wait_ge(sem("num_made"), hn + 1)
                    link(nc.vector.tensor_scalar(den[:, :], st[:, 4, :], -1.0, None, ALU.mult))
                    link(nc.vector.tensor_tensor(den[:, :], den[:, :], st[:, 4, :], ALU.max))
                    link(nc.vector.tensor_tensor(den[:, :], den[:, :], en_b[:, :], ALU.max))
                    link(nc.vector.reciprocal(den[:, :], den[:, :]))
                    nc.vector.tensor_tensor(tmp[:, 2 * h:2 * h + 2, :], st[:, 6:8, :], den[:, :].unsqueeze(1).broadcast_to([P, 2, T]), ALU.mult).then_inc(sem("head_done"), 1)
                dve.wait_ge(sem("hm_summed"), 2 * l + 1)
                for h in range(H):
                    for e in range(2):
                        i = nc.vector.scalar_tensor_tensor(tmp[:, 2 * h + e, :], st[:, h, :], -1.0 / DH, tmp[:, 2 * h + e, :], ALU.mult, ALU.add)
                i.then_inc(sem("hm_centred"), 1)
                long_taps(l, 3)
                dve.wait_ge(sem("hm_std"), l + 1)
                nc.vector.reciprocal(vrow, vrow).then_inc(sem("hm_inverse"), 1)
                long_taps(l, 1)
                dve.wait_ge(sem("hm_spread"), l + 1)
                for c in range(CT):
                    i = nc.vector.scalar_tensor_tensor(tmp[:, c, :], tmp[:, c, :], col(l, G_MH, c), st[:, c // 2, :], ALU.mult, ALU.mult)
                link(i)
                dve.sem_inc(sem("hm_done"), 1)
                long_taps(l, KC)
                link(nc.vector.tensor_tensor(U[:, 8:16, :], tmp[:, :, :], U[:, 8:16, :], ALU.mult))
                for b in range(4):
                    dve.wait_ge(sem("gn_summed"), 4 * l + b + 1)
                    nc.vector.scalar_tensor_tensor(U[:, 16 + 2 * b:18 + 2 * b, :], st[:, 2 * b:2 * b + 2, :], -1.0 / P, U[:, 16 + 2 * b:18 + 2 * b, :],
                                                   ALU.mult, ALU.add).then_inc(sem("gn_centred"), 1)
                dve.wait_ge(sem("gn_std"), l + 1)
                nc.vector.reciprocal(vrow, vrow).then_inc(sem("gn_inverse"), 1)
                for b in range(4):
                    dve.wait_ge(sem("gn_spread"), 4 * l + b + 1)
                    nc.vector.tensor_tensor(U[:, 16 + 2 * b:18 + 2 * b, :], U[:, 16 + 2 * b:18 + 2 * b, :], st[:, 2 * b:2 * b + 2, :], ALU.mult).then_inc(sem("gn_scaled"), 1)

                post_norm(l, 2)
                pre_norm(l, 1)
                if l == DEPTH - 1:
                    dve.wait_ge(sem("mem_std"), 1)
                    link(nc.vector.reciprocal(mstat[:, 1, :], mstat[:, 1, :]))
                    for t in range(2):
                        i = nc.vector.tensor_scalar(memtok[:, t, :], memtok[:, t, :], mstat[:, 1, t:t + 1], None, ALU.mult)
                    i.then_inc(sem("mem_scaled"), 1)
                    dve.wait_ge(sem("bias_in"), 32)
                    nc.vector.memset(bias_w[0:NH, T:512], NEG).then_inc(sem("bias_masked"), 1)
                post_norm(l, 3)

            def gain_norm(g, n):
                rsqrt_finish()
                for c in range(CT):
                    i = nc.vector.scalar_tensor_tensor(hT[:, c, :], xT[:, c, :], pc2[:, g + c:g + c + 1], rstd[:, :], ALU.mult, ALU.mult)
                    i.then_inc(sem("h_ready"), 1)
                dve.wait_ge(sem("h_ready"), n * CT)
                dve.sem_inc(sem("rstd_used"), 1)

            dve.wait_ge(sem("x_ready"), 2 * DEPTH * CT)
            gain_norm(G_MIX2, 5)
            dve.wait_ge(sem("cmpT_kept"), 1)
            for m in range(2):
                for g in range(2):
                    for hf in range(2):
                        src = cmpT[:, m, g, 16 * hf:16 * hf + 16 * NCMP].rearrange("p (c i) -> p c i", i=16)
                        i = nc.vector.tensor_tensor(blk[:, m, g, :, 16 * hf:16 * hf + 16], src,
                                                    pe_T[:, m, 16 * hf:16 * hf + 16].unsqueeze(1).broadcast_to([P, NCMP, 16]), ALU.add)
            i.then_inc(sem("blk_ready"), 1)
            dve.wait_ge(sem("proj_drained"), GATE_BANK)
            link(nc.vector.tensor_scalar(bgate[:, 0, 0:NH], bgate[:, 0, 0:NH], has[:, 0:1], None, ALU.mult))
            dve.wait_ge(sem("toeplitz_in"), 32)
            merge_jobs = 0

            def merge(job, tiles, branch, how):
                nonlocal merge_jobs
                sm, v, b = job
                dve.wait_ge(sem(sm), v)
                src = pj[b][:, :, :]
                if how == "x":
                    i = nc.vector.tensor_tensor(xT[:, tiles:tiles + 2, :], xT[:, tiles:tiles + 2, :], src, ALU.add)
                    return i.then_inc(sem("merge_drained"), 1)
                g = gm[:, CT * branch + tiles:CT * branch + tiles + 2, :]
                dst = merged[:, tiles:tiles + 2, :]
                if how == "first":
                    i = nc.vector.tensor_tensor(dst, src, g, ALU.mult)
                    return i.then_inc(sem("merge_drained"), 1)
                link(nc.vector.tensor_tensor(g, src, g, ALU.mult))
                nc.vector.tensor_tensor(dst, dst, g, ALU.add).then_inc(sem("merge_drained"), 1)

            for u, (g, s) in enumerate(UNITS):
                pb, sv = probs[u % 2], stat[:, u % 2]
                n = P * (s + 1)
                dve.wait_ge(sem("scores2_made"), u + 1)
                if u == 1:
                    dve.wait_ge(sem("vx_kept"), 1)
                if g == "x":
                    link(nc.vector.tensor_scalar(pb[:, 0], st[:, 0:R, :], float(P) ** -0.5, None, ALU.mult))
                    dve.sem_inc(sem("scores_kept"), 1)
                    link(nc.vector.tensor_reduce(sv[:, 0, 1, :], pb[:, 0], AX.X, ALU.max))
                    nc.vector.tensor_scalar(sv[:, 0, 1, :], sv[:, 0, 1, :], -1.0, None, ALU.mult).then_inc(sem("max_ready"), 1)
                else:
                    nb = NCMP if s else NCMP // 2
                    bs = bias[s][:, R * g:R * g + R, :]
                    nc.vector.scalar_tensor_tensor(pcmp[:, u % 2, :, 0:nb], ms[0][:, 0, 0:64].rearrange("p (r c) -> p r c", c=16)[:, :, 0:nb],
                                                   HD ** -0.5, bs[:, :, CMP_LEN - 1:CMP_LEN + CMP_STRIDE * (nb - 1):CMP_STRIDE], ALU.mult, ALU.add)
                    for m in range(2):
                        i = nc.vector.scalar_tensor_tensor(pb[:, m, :, 0:n], st[:, R * m:R * m + R, 0:n], HD ** -0.5, bs, ALU.mult, ALU.add)
                    link(i)
                    dve.sem_inc(sem("scores_kept"), 1)
                    nc.vector.tensor_reduce(sv[:, 0, 0, :], pcmp[:, u % 2, :, 0:nb], AX.X, ALU.max)
                    for m in range(2):
                        i = nc.vector.tensor_reduce(sv[:, 0, 1 + m, :], pb[:, m, :, 0:n], AX.X, ALU.max)
                    link(i)
                    nc.vector.tensor_scalar(sv[:, 0], sv[:, 0], -1.0, None, ALU.mult).then_inc(sem("max_ready"), 1)
                dve.wait_ge(sem("exp_done"), u + 1)
                if g == "x":
                    link(nc.vector.reciprocal(sv[:, 2, 1, :], sv[:, 1, 1, :]))
                    nc.vector.tensor_tensor(pb[:, 0], pb[:, 0], sv[:, 2, 1, :].unsqueeze(2).broadcast_to([P, R, T]), ALU.mult).then_inc(sem("probs_ready"), 1)
                else:
                    link(nc.vector.reciprocal(sv[:, 2], sv[:, 1]))
                    gates3 = bgate[:, s, :].rearrange("p (m h) -> p m h", m=3)[:, :, R * g:R * g + R]
                    link(nc.vector.tensor_tensor(sv[:, 2], sv[:, 2], gates3, ALU.mult))
                    nc.vector.tensor_tensor(pcmp[:, u % 2, :, 0:nb], pcmp[:, u % 2, :, 0:nb], sv[:, 2, 0, :].unsqueeze(2).broadcast_to([P, R, nb]), ALU.mult)
                    for m in range(2):
                        i = nc.vector.tensor_tensor(pb[:, m, :, 0:n], pb[:, m, :, 0:n], sv[:, 2, 1 + m, :].unsqueeze(2).broadcast_to([P, R, n]), ALU.mult)
                    i.then_inc(sem("probs_ready"), 1)
                if u == 0:
                    dve.wait_ge(sem("pool_kept"), 1)
                    dve.wait_ge(sem("cmp_made"), 1)
                    dve.wait_ge(sem("rcount_in"), 16)
                    src = poolT
                    for k in range(4):
                        sh, dst = 1 << k, win[k % 2]
                        nc.vector.tensor_copy(dst[:, k:4, 0:sh], src[:, k:4, 0:sh])
                        link(nc.vector.tensor_tensor(dst[:, k:4, sh:T], src[:, k:4, sh:T], src[:, k:4, 0:T - sh], ALU.add))
                        src = dst
                    for k in range(4):
                        i = nc.vector.tensor_tensor(win[k % 2][:, k, :], win[k % 2][:, k, :], rc[:, k, :], ALU.mult)
                    link(i)
                    for k in range(4):
                        i = nc.vector.tensor_tensor(win[0][:, k, :], win[k % 2][:, k, :], poolT[:, k, :], ALU.subtract)
                    i.then_inc(sem("pooled"), 1)
                if FILL[u] and FILL[u][0] == "pool_out0":
                    for j in range(2):
                        for k in range(2):
                            done = ("half_slot", j + 1, MERGE_BANKS[2 * j + k]) if k == 0 else ("slot_used", job_at[(f"pool_out{j}", 2, 0)] + 1, MERGE_BANKS[2 * j + k])
                            merge(done, 4 * j + 2 * k, 0, "first")
            for j in range(4):
                merge(("slot_used", job_at[(f"nsa_out{j}", 2, 0)] + 1, MERGE_BANKS[4 + j]), 2 * j, 1, "more")
            for j in range(2):
                for k in range(2):
                    done = ("half_slot", 2 + j + 1, MERGE_BANKS[8 + 2 * j + k]) if k == 0 else ("slot_used", job_at[(f"x_out{j}", 2, 0)] + 1, MERGE_BANKS[8 + 2 * j + k])
                    merge(done, 4 * j + 2 * k, 2, "more")
            for j in range(4):
                merge(("slot_used", job_at[(f"w_o{j}", 2, 0)] + 1, MERGE_BANKS[12 + j]), 2 * j, 0, "x")
            dve.wait_ge(sem("merge_drained"), 16)
            dve.sem_inc(sem("x2_ready"), 1)
            gain_norm(G_FFN2, 6)
            for s in range(2):
                dve.wait_ge(sem("sub_scores_kept"), s + 1)
                top_of(dve, link, s_sb, top_v, top_i, 2 * PH)
                tv = top_v[:, :, :].rearrange("p (h q) k -> p h q k", q=2)
                cands = cand.rearrange("p h (i j) -> p h i j", i=TOPK)
                link(nc.vector.tensor_tensor(cands, tv[:, :, 0, :].unsqueeze(3).broadcast_to([P, PH, TOPK, TOPK]),
                                             tv[:, :, 1, :].unsqueeze(2).broadcast_to([P, PH, TOPK, TOPK]), ALU.add))
                top_of(dve, link, cand, best, pos, PH)
                dve.sem_inc(sem("top_done"), 1)
                link(nc.vector.tensor_tensor(gate[:, s], best[:, :, :], best[:, :, 0:1].broadcast_to([P, PH, TOPK]), ALU.subtract))
                dve.sem_inc(sem("best_ready"), 1)
                posf = pos[:, :, :].rearrange("p h k -> p (h k)")
                nc.vector.tensor_single_scalar(half[:, 0, :], posf, 4, ALU.logical_shift_right)
                nc.vector.tensor_single_scalar(half[:, 1, :], posf, 15, ALU.bitwise_and)
                link(nc.vector.tensor_copy(top_f[:, :, :], top_i[:, :, :]))
                link(nc.vector.tensor_copy(half_f[:, :, :], half[:, :, :]))
                tf = top_f[:, :, :].rearrange("p (h q) k -> p h q k", q=2)
                for q in range(2):
                    e3 = eq.rearrange("p (n j) -> p n j", j=TOPK)
                    e4 = eq.rearrange("p (h k j) -> p h k j", h=PH, j=TOPK)
                    link(nc.vector.tensor_tensor(e3, half_f[:, q, :].unsqueeze(2).broadcast_to([P, PH * TOPK, TOPK]),
                                                 iota16[:, :].unsqueeze(1).broadcast_to([P, PH * TOPK, TOPK]), ALU.is_equal))
                    link(nc.vector.tensor_tensor(e4, e4, tf[:, :, q, :].unsqueeze(2).broadcast_to([P, PH, TOPK, TOPK]), ALU.mult))
                    link(nc.vector.tensor_reduce(part[:, q, :], e3, AX.X, ALU.add))
                nc.vector.scalar_tensor_tensor(ids[:, s, :], part[:, 0, :], float(P), part[:, 1, :], ALU.mult, ALU.add).then_inc(sem("ids_ready"), 1)
                dve.wait_ge(sem("gate_exp"), s + 1)
                link(nc.vector.tensor_reduce(gsum[:, :], gate[:, s], AX.X, ALU.add))
                link(nc.vector.reciprocal(gsum[:, :], gsum[:, :]))
                link(nc.vector.tensor_tensor(gate[:, s], gate[:, s], gsum[:, :].unsqueeze(2).broadcast_to([P, PH, TOPK]), ALU.mult))

            dve.wait_ge(sem("tok_kept"), 2)
            total = 2 * PH * TOPK
            for n in range(total + LAG):
                if n < total:
                    s, k = divmod(n, PH * TOPK)
                    dve.wait_ge(sem(f"u_row{n % NBUF}"), 16 * (n // NBUF + 1))
                    row = ubuf[:, n % NBUF, :]
                    i = nc.vector.tensor_tensor_reduce(row, row, h_tok[:, s, :], 1.0, 0.0, ALU.mult, ALU.add, dots[:, s, k // TOPK, k % TOPK:k % TOPK + 1])
                    i.then_inc(sem("u_used"), 1)
                    if n % TOPK == TOPK - 1:
                        dve.wait_ge(sem("u_used"), n + 1)
                        dve.sem_inc(sem("dots_ready"), 1)
                m = n - LAG
                if m >= 0:
                    s, k = divmod(m, PH * TOPK)
                    if m % TOPK == 0:
                        dve.wait_ge(sem("gelu_done"), m // TOPK + 1)
                        h = k // TOPK
                        link(nc.vector.tensor_tensor(wgt[:, s, h, :], wgt[:, s, h, :], gate[:, s, h, :], ALU.mult))
                    dve.wait_ge(sem(f"v_row{m % NBUF}"), 16 * (m // NBUF + 1))
                    if k:
                        dve.wait_ge(sem("v_used"), m)
                    nc.vector.scalar_tensor_tensor(acc[:, s, :], vbuf[:, m % NBUF, :], wgt[:, s, k // TOPK, k % TOPK:k % TOPK + 1], acc[:, s, :],
                                                   ALU.mult, ALU.add).then_inc(sem("v_used"), 1)
                    if k == PH * TOPK - 1:
                        dve.wait_ge(sem("v_used"), m + 1)
                        if s == 1:
                            dve.sem_inc(sem("acc_ready"), 2)
            dve.wait_ge(sem("g_fin_in"), 16)
            for s in range(2):
                dve.wait_ge(sem("last_std"), s + 1)
                link(nc.vector.reciprocal(mstat[:, 1, s:s + 1], mstat[:, 1, s:s + 1]))
                nc.vector.scalar_tensor_tensor(h_tok[:, s, :], acc[:, s, :], mstat[:, 1, s:s + 1], g_fin, ALU.mult, ALU.mult).then_inc(sem("out_ready"), 1)


def kernel(**inputs):
    import numpy as _np
    import concourse.bacc as _bacc
    from concourse.bass_utils import run_bass_kernel_spmd as _run

    nc = _bacc.Bacc("TRN2", target_bir_lowering=False, num_devices=1)
    arrays, aps = {}, {}
    dist = _np.arange(256)
    large = 16 + (_np.log(_np.maximum(dist, 1) / 16.0) / _np.log(128 / 16.0) * 16).astype(_np.int64)
    bucket = _np.where(dist < 16, dist, _np.minimum(large, N_BUCKETS - 1))
    onehot = _np.zeros((N_BUCKETS, 512), _np.float32)
    onehot[bucket, 255 - dist] = 1.0
    t = _np.arange(T)
    rcount = _np.stack([1.0 / _np.minimum(t + 1, w) for w in POOL_WINDOWS]).astype(_np.float32)
    for name, v in list(inputs.items()) + [("onehot", onehot), ("rcount", rcount)]:
        v = _np.ascontiguousarray(v)
        arrays[f"in_{name}"] = v
        aps[name] = nc.dram_tensor(f"in_{name}", v.shape, mybir.dt.from_np(v.dtype), kind="ExternalInput").ap()
    out = nc.dram_tensor("out_0", (1, T, D), F32, kind="ExternalOutput").ap()
    build_program(nc, aps, out)
    r = _run(nc, [arrays], core_ids=[0])
    return r.results[0]["out_0"]
```

```python
from contextlib import ExitStack

import concourse.bass as bass
from concourse import mybir

ALU = mybir.AluOpType
ACT = mybir.ActivationFunctionType
AX = mybir.AxisListType
F32 = mybir.dt.float32
U32 = mybir.dt.uint32

P = 128
T = 256
D = 1024
CT = D // P
DEPTH = 2
H = 4
DH = 256
FF = 4 * D
KM = 4
KC = 31
DVE_TILES = (7, 6)
NEG = -1e30
EPS = 1e-6

SLOT = 2048
RING = 4
ADA_CHUNKS = 24

POOL_CONV_STEPS = [KC * (CT - n) + KC - 1 for n in DVE_TILES]
FIRST_CHUNKS = 8
W_IN_ORDER = [0, 1, 2, 3] + list(range(8, 16)) + [4, 5, 6, 7]

B_ADA, G_PRE_MIX, G_PRE_MLP, G_POST_MIX, G_POST_MLP = 0, 48, 56, 64, 72
B_CONV_M, G_MH, B_DW, G_CN, B_CN = 80, 88, 96, 104, 112
W_DW, W_CONV = 120, 368
NPC = 400


NH, G, R, HD = 16, 4, 4, 64
N_BUCKETS = 32
CMP_LEN, CMP_STRIDE = 32, 16
NCMP = (T - CMP_LEN) // CMP_STRIDE + 1
POOL_WINDOWS = (2, 4, 8, 16)
XH = 4
KV0, GN0, QX0, GM0 = 1536, 3072, 3120, 3632
PH, TOPK = 8, 16
NBUF = 8
LAG = 20
G_MIX2, G_MEM2, G_FFN2, POOL_SC2 = 0, 8, 16, 24
UNITS = [(g, s) for g in range(G) for s in range(2)] + [("x", 0), ("x", 1)]
FILL = [["pool0", "pool1"], ["gm0", "gm1"], ["gm2", "gm3"], ["gm4", "gm5"], ["gm6", "gm7"], ["gm8", "gm9"],
        ["mix", "gm10", "gm11"], ["pool_out0", "pool_out1"], ["nsa_out0", "nsa_out1"], ["nsa_out2", "nsa_out3"]]


def weight_jobs():
    jobs = []
    for l in range(DEPTH):
        for j in W_IN_ORDER:
            jobs.append(("w_in", l, j))
        for j in range(8):
            jobs.append(("w_out", l, j))
        for j in range(16):
            jobs.append(("w_ff1", l, j))
        for j in range(16):
            jobs.append(("w_ff2", l, j))
    for j in ("kcmp", "vcmp", "q0", "q1", "q2", "q3", "ksel", "vsel", "kwin", "vwin", "qx0", "qx1",
              "memk0", "memk1", "memv0", "memv1"):
        jobs.append((j, 2, 0))
    for names in FILL:
        jobs += [(j, 2, 0) for j in names if j != "mix"]
    for name, n in (("x_out", 2), ("w_o", 4), ("peer_q", 8)):
        jobs += [(f"{name}{j}", 2, 0) for j in range(n)]
    return jobs


def second_weight(a, name):
    w_in = a["w_in_2"][0].rearrange("(k p) n -> p k n", p=P)
    parts = ("kcmp", "vcmp", "ksel", "vsel", "kwin", "vwin")
    if name in parts:
        c = KV0 + 256 * parts.index(name)
        return w_in[:, :, c:c + 256]
    base = name.rstrip("0123456789")
    j = int(name[len(base):])
    if base == "pool":
        return w_in[:, :, 256 * j:256 * j + 256]
    if base == "qx":
        return w_in[:, :, QX0 + 256 * j:QX0 + 256 * j + 256]
    if base == "gm":
        return w_in[:, :, GM0 + 256 * j:GM0 + 256 * j + 256]
    if base in ("memk", "memv"):
        c = 512 * (base == "memv") + 256 * j
        return a["w_mem_kv_2"][0].rearrange("(k p) n -> p k n", p=P)[:, :, c:c + 256]
    if base in ("pool_out", "x_out"):
        return a[f"w_{base}_2"][0].rearrange("(k p) n -> p k n", p=P)[:, :, 512 * j:512 * j + 512]
    w = {"nsa_out": "w_nsa_out_2", "w_o": "w_o_2", "peer_q": "w_peer_q_2"}[base]
    return a[w][0].rearrange("(k p) n -> p k n", p=P)[:, :, 256 * j:256 * j + 256]


def top_of(dve, link, values, top, where, groups):
    v = dve
    for c in range(groups):
        i = v.max(top[:, c, 0:8], values[:, c, :])
    link(i)
    for c in range(groups):
        i = v.max_index(where[:, c, 0:8], top[:, c, 0:8], values[:, c, :])
    link(i)
    for c in range(groups):
        i = v.match_replace(values[:, c, :], top[:, c, 0:8], values[:, c, :], -3.0e38)
    link(i)
    for c in range(groups):
        i = v.max(top[:, c, 8:16], values[:, c, :])
    link(i)
    for c in range(groups):
        i = v.max_index(where[:, c, 8:16], top[:, c, 8:16], values[:, c, :])
    link(i)


def build_program(nc, a, out):
    ctx = ExitStack()
    with ctx:
        def sb(name, shape, dt=F32):
            return ctx.enter_context(nc.sbuf_tensor(name, shape, dt))

        ring = sb("ring", [P, RING, SLOT])
        xT = sb("xT", [P, CT, T])
        hT = sb("hT", [P, CT, T])
        tmp = sb("tmp", [P, CT, T])
        region = sb("region", [P, 32768])
        at = 0

        def cut(n):
            nonlocal at
            at += n
            return region[:, at - n:at]

        U = cut(8192).rearrange("p (c t) -> p c t", t=T)
        xc = cut(2048).rearrange("p (c t) -> p c t", t=T)
        qT = cut(2048).rearrange("p (c t) -> p c t", t=T)
        kT = cut(2048).rearrange("p (c t) -> p c t", t=T)
        vtok = cut(2048).rearrange("p (s e) -> p s e", s=2)
        wqkv = cut(6144).rearrange("p (m c e) -> p m c e", m=3, c=2 * H)
        ada_in = cut(4096).rearrange("p (b k n) -> p b k n", b=2, k=CT)
        ada_acc = cut(6144)
        x_tok = tmp[:, :, :].rearrange("p c t -> p (c t)").rearrange("p (s d) -> p s d", s=2)
        def piece(lo, n):
            return region[:, lo:lo + n]

        gm = piece(0, 6144).rearrange("p (c t) -> p c t", t=T)
        poolT = piece(6144, 1024).rearrange("p (c t) -> p c t", t=T)
        qxT = piece(7168, 1024).rearrange("p (c t) -> p c t", t=T)
        wcmp = piece(8192, 4096).rearrange("p (m i e) -> p m i e", m=2, i=CMP_LEN)
        oT = piece(8192, 2048).rearrange("p (c t) -> p c t", t=T)
        merged = piece(10240, 2048).rearrange("p (c t) -> p c t", t=T)
        q2T = piece(12288, 2048).rearrange("p (c t) -> p c t", t=T)
        cmpT = piece(14336, 1024).rearrange("p (m c t) -> p m c t", m=2, t=T)
        oxT = piece(14336, 1024).rearrange("p (c t) -> p c t", t=T)
        kselT = piece(15360, 1024).rearrange("p (m c t) -> p m c t", m=2, t=T)
        onehot = piece(16384, 512)
        bias_w = piece(16896, 512)
        rel = piece(17408, NH)
        wqkv_free = piece(18432, 1024)
        v2 = piece(16384, 1024).rearrange("p (m s e) -> p m s e", m=2, s=2)
        kxT = piece(17408, 1024).rearrange("p (c t) -> p c t", t=T)
        vx = piece(18432, 1024).rearrange("p (s e) -> p s e", s=2)
        probs = [piece(19456, 2048).rearrange("p (m r t) -> p m r t", m=2, r=R),
                 piece(24576, 2048).rearrange("p (m r t) -> p m r t", m=2, r=R)]
        probsT = piece(21504, 2048).rearrange("p (m j r t) -> p m j r t", m=2, j=2, r=R)
        memtok = piece(22528, 2048).rearrange("p (s d) -> p s d", s=2)
        memT = piece(24576, 2048).rearrange("p (c t) -> p c t", t=T)
        bias = [piece(26624, 2048).rearrange("p (h t) -> p h t", h=NH), piece(28672, 4096).rearrange("p (h t) -> p h t", h=NH)]
        blk = tmp[:, :, :].rearrange("p c t -> p (c t)")[:, 0:1920].rearrange("p (m g c i) -> p m g c i", m=2, g=2, i=CMP_LEN)
        win = [tmp[:, 0:4, :], tmp[:, 4:8, :]]
        qpT = piece(0, 4096).rearrange("p (c t) -> p c t", t=T)
        subT = piece(4096, 2048).rearrange("p (c t) -> p c t", t=P)
        s_sb = piece(0, 4096).rearrange("p (b c t) -> p b c t", b=PH, t=P)
        acc = piece(8192, 2048).rearrange("p (s d) -> p s d", s=2)
        h_tok = piece(10240, 2048).rearrange("p (s d) -> p s d", s=2)
        ubuf = piece(12288, 8192).rearrange("p (b d) -> p b d", b=NBUF)
        vbuf = piece(20480, 8192).rearrange("p (b d) -> p b d", b=NBUF)
        eq = piece(28672, 2048)
        sub_raw = piece(30720, 2048).rearrange("p (c t) -> p c t", t=P)
        cand = tmp[:, 0:2, :]
        g_fin = ring[:, 0, 0:D]

        vT = tmp
        y = hT

        prow = qT.rearrange("p c t -> p (c t)")[:, 0:DEPTH * 4 * P].rearrange("p (l k q) -> p l k q", l=DEPTH, k=4)
        small = sb("small", [P, 3584])

        def small_piece(lo, n, rows=P):
            return small[0:rows, lo:lo + n]

        pc = sb("pc", [P, DEPTH, NPC])
        modc = sb("modc", [P, 48])
        mod_scale = sb("mod_scale", [P, 4, CT])
        c_act = sb("c_act", [P, CT])
        wg = sb("wg", [P, 6, H * 2 * H])
        bg = sb("bg", [2 * H, 1])
        ident = sb("ident", [P, P])
        ones = sb("ones", [P, P])
        eps_col = sb("eps_col", [P, 1])
        causal = sb("causal", [P, 2, T])
        wpg = small_piece(1504, 512).rearrange("p (g d) -> p g d", g=4)
        pick = small_piece(2048, 1024, CT).rearrange("p (h q) -> p h q", h=CT)
        rstd = sb("rstd", [P, T])
        gates = small_piece(3328, 256, 2 * H)
        vrow = small_piece(0, 256, CT)
        to_row = sb("to_row", [P, CT, CT])
        grow = wqkv.rearrange("p m c e -> p (m c e)")[0:H, 0:7 * T].rearrange("p (n t) -> p n t", t=T)
        fgr = grow[:, 0:3, :]
        lrow = grow[:, 3:7, :]
        ada_first = [region[:, 0:8192].rearrange("p (k n) -> p k n", k=CT), region[:, 14336:22528].rearrange("p (k n) -> p k n", k=CT)]
        zrow = small_piece(3072, 256, H)
        rows = small_piece(1536, 512, H).rearrange("p (s t) -> p s t", s=2)
        rcol = sb("rcol", [P, 2, H])
        wlog = small_piece(0, 512).rearrange("p (s t) -> p s t", s=2)
        sT = small_piece(512, 512).rearrange("p (s t) -> p s t", s=2)
        en_b = small_piece(1024, 256)
        den = small_piece(1280, 256)
        c_rows = kT.rearrange("p c t -> p (c t)")[0:CT, 512:640]
        prow2 = kT.rearrange("p c t -> p (c t)")[:, 0:P]
        pc2 = sb("pc2", [P, 28])
        pe_T = sb("pe_T", [P, 2, CMP_LEN])
        pe_raw = kT.rearrange("p c t -> p (c t)")[0:CMP_LEN, 256:512].rearrange("p (m h d) -> p m h d", m=2, h=2)
        wgn = small_piece(0, 384).rearrange("p (k n) -> p k n", k=CT)
        bgate = small_piece(448, 96).rearrange("p (s n) -> p s n", s=2)
        has = sb("has", [P, 1])
        cmpc = small_piece(384, 60).rearrange("p (m g c) -> p m g c", m=2, g=2)
        vc = small_piece(544, 256, NCMP).rearrange("p (g e) -> p g e", g=2)
        pcmp = small_piece(800, 120).rearrange("p (b r c) -> p b r c", b=2, r=R)
        pcmpT = small_piece(920, 512, NCMP).rearrange("p (r t) -> p r t", r=R)
        stat = small_piece(1432, 72).rearrange("p (b n m r) -> p b n m r", b=2, n=3, m=3)
        rc = piece(19456 + 2048 + 2048 + 0, 1024).rearrange("p (g t) -> p g t", g=4)
        mstat = sb("mstat", [P, 2, 2])
        top_v = small_piece(0, 64).rearrange("p (c k) -> p c k", k=TOPK)
        top_i = small_piece(256, 64).bitcast(U32).rearrange("p (c k) -> p c k", k=TOPK)
        top_f = small_piece(512, 64).rearrange("p (c k) -> p c k", k=TOPK)
        best = small_piece(768, 32).rearrange("p (c k) -> p c k", k=TOPK)
        pos = small_piece(896, 32).bitcast(U32).rearrange("p (c k) -> p c k", k=TOPK)
        half = small_piece(1024, 64).bitcast(U32).rearrange("p (c k) -> p c k", c=2)
        half_f = small_piece(1280, 64).rearrange("p (c k) -> p c k", c=2)
        part = small_piece(1536, 64).rearrange("p (c k) -> p c k", c=2)
        ids = small_piece(1792, 256).bitcast(U32)
        gate = small_piece(2048, 256).rearrange("p (u k) -> p u k", k=TOPK)
        gsum = sb("gsum", [P, 2 * PH])
        dots = small_piece(2304, 256).rearrange("p (u k) -> p u k", k=TOPK)
        wgt = small_piece(2560, 256).rearrange("p (u k) -> p u k", k=TOPK)
        iota16 = sb("iota16", [P, TOPK])
        bias_dram = nc.dram_tensor("bias_dram", (P, NH, 512), F32, kind="Internal").ap()

        pj = [ctx.enter_context(nc.psum_tensor(f"pj{i}", [P, 2, T], F32)) for i in range(2)]
        st = ctx.enter_context(nc.psum_tensor("st", [P, CT, T], F32))
        ms = [ctx.enter_context(nc.psum_tensor(f"ms{i}", [P, 2, T], F32)) for i in range(2)]

        sems = {}

        def sem(name):
            if name not in sems:
                sems[name] = ctx.enter_context(nc.semaphore(name))
            return sems[name]

        ring_full = [sem(f"ring_full{i}") for i in range(RING)]
        jobs = weight_jobs()
        job_at = {j: n for n, j in enumerate(jobs)}
        full_at = []
        for n, j in enumerate(jobs):
            before = full_at[n - RING] if n >= RING else 0
            full_at.append(before + (64 if j[0] in ("q0", "q1", "q2", "q3") else 16))

        MERGE_BANKS, GATE_BANK, banks = [], None, 64 * DEPTH
        for j in jobs[job_at[("kcmp", 2, 0)]:job_at[("vwin", 2, 0)] + 1]:
            banks += 1
        banks += 1
        GATE_BANK = banks
        banks += 6
        for (g, s), names in zip(UNITS, FILL):
            for name in names:
                if name[:8] == "pool_out":
                    MERGE_BANKS += [banks % 2, (banks + 1) % 2]
                    banks += 2
                elif name[:7] == "nsa_out":
                    MERGE_BANKS.append(banks % 2)
                    banks += 1
                else:
                    banks += 2 if name == "mix" else 1
            banks += 3 if g == "x" else 2 * (s + 1) + 2
        MERGE_BANKS += [(banks + k) % 2 for k in range(8)]

        block = ctx.enter_context(nc.Block())

        @block.sync
        def _(sp):
            def load_params(l):
                r = prow[:, l]
                for dst, n, src in (
                    (B_ADA, 48, a["b_ada"]), (G_PRE_MIX, 8, a["g_pre_mix"]), (G_PRE_MLP, 8, a["g_pre_mlp"]),
                    (G_POST_MIX, 8, a["g_post_mix"]), (G_POST_MLP, 8, a["g_post_mlp"]), (B_CONV_M, 8, a["b_conv_m"]),
                    (G_MH, 8, a["g_mh"]), (B_DW, 8, a["b_dw"]), (G_CN, 8, a["g_cn"]), (B_CN, 8, a["b_cn"]),
                ):
                    sp.dma_start(r[dst:dst + n, 0, :], src[l].rearrange("(r q) -> r q", q=P)).then_inc(sem("params_in"), 16)
                wdw = a["w_dw"][l].rearrange("k (c q) -> (k c) q", q=P)
                sp.dma_start(r[:, 1, :], wdw[0:P, :]).then_inc(sem("params_in"), 16)
                sp.dma_start(r[0:120, 2, :], wdw[P:248, :]).then_inc(sem("params_in"), 16)
                sp.dma_start(r[0:32, 3, :], a["w_conv_m"][l].rearrange("k (c q) -> (k c) q", q=P)).then_inc(sem("params_in"), 16)

            sp.dma_start(c_rows, a["c"][0].rearrange("(r q) -> r q", q=P)).then_inc(sem("c_in"), 16)
            sp.dma_start(x_tok, a["x"][0].rearrange("(s p) d -> p s d", p=P)).then_inc(sem("x_in"), 16)
            for l in range(DEPTH):
                load_params(l)
                if l == 0:
                    for j in range(4):
                        sp.dma_start(ada_first[j // 2][:, :, 512 * (j % 2):512 * (j % 2) + 512],
                                     a["w_ada"][0].rearrange("(k p) n -> p k n", p=P)[:, :, 512 * j:512 * j + 512]).then_inc(sem(f"ada_first{j}"), 16)

            def load_layer(l):
                sp.wait_ge(sem("mod_first"), 1)
                if l:
                    sp.wait_ge(sem("head_done"), H * l)
                for m, w in enumerate((a["w_q"], a["w_k"], a["w_v"])):
                    sp.dma_start(wqkv[:, m], w[l].rearrange("h (c p) e -> p (h c) e", p=P)).then_inc(sem("wqkv_in"), 16)
                sp.dma_start(wg[:, :, :], a["w_gates"][l].rearrange("(j p h) g -> p j (h g)", p=P, h=H)).then_inc(sem("wg_in"), 16)
                sp.dma_start(bg[:, :], a["b_gates"][l].rearrange("(g o) -> g o", o=1)).then_inc(sem("wg_in"), 16)

            for lo, n, src in ((G_MIX2, 8, a["g_mix_2"][0]), (G_MEM2, 8, a["g_mem_2"][0]), (G_FFN2, 8, a["g_ffn_2"][0]),
                               (POOL_SC2, 4, a["pool_scale_2"][0])):
                sp.dma_start(prow2[lo:lo + n, :], src.rearrange("(r q) -> r q", q=P)).then_inc(sem("params2_in"), 16)
            for m, src in enumerate((a["pe_k_2"][0], a["pe_v_2"][0])):
                for h in range(2):
                    sp.dma_start(pe_raw[:, m, h, :], src).then_inc(sem("params2_in"), 16)

            for n, (name, l, j) in enumerate(jobs):
                if n >= RING:
                    sp.wait_ge(sem("slot_used"), n - RING + 1)
                dst = ring[:, n % RING, :]
                if name in ("w_in", "w_ff1"):
                    src = a[name][l].rearrange("(k p) n -> p k n", p=P)[:, :, 256 * j:256 * j + 256]
                    dst = dst.rearrange("p (k n) -> p k n", n=256)
                elif name == "w_out":
                    src = a[name][l].rearrange("(k p) n -> p k n", p=P)[:, :, P * j:P * j + P]
                    dst = dst.rearrange("p (k n) -> p k n", n=P)
                elif name in ("q0", "q1", "q2", "q3"):
                    gp, rp = divmod(int(name[1]), 2)
                    w = a["w_in_2"][0].rearrange("(k p) n -> p k n", p=P)
                    dst = dst.rearrange("p (k r h d) -> p k r h d", r=2, h=2, d=HD)
                    for r in range(2):
                        for hf in range(2):
                            c = 512 + 256 * (2 * gp + hf) + P * rp + HD * r
                            sp.dma_start(dst[:, :, r, hf, :], w[:, :, c:c + HD]).then_inc(ring_full[n % RING], 16)
                    continue
                elif l == 2:
                    src = second_weight(a, name)
                    dst = dst.rearrange("p (k n) -> p k n", n=src.shape[2])
                else:
                    src = a[name][l].rearrange("(k p) n -> p k n", p=P)[:, 16 * (j % 2):16 * (j % 2) + 16, P * (j // 2):P * (j // 2) + P]
                    dst = dst.rearrange("p (k n) -> p k n", n=P)
                sp.dma_start(dst, src).then_inc(ring_full[n % RING], 16)
                if name == "w_in" and j == (3 if l == 0 else 11):
                    load_layer(l)

            sp.wait_ge(sem("slot_used"), len(jobs))
            sp.dma_start(g_fin, a["g_final_2"].partition_broadcast(P)).then_inc(sem("g_fin_in"), 16)
            for s in range(2):
                sp.wait_ge(sem("out_ready"), s + 1)
                sp.dma_start(out[0, P * s:P * s + P, :], h_tok[:, s, :]).then_inc(sem("out_done"), 16)
            sp.wait_ge(sem("out_done"), 32)

        @block.gpsimd
        def _(pool):
            nc.gpsimd.memset(ident[:, :], 0.0).then_inc(sem("pool_c"), 1)
            nc.gpsimd.memset(causal[:, :, :], 0.0).then_inc(sem("pool_c"), 1)
            nc.gpsimd.memset(pick[:, :, :], 0.0).then_inc(sem("pool_c"), 1)
            nc.gpsimd.memset(to_row[:, :, :], 0.0)
            nc.gpsimd.memset(ones[:, :], 1.0)
            nc.gpsimd.memset(eps_col[:, :], EPS)
            nc.gpsimd.memset(zrow[:, :], 0.0).then_inc(sem("pool_c"), 1)
            pool.wait_ge(sem("pool_c"), 4)
            nc.gpsimd.affine_select(out=ident[:, :], in_=ident[:, :], compare_op=ALU.not_equal, fill=1.0, base=0,
                                    pattern=[[-1, P]], channel_multiplier=1)
            nc.gpsimd.affine_select(out=causal[:, :, :], in_=causal[:, :, :], compare_op=ALU.is_ge, fill=NEG, base=0,
                                    pattern=[[-P, 2], [1, T]], channel_multiplier=-1)
            nc.gpsimd.affine_select(out=to_row[:, :, :], in_=to_row[:, :, :], compare_op=ALU.not_equal, fill=1.0, base=0,
                                    pattern=[[1, CT], [-1, CT]], channel_multiplier=0)
            nc.gpsimd.affine_select(out=pick[:, :, :], in_=pick[:, :, :], compare_op=ALU.not_equal, fill=1.0, base=0,
                                    pattern=[[-1, CT], [0, P]], channel_multiplier=1).then_inc(sem("consts"), 1)

            nc.gpsimd.memset(has[:, :], 1.0).then_inc(sem("pool_c"), 1)
            pool.wait_ge(sem("pool_c"), 5)
            nc.gpsimd.affine_select(out=has[:, :], in_=has[:, :], compare_op=ALU.is_ge, fill=0.0, base=-(CMP_LEN - 1),
                                    pattern=[[0, 1]], channel_multiplier=1)
            nc.gpsimd.iota(iota16[:, :], pattern=[[1, TOPK]], base=0, channel_multiplier=0,
                           allow_small_or_imprecise_dtypes=True).then_inc(sem("consts2"), 1)

            def load(n):
                l, j = divmod(n, ADA_CHUNKS)
                src = a["w_ada"][l].rearrange("(k p) n -> p k n", p=P)[:, :, 256 * j:256 * j + 256]
                pool.dma_start(ada_in[:, n % 2], src).then_inc(sem(f"ada_full{n % 2}"), 16)

            conv_steps = 0

            def conv_rest(l, products):
                nonlocal conv_steps
                pool.wait_ge(sem("glu_ready"), l + 1)
                first = DVE_TILES[l]
                src, dst = U[:, 24 + first:32], U[:, 16 + first:24]
                for back in range(KC):
                    for i in range(CT - first):
                        at_ = W_DW + (KC - 1 - back) * CT + first + i
                        wc, bc = pc[:, l, at_:at_ + 1], pc[:, l, B_DW + first + i:B_DW + first + i + 1]
                        if back == 0:
                            nc.gpsimd.tensor_scalar(dst[:, i, :], src[:, i, :], wc, bc, ALU.mult, ALU.add).then_inc(sem("pool_conv_step"), 1)
                        else:
                            nc.gpsimd.tensor_scalar(products[:, i, 0:T - back], src[:, i, 0:T - back], wc, None, ALU.mult).then_inc(sem("pool_conv_step"), 1)
                        conv_steps += 1
                    pool.wait_ge(sem("pool_conv_step"), conv_steps)
                    if back:
                        nc.gpsimd.tensor_tensor(dst[:, :, back:T], dst[:, :, back:T], products[:, 0:CT - first, 0:T - back], ALU.add).then_inc(sem("pool_conv_step"), 1)
                        conv_steps += 1
                        pool.wait_ge(sem("pool_conv_step"), conv_steps)

            total = DEPTH * ADA_CHUNKS
            load(FIRST_CHUNKS)
            pool.wait_ge(sem("c_ready"), 1)
            step = 0
            for n in range(FIRST_CHUNKS, total):
                l, j = divmod(n, ADA_CHUNKS)
                if l and j == 0:
                    conv_rest(l - 1, ada_in[:, (n + 1) % 2])
                if n + 1 < total:
                    load(n + 1)
                pool.wait_ge(sem(f"ada_full{n % 2}"), 16 * ((n - FIRST_CHUNKS) // 2 + 1))
                if l and j == 0:
                    pool.wait_ge(sem("mod_summed"), l)
                acc = ada_acc[:, 256 * j:256 * j + 256]
                w = ada_in[:, n % 2]
                c_wide = c_act[:, :].unsqueeze(2).broadcast_to([P, CT, 256])
                for dst, x0, x1, op in ((w, w, c_wide, ALU.mult), (w[:, 0:4], w[:, 0:4], w[:, 4:8], ALU.add),
                                        (w[:, 0:2], w[:, 0:2], w[:, 2:4], ALU.add), (acc, w[:, 0], w[:, 1], ALU.add)):
                    nc.gpsimd.tensor_tensor(dst, x0, x1, op).then_inc(sem("ada_step"), 1)
                    step += 1
                    pool.wait_ge(sem("ada_step"), step)

            conv_rest(DEPTH - 1, ada_in[:, 0])
            pool.wait_ge(sem("mod_summed"), DEPTH)
            pool.dma_start(memtok, a["mem_2"][0].rearrange("(s p) d -> p s d", p=P)).then_inc(sem("mem_in"), 16)
            pool.wait_ge(sem("head_done"), H * DEPTH)
            pool.dma_start(onehot[0:N_BUCKETS, :], a["onehot"]).then_inc(sem("bias_in"), 16)
            pool.dma_start(rel[0:N_BUCKETS, :], a["rel_bias_2"]).then_inc(sem("bias_in"), 16)
            pool.wait_ge(sem("mix_ready"), DEPTH * CT)
            pool.dma_start(wgn[:, :, :], a["w_in_2"][0].rearrange("(k p) n -> p k n", p=P)[:, :, GN0:GN0 + 48]).then_inc(sem("wgn_in"), 16)
            for m, w in enumerate((a["w_cmp_k_2"], a["w_cmp_v_2"])):
                for h in range(2):
                    pool.dma_start(wcmp[HD * h:HD * h + HD, m], w[0].rearrange("(i d) e -> d i e", d=HD)).then_inc(sem("wcmp_in"), 16)
            pool.wait_ge(sem("bias_masked"), 1)
            pool.wait_ge(sem("bias_copied"), 1)
            pool.dma_start(bias_dram.rearrange("p h u -> h p u"), bias_w[0:NH, :].unsqueeze(1).broadcast_to([NH, P, 512])).then_inc(sem("bias_out"), 16)
            pool.wait_ge(sem("bias_out"), 16)
            for s in range(2):
                n = P * (s + 1)
                src = bass.AP(tensor=bias_dram.tensor, offset=255 - P * s, ap=[[NH * 512 - 1, P], [512, NH], [1, n]])
                pool.dma_start(bias[s], src).then_inc(sem("toeplitz_in"), 16)
            pool.wait_ge(sem("memT_ready"), 1)
            pool.dma_start(rc, a["rcount"].partition_broadcast(P)).then_inc(sem("rcount_in"), 16)
            pool.wait_ge(sem("x_ready"), 2 * DEPTH * CT)
            pool.dma_start(wpg[:, :, :], a["w_pool_grp_2"][0].rearrange("g c d -> c g d")).then_inc(sem("wpg_in"), 16)
            pool.wait_ge(sem("attention_done"), 1)
            pool.dma_start(sub_raw, a["peer_sub_keys_2"][0].rearrange("h p k c -> k (h p) c")).then_inc(sem("sub_in"), 16)

            total = 2 * PH * TOPK
            for n in range(total + LAG):
                for table, buf, name, m in ((a["peer_u_2"], ubuf, "u", n), (a["peer_v_2"], vbuf, "v", n - LAG)):
                    if not 0 <= m < total:
                        continue
                    if name == "u" and m % TOPK == 0:
                        pool.wait_ge(sem("ids_ready"), m // TOPK + 1)
                    if m >= NBUF:
                        pool.wait_ge(sem(f"{name}_used"), m - NBUF + 1)
                    nc.gpsimd.indirect_dma_start(
                        out=buf[:, m % NBUF, :], out_offset=None, in_=table[0],
                        in_offset=bass.IndirectOffsetOnAxis(ap=ids[:, m:m + 1], axis=0)).then_inc(sem(f"{name}_row{m % NBUF}"), 16)

        @block.tensor
        def _(pe):
            bank = 0
            emptied = {"proj_drained": 0, "merge_drained": 0}
            emptied_at = []

            def take_bank(by="proj_drained", other=False):
                nonlocal bank
                if bank >= 2 and not other:
                    pe.wait_ge(sem(emptied_at[bank - 2][0]), emptied_at[bank - 2][1])
                emptied[by] += 1
                emptied_at.append((by, emptied[by]))
                bank += 1
                return pj[(bank - 1) % 2]

            def ring_slot(job):
                n = job_at[job]
                pe.wait_ge(ring_full[n % RING], full_at[n])
                return ring[:, n % RING, :]

            norms = 0

            def norm_sum():
                nonlocal norms
                for c in range(CT):
                    pe.wait_ge(sem("squares"), CT * norms + c + 1)
                    i = nc.tensor.matmul(ms[0][:, 0, :], ones[:, :], tmp[:, c, :], start=(c == 0), stop=(c == CT - 1))
                i.then_inc(sem("norm_summed"), 1)
                norms += 1

            pe.wait_ge(sem("consts"), 1)
            pe.wait_ge(sem("c_in"), 16)
            nc.tensor.transpose(ms[0][:, 0, 0:CT], c_rows, ident[0:CT, 0:CT]).then_inc(sem("c_turned"), 1)
            pe.wait_ge(sem("x_in"), 16)
            for c in range(CT):
                for s in range(2):
                    i = nc.tensor.transpose(st[:, c, P * s:P * s + P], x_tok[:, s, P * c:P * c + P], ident[:, :])
            i.then_inc(sem("x_turned"), 1)
            norm_sum()
            pe.wait_ge(sem("params_in"), 16 * 13 * DEPTH)
            pe.wait_ge(sem("std_ready"), 1)
            for l in range(DEPTH):
                b = ms[l][:, :, :].rearrange("p s t -> p (s t)")
                for k, n, c0 in ((0, W_DW, 0), (1, P, W_DW), (2, 120, W_DW + P), (3, 32, W_CONV)):
                    i = nc.tensor.transpose(b[:, c0:c0 + n], prow[0:n, l, k, :], ident[0:n, 0:n])
                i.then_inc(sem("params_turned"), 1)

            pe.wait_ge(sem("params2_in"), 16 * 8)
            pe.wait_ge(sem("params_kept"), 1)
            nc.tensor.transpose(ms[0][:, 0, 0:28], prow2[0:28, :], ident[0:28, 0:28])
            for m in range(2):
                i = nc.tensor.transpose(ms[0][:, 1, CMP_LEN * m:CMP_LEN * m + CMP_LEN], pe_raw[:, m].rearrange("p h d -> p (h d)"),
                                        ident[0:CMP_LEN, 0:CMP_LEN])
            i.then_inc(sem("params2_turned"), 1)
            pe.wait_ge(sem("params_kept"), 2)
            for m in range(2 * FIRST_CHUNKS):
                if m % 4 == 0:
                    pe.wait_ge(sem("first_partial"), m // 4 + 1)
                i = nc.tensor.matmul(ms[1][:, 0, m:m + 1], ada_acc[:, P * m:P * m + P], ones[:, 0:1], start=True, stop=True)
            i.then_inc(sem("mod_first"), 1)
            def wide_tile(job, m, b, first_wait=None):
                w = ring_slot(job).rearrange("p (k n) -> p k n", n=256)
                for k in range(CT):
                    if first_wait is not None and m == 0:
                        pe.wait_ge(sem("h_ready"), first_wait + k + 1)
                    i = nc.tensor.matmul(b[:, m, :], w[:, k, P * m:P * m + P], hT[:, k, :], start=(k == 0), stop=(k == CT - 1))
                if m == 1:
                    i.then_inc(sem("slot_used"), 1)

            def wide(name, l, js, first_wait=None):
                for j in js:
                    b = take_bank()
                    for m in range(2):
                        wide_tile((name, l, j), m, b, first_wait if j == js[0] else None)

            def sum_modulation(l, first, last, signal):
                pe.wait_ge(sem("ada_step"), 4 * (ADA_CHUNKS * l + last // 2 - FIRST_CHUNKS))
                for m in range(first, last):
                    i = nc.tensor.matmul(ms[1][:, 0, m:m + 1], ada_acc[:, P * m:P * m + P], ones[:, 0:1], start=True, stop=True)
                i.then_inc(sem(signal), 1)

            for l in range(DEPTH):
                if l:
                    sum_modulation(l, 0, 2 * FIRST_CHUNKS, "mod_first")
                    norm_sum()
                wide("w_in", l, W_IN_ORDER[:12], 16 * l)

                pe.wait_ge(sem("wqkv_in"), 48 * (l + 1))
                pe.wait_ge(sem("proj_drained"), bank)
                for m in (2, 0, 1):
                    if m == 0:
                        pe.wait_ge(sem("xc_ready"), l + 1)
                    for h in range(H):
                        b = take_bank()
                        for e in range(2):
                            for d in range(2):
                                src = U if m == 2 else xc
                                i = nc.tensor.matmul(b[:, e, :], wqkv[:, m, 2 * h + d, P * e:P * e + P], src[:, 2 * h + d, :],
                                                     start=(d == 0), stop=(d == 1))
                        i.then_inc(sem("qkv_made"), 1)
                    if m == 2:
                        for s in range(2):
                            for hp in range(2):
                                b = take_bank()
                                for h in range(2):
                                    for d in range(2):
                                        c = 2 * (2 * hp + h) + d
                                        i = nc.tensor.matmul(b[:, h, :], U[:, c, P * s:P * s + P], wqkv[:, 2, c, :],
                                                             start=(d == 0), stop=(d == 1))
                                i.then_inc(sem("qkv_made"), 1)

                pe.wait_ge(sem("wg_in"), 32 * (l + 1))
                pe.wait_ge(sem("proj_drained"), bank)
                n = 0
                for m, src in enumerate((qT, kT, vT)):
                    for e in range(2):
                        for h in range(H):
                            i = nc.tensor.matmul(ms[0][0:2 * H, 0, :], wg[:, 2 * m + e, 8 * h:8 * h + 8], src[:, 2 * h + e, :],
                                                 start=(n == 0), stop=(n == 23))
                            n += 1
                i.then_inc(sem("gates_made"), 1)
                pe.wait_ge(sem("gates_kept"), l + 1)
                nc.tensor.matmul(ms[0][0:H, 1, :], ident[0:2 * H, H:2 * H], gates[:, :], start=True, stop=True).then_inc(sem("fg_moved"), 1)

                wide("w_in", l, [4])
                sum_modulation(l, 2 * FIRST_CHUNKS, 48, "mod_summed")
                pe.wait_ge(sem("rows_ready"), l + 1)
                for s in range(2):
                    i = nc.tensor.transpose(ms[0][:, 0, H * s:H * s + H], lrow[:, 2, P * s:P * s + P], ident[0:H, 0:H])
                i.then_inc(sem("r_turned"), 1)

                for h in range(H):
                    hn = l * H + h
                    if h == 0:
                        pe.wait_ge(sem("rcol_kept"), l + 1)
                        pe.wait_ge(sem("mod_kept"), l + 1)
                    else:
                        pe.wait_ge(sem("head_done"), hn)
                    nc.tensor.matmul(ms[0][:, :, :].rearrange("p a t -> p (a t)"), pick[0:H, h, :],
                                     rows[:, :, :].rearrange("p a t -> p (a t)"), start=True, stop=True).then_inc(sem("rows_spread"), 1)
                    for s in range(2):
                        t0 = P * s
                        for d in range(2):
                            i = nc.tensor.matmul(ms[1][:, s, t0:T], kT[:, 2 * h + d, P * s:P * s + P], qT[:, 2 * h + d, t0:T],
                                                 start=(d == 0), stop=(d == 1))
                    i.then_inc(sem("scores_made"), 1)
                    z = ("w_in", l, 5 + h)
                    if h < 3:
                        b = take_bank()
                        wide_tile(z, 0, b)
                    pe.wait_ge(sem("s_ready"), hn + 1)
                    for s in range(2):
                        i = nc.tensor.matmul(st[:, 4, P * s:T], ones[:, :], sT[:, s, P * s:T], start=(s == 0), stop=(s == 1))
                    for e in range(2):
                        for s in range(2):
                            i = nc.tensor.matmul(st[:, 6 + e, P * s:T], vtok[:, s, DH * h + P * e:DH * h + P * e + P], sT[:, s, P * s:T],
                                                 start=(s == 0), stop=(s == 1))
                    i.then_inc(sem("num_made"), 1)
                    if h < 3:
                        wide_tile(z, 1, b)

                for h in range(H):
                    pe.wait_ge(sem("head_done"), l * H + h + 1)
                    for e in range(2):
                        i = nc.tensor.matmul(st[:, h, :], ones[:, :], tmp[:, 2 * h + e, :], start=(e == 0), stop=(e == 1))
                    i.then_inc(sem("hm_summed"), 1)
                for c in range(CT):
                    if c % 2 == 0:
                        pe.wait_ge(sem("hm_squared"), H * l + c // 2 + 1)
                    i = nc.tensor.matmul(ms[0][0:CT, 0, :], to_row[:, c // 2, :], hT[:, c, :], start=(c == 0), stop=(c == CT - 1))
                i.then_inc(sem("var_made"), 1)
                pe.wait_ge(sem("var_inverse"), 2 * l + 1)
                for h in range(H):
                    i = nc.tensor.matmul(st[:, h, :], pick[:, h, :], vrow, start=True, stop=True)
                i.then_inc(sem("hm_spread"), 1)
                def out_half(j, b, half):
                    w = ring_slot(("w_out", l, j)).rearrange("p (k n) -> p k n", n=P)
                    for k in range(8 * half, 8 * half + 8):
                        if j == 0 and half:
                            pe.wait_ge(sem("mix_ready"), CT * l + k - 7)
                        elif j == 0 and k % 2 == 0:
                            pe.wait_ge(sem("mlstm_ready"), 4 * l + k // 2 + 1)
                        i = nc.tensor.matmul(b[:, 0, :], w[:, k, :], U[:, 8 + k, :], start=(k == 0), stop=(k == 15))
                    if half:
                        i.then_inc(sem("slot_used"), 1)

                begun = [take_bank(), take_bank()]
                for j in range(2):
                    out_half(j, begun[j], 0)
                pe.wait_ge(sem("conv_ready"), l + 1)
                pe.wait_ge(sem("pool_conv_step"), sum(POOL_CONV_STEPS[:l + 1]))
                for c in range(CT):
                    i = nc.tensor.matmul(st[:, c, :], ones[:, :], U[:, 16 + c, :], start=True, stop=True)
                    if c % 2:
                        i.then_inc(sem("gn_summed"), 1)
                for c in range(CT):
                    if c % 2 == 0:
                        pe.wait_ge(sem("gn_squared"), 4 * l + c // 2 + 1)
                    i = nc.tensor.matmul(ms[0][0:CT, 0, :], to_row[:, c, :], tmp[:, c, :], start=(c == 0), stop=(c == CT - 1))
                i.then_inc(sem("var_made"), 1)
                take_bank(other=True)
                begun.append(ms[1])
                out_half(2, begun[2], 0)
                pe.wait_ge(sem("var_inverse"), 2 * l + 2)
                for c in range(CT):
                    i = nc.tensor.matmul(st[:, c, :], pick[:, c, :], vrow, start=True, stop=True)
                    if c % 2:
                        i.then_inc(sem("gn_spread"), 1)

                for j in range(8):
                    if j < len(begun):
                        b = begun[j]
                    else:
                        b = take_bank()
                        out_half(j, b, 0)
                    out_half(j, b, 1)
                norm_sum()
                norm_sum()
                wide("w_ff1", l, list(range(16)), 16 * l + 8)
                pe.wait_ge(sem("proj_drained"), bank)
                for j in range(16):
                    w = ring_slot(("w_ff2", l, j)).rearrange("p (k n) -> p k n", n=P)
                    if j % 2 == 0:
                        b = take_bank()
                    for k in range(16):
                        kk = 16 * (j % 2) + k
                        i = nc.tensor.matmul(b[:, 0, :], w[:, k, :], U[:, kk, :], start=(kk == 0), stop=(kk == 31))
                    i.then_inc(sem("slot_used"), 1)
                if l == DEPTH - 1:
                    pe.wait_ge(sem("mem_scaled"), 1)
                    for c in range(CT):
                        for s in range(2):
                            i = nc.tensor.transpose(st[:, c, P * s:P * s + P], memtok[:, s, P * c:P * c + P], ident[:, :])
                    i.then_inc(sem("mem_turned"), 1)
                    pe.wait_ge(sem("bias_in"), 32)
                    nc.tensor.matmul(ms[1][0:NH, :, :].rearrange("p a t -> p (a t)"), rel[0:N_BUCKETS, :], onehot[0:N_BUCKETS, :],
                                     start=True, stop=True).then_inc(sem("bias_made"), 1)
                norm_sum()

            def second_slot(name):
                return ring_slot((name, 2, 0))

            def columns(name, src, h_first=False, by="proj_drained", k_tiles=CT, tiles=(0, 1), last=True):
                w = second_slot(name).rearrange("p (k n) -> p k n", k=k_tiles)
                b = take_bank(by)
                for n, m in enumerate(tiles):
                    for k in range(k_tiles):
                        if h_first and n == 0:
                            pe.wait_ge(sem("h_ready"), 4 * CT + k + 1)
                        i = nc.tensor.matmul(b[:, n, :], w[:, k, P * m:P * m + P], src[:, k, :], start=(k == 0), stop=(k == k_tiles - 1))
                if last:
                    i.then_inc(sem("slot_used"), 1)
                else:
                    i.then_inc(sem("half_slot"), 1)

            def tokens(name, src):
                w = second_slot(name).rearrange("p (k n) -> p k n", k=CT)
                b = take_bank()
                for n in range(2):
                    for k in range(CT):
                        i = nc.tensor.matmul(b[:, n, :], src[:, k, P * n:P * n + P], w[:, k, :], start=(k == 0), stop=(k == CT - 1))
                i.then_inc(sem("slot_used"), 1)

            norm_sum()
            columns("kcmp", hT, h_first=True)
            columns("vcmp", hT)
            for j in range(4):
                w = second_slot(f"q{j}").rearrange("p (k r n) -> p k r n", k=CT, r=2)
                b = take_bank()
                for r in range(2):
                    for k in range(CT):
                        i = nc.tensor.matmul(b[:, r, :], w[:, k, r, :], hT[:, k, :], start=(k == 0), stop=(k == CT - 1))
                i.then_inc(sem("slot_used"), 1)
            columns("ksel", hT)
            tokens("vsel", hT)
            columns("kwin", hT)
            tokens("vwin", hT)
            pe.wait_ge(sem("wgn_in"), 16)
            b = take_bank()
            for s in range(2):
                for k in range(CT):
                    i = nc.tensor.matmul(b[:, 0, 48 * s:48 * s + 48], hT[:, k, P * s:P * s + P], wgn[:, k, :], start=(k == 0), stop=(k == CT - 1))
            i.then_inc(sem("bgate_made"), 1)
            pe.wait_ge(sem("wcmp_in"), 64)
            pe.wait_ge(sem("blk_ready"), 1)
            for m in range(2):
                for h in range(2):
                    lo = HD * h
                    for i_ in range(CMP_LEN):
                        i = nc.tensor.matmul(ms[1][lo:lo + HD, 0, 32 * m:32 * m + 2 * NCMP].rearrange("p (g c) -> p g c", g=2),
                                             wcmp[lo:lo + HD, m, i_, :], blk[lo:lo + HD, m, :, :, i_],
                                             start=(i_ == 0), stop=(i_ == CMP_LEN - 1))
            i.then_inc(sem("cmp_made"), 1)
            columns("qx0", hT)
            columns("qx1", hT)
            pe.wait_ge(sem("cmp_kept"), 1)
            for g in range(2):
                i = nc.tensor.transpose(ms[1][0:NCMP, 1, P * g:P * g + P], cmpc[:, 1, g, :], ident[:, :])
            i.then_inc(sem("vc_turned"), 1)
            pe.wait_ge(sem("memT_ready"), 1)
            columns("memk0", memT)
            columns("memk1", memT)
            tokens("memv0", memT)

            def scores(u):
                g, s = UNITS[u]
                if u:
                    pe.wait_ge(sem("scores_kept"), u)
                if g == "x":
                    for h in range(XH):
                        i = nc.tensor.matmul(st[:, h, :], qxT[:, h, P * s:P * s + P], kxT[:, h, :], start=True, stop=True)
                    i.then_inc(sem("scores2_made"), 1)
                    return
                gp, lo, n = g // 2, HD * (g % 2), P * (s + 1)
                for m in range(2):
                    for r in range(R):
                        nc.tensor.matmul(st[:, R * m + r, 0:n], q2T[lo:lo + HD, R * gp + r, P * s:P * s + P], kselT[lo:lo + HD, m, gp, 0:n],
                                         start=True, stop=True)
                for r in range(R):
                    i = nc.tensor.matmul(ms[0][:, 0, 16 * r:16 * r + NCMP], q2T[lo:lo + HD, R * gp + r, P * s:P * s + P],
                                         cmpc[lo:lo + HD, 0, gp, :], start=True, stop=True)
                i.then_inc(sem("scores2_made"), 1)

            def turn(u):
                g, s = UNITS[u]
                pb = probs[u % 2]
                pe.wait_ge(sem("probs_ready"), u + 1)
                for m in range(1 if g == "x" else 2):
                    for j in range(2 if g == "x" else s + 1):
                        b = take_bank().rearrange("p a t -> p (a t)")
                        for r in range(R):
                            i = nc.tensor.transpose(b[:, P * r:P * r + P], pb[:, m, r, P * j:P * j + P], ident[:, :])
                        i.then_inc(sem("turned"), 1)
                if g != "x":
                    nb = NCMP if s else NCMP // 2
                    b = take_bank().rearrange("p a t -> p (a t)")
                    for r in range(R):
                        i = nc.tensor.transpose(b[0:nb, P * r:P * r + P], pcmp[:, u % 2, r, 0:nb], ident[:, :])
                    i.then_inc(sem("turned"), 1)

            def values(u):
                g, s = UNITS[u]
                b = take_bank()
                pe.wait_ge(sem("turned_kept"), u + 1)
                if g == "x":
                    o = b.rearrange("p a t -> p (a t)")
                    for h in range(XH):
                        for j in range(2):
                            i = nc.tensor.matmul(o[:, P * h:P * h + P], vx[:, j, P * h:P * h + P], probsT[:, 0, j, h, :], start=(j == 0), stop=(j == 1))
                    i.then_inc(sem("o_made"), 1)
                    return
                nb = NCMP if s else NCMP // 2
                gp, lo = g // 2, HD * (g % 2)
                for hf in range(2):
                    o = b[HD * hf:HD * hf + HD, 0, :].rearrange("p (a t) -> p a t", a=2)
                    for m in range(2):
                        for j in range(s + 1):
                            nc.tensor.matmul(o, v2[:, m, j, HD * g:HD * g + HD], probsT[:, m, j, hf:R:2, :], start=(m == 0 and j == 0), stop=False)
                    i = nc.tensor.matmul(o, vc[0:nb, gp, lo:lo + HD], pcmpT[0:nb, hf:R:2, :], start=False, stop=True)
                i.then_inc(sem("o_made"), 1)

            pe.wait_ge(sem("vc_kept"), 1)
            scores(0)
            tokens("memv1", memT)
            pe.wait_ge(sem("vx_kept"), 1)
            for u in range(len(UNITS)):
                if u + 1 < len(UNITS):
                    scores(u + 1)
                for name in FILL[u]:
                    if name == "mix":
                        pe.wait_ge(sem("wpg_in"), 16)
                        pe.wait_ge(sem("pooled"), 1)
                        for m in range(2):
                            b = take_bank()
                            for k in range(2):
                                i = nc.tensor.matmul(b[:, k, :], wpg[:, 2 * m + k, :], win[0][:, 2 * m + k, :], start=True, stop=True)
                            i.then_inc(sem("mixed"), 1)
                    elif name[:8] == "pool_out":
                        pe.wait_ge(sem("mix_kept"), 1)
                        columns(name, poolT, by="merge_drained", k_tiles=4, last=False)
                        columns(name, poolT, by="merge_drained", k_tiles=4, tiles=(2, 3))
                    elif name[:7] == "nsa_out":
                        pe.wait_ge(sem("o_kept"), 2 * G)
                        columns(name, oT, by="merge_drained")
                    else:
                        columns(name, hT)
                turn(u)
                values(u)
            pe.wait_ge(sem("o_kept"), len(UNITS))
            for j in range(2):
                columns(f"x_out{j}", oxT, by="merge_drained", k_tiles=4, last=False)
                columns(f"x_out{j}", oxT, by="merge_drained", k_tiles=4, tiles=(2, 3))
            pe.wait_ge(sem("merge_drained"), 12)
            for j in range(4):
                columns(f"w_o{j}", merged, by="merge_drained")
            pe.wait_ge(sem("sub_in"), 16)
            for c in range(2 * PH):
                i = nc.tensor.transpose(st[:, c // 2, P * (c % 2):P * (c % 2) + P], sub_raw[:, c, :], ident[:, :])
            i.then_inc(sem("sub_turned"), 1)
            norm_sum()
            pe.wait_ge(sem("sub_kept"), 1)

            def sub_scores(h):
                pe.wait_ge(sem("qp_kept"), h + 1)
                if h >= 2:
                    pe.wait_ge(sem("sub_scores_kept"), h - 1)
                else:
                    pe.wait_ge(sem("std_ready"), norms)
                for s in range(2):
                    for q in range(2):
                        i = nc.tensor.matmul(ms[h % 2][:, s, P * q:P * q + P], qpT[:, 2 * h + q, P * s:P * s + P], subT[:, 2 * h + q, :],
                                             start=True, stop=True)
                i.then_inc(sem("sub_scores"), 1)

            def to_tokens(n, src):
                if n:
                    pe.wait_ge(sem("tok_kept"), n)
                for s in range(2):
                    for c in range(CT):
                        i = nc.tensor.transpose(st[:, 4 * s + c // 2, P * (c % 2):P * (c % 2) + P], src[:, c, P * s:P * s + P], ident[:, :])
                i.then_inc(sem("tok_turned"), 1)

            for j in range(PH):
                w = second_slot(f"peer_q{j}").rearrange("p (k n) -> p k n", k=CT)
                b = take_bank()
                for m in range(2):
                    for k in range(CT):
                        if j == 0 and m == 0:
                            pe.wait_ge(sem("h_ready"), 5 * CT + k + 1)
                        i = nc.tensor.matmul(b[:, m, :], w[:, k, P * m:P * m + P], hT[:, k, :], start=(k == 0), stop=(k == CT - 1))
                i.then_inc(sem("slot_used"), 1)
                sub_scores(j)
                if j < 2:
                    to_tokens(j, (hT, xT)[j])

        @block.scalar
        def _(act):
            steps = 0

            def link(i):
                nonlocal steps
                steps += 1
                i.then_inc(sem("act_step"), 1)
                act.wait_ge(sem("act_step"), steps)

            norms = 0
            bank = 0
            qkv = 0

            def norm(src, x_at=None):
                nonlocal norms
                if src is xT:
                    for c in range(CT):
                        if norms and x_at is not None:
                            act.wait_ge(sem("x_ready"), x_at + c + 1)
                        nc.scalar.activation(tmp[:, c, :], src[:, c, :], ACT.Square).then_inc(sem("squares"), 1)
                norms += 1
                act.wait_ge(sem("norm_summed"), norms)
                if norms > 1:
                    act.wait_ge(sem("rstd_used"), norms - 1)
                nc.scalar.activation(rstd[:, :], ms[0][:, 0, :], ACT.Sqrt, bias=eps_col[:, 0:1], scale=1.0 / D).then_inc(sem("std_ready"), 1)

            act.wait_ge(sem("c_turned"), 1)
            nc.scalar.activation(c_act[:, :], ms[0][:, 0, 0:CT], ACT.Silu).then_inc(sem("c_ready"), 1)
            act.wait_ge(sem("x_turned"), 1)
            nc.scalar.copy(xT[:, :, :], st[:, :, :]).then_inc(sem("x_kept"), 1)
            act.wait_ge(sem("x_kept"), 1)
            act.wait_ge(sem("consts"), 1)
            norm(xT)
            for l in range(DEPTH):
                act.wait_ge(sem("params_turned"), l + 1)
                b = ms[l][:, :, :].rearrange("p s t -> p (s t)")
                nc.scalar.copy(pc[:, l, :], b[:, 0:NPC]).then_inc(sem("params_kept"), 1)
            act.wait_ge(sem("params2_turned"), 1)
            nc.scalar.copy(pc2[:, :], ms[0][:, 0, 0:28])
            nc.scalar.copy(pe_T[:, :, :].rearrange("p m i -> p (m i)"), ms[0][:, 1, 0:2 * CMP_LEN]).then_inc(sem("params2_kept"), 1)
            act.wait_ge(sem("params2_kept"), 1)

            def drain(dst, func, n=2, job=None, other=None):
                nonlocal bank, qkv
                if job:
                    act.wait_ge(sem("slot_used"), job_at[job] + 1)
                else:
                    qkv += 1
                    act.wait_ge(sem("qkv_made"), qkv)
                i = nc.scalar.activation(dst, (other or pj[bank % 2])[:, 0:n, :], func)
                i.then_inc(sem("proj_drained"), 1)
                bank += 1
                return i

            h_tiles = 0

            def finish_h(shift):
                nonlocal h_tiles
                for c in range(CT):
                    h_tiles += 1
                    act.wait_ge(sem("h_scaled"), h_tiles)
                    nc.scalar.activation(hT[:, c, :], hT[:, c, :], ACT.Identity, bias=modc[:, shift + c:shift + c + 1]).then_inc(sem("h_ready"), 1)

            def drain_y(c, job, other=None):
                i = drain(y[:, c:c + 1, :], ACT.Copy, 1, job, other)
                act.wait_ge(sem("proj_drained"), bank)
                nc.scalar.activation(tmp[:, c, :], y[:, c, :], ACT.Square).then_inc(sem("squares"), 1)

            def drain_u(l, js):
                for j in js:
                    drain(U[:, 2 * j:2 * j + 2, :], ACT.Sigmoid if j >= 12 or 4 <= j < 8 else ACT.Copy, job=("w_in", l, j))

            for l in range(DEPTH):
                if l:
                    norm(xT, CT * (2 * l - 1))
                finish_h(0)
                drain_u(l, W_IN_ORDER[:8])
                act.wait_ge(sem("conv_m_ready"), l + 1)
                nc.scalar.activation(xc[:, :, :], xc[:, :, :], ACT.Silu).then_inc(sem("xc_ready"), 1)
                drain_u(l, W_IN_ORDER[8:12])
                for h in range(H):
                    drain(vT[:, 2 * h:2 * h + 2, :], ACT.Copy)
                for s in range(2):
                    for hp in range(2):
                        drain(vtok[:, s, 512 * hp:512 * hp + 512].rearrange("p (a t) -> p a t", a=2), ACT.Copy)
                for dst in (qT, kT):
                    for h in range(H):
                        drain(dst[:, 2 * h:2 * h + 2, :], ACT.Copy)

                act.wait_ge(sem("gates_made"), l + 1)
                nc.scalar.activation(gates[:, :], ms[0][0:2 * H, 0, :], ACT.Identity, bias=bg[:, 0:1]).then_inc(sem("gates_kept"), 1)
                act.wait_ge(sem("qkv_made"), 16 * (l + 1))
                act.wait_ge(sem("fg_moved"), l + 1)
                link(nc.scalar.activation(fgr[:, 0, :], ms[0][0:H, 1, :], ACT.Copy))
                link(nc.scalar.activation(fgr[:, 1, :], fgr[:, 0, :], ACT.Abs))
                link(nc.scalar.activation(fgr[:, 1, :], fgr[:, 1, :], ACT.Exp, scale=-1.0))
                nc.scalar.activation(fgr[:, 2, :], fgr[:, 1, :], ACT.Ln, bias=ones[0:H, 0:1]).then_inc(sem("softplus"), 1)
                drain_u(l, [4])
                act.wait_ge(sem("m_ready"), l + 1)
                nc.scalar.activation(rows[:, 1, :], lrow[:, 1, :], ACT.Exp, scale=-1.0).then_inc(sem("rows_ready"), 1)
                act.wait_ge(sem("r_turned"), l + 1)
                nc.scalar.copy(rcol[:, :, :].rearrange("p s h -> p (s h)"), ms[0][:, 0, 0:2 * H]).then_inc(sem("rcol_kept"), 1)

                for h in range(H):
                    hn = l * H + h
                    act.wait_ge(sem("rows_spread"), hn + 1)
                    if hn:
                        act.wait_ge(sem("head_done"), hn)
                    nc.scalar.copy(en_b[:, :], ms[0][:, 1, :]).then_inc(sem("en_kept"), 1)
                    act.wait_ge(sem("wlog_ready"), hn + 1)
                    nc.scalar.activation(wlog[:, 0, :], wlog[:, 0, :], ACT.Exp)
                    nc.scalar.activation(wlog[:, 1, P:T], wlog[:, 1, P:T], ACT.Exp).then_inc(sem("w_ready"), 1)
                    if h < 3:
                        drain_u(l, [5 + h])

                for h in range(H):
                    act.wait_ge(sem("hm_centred"), H * l + h + 1)
                    nc.scalar.activation(hT[:, 2 * h:2 * h + 2, :], tmp[:, 2 * h:2 * h + 2, :], ACT.Square).then_inc(sem("hm_squared"), 1)
                act.wait_ge(sem("var_made"), 2 * l + 1)
                nc.scalar.activation(vrow, ms[0][0:CT, 0, :], ACT.Sqrt, bias=eps_col[0:CT, 0:1], scale=1.0 / DH).then_inc(sem("var_std"), 1)

                for b in range(4):
                    act.wait_ge(sem("gn_centred"), 4 * l + b + 1)
                    nc.scalar.activation(tmp[:, 2 * b:2 * b + 2, :], U[:, 16 + 2 * b:18 + 2 * b, :], ACT.Square).then_inc(sem("gn_squared"), 1)
                act.wait_ge(sem("var_made"), 2 * l + 2)
                nc.scalar.activation(vrow, ms[0][0:CT, 0, :], ACT.Sqrt, bias=eps_col[0:CT, 0:1], scale=1.0 / P).then_inc(sem("var_std"), 1)
                for c in range(CT):
                    if c % 2 == 0:
                        act.wait_ge(sem("gn_scaled"), 4 * l + c // 2 + 1)
                    nc.scalar.activation(U[:, 16 + c, :], U[:, 16 + c, :], ACT.Silu, bias=pc[:, l, B_CN + c:B_CN + c + 1],
                                         scale=pc[:, l, G_CN + c:G_CN + c + 1]).then_inc(sem("mix_ready"), 1)

                for c in range(CT):
                    drain_y(c, ("w_out", l, c), ms[1] if c == 2 else None)
                norm(y)
                norm(xT, CT * 2 * l)
                finish_h(24)
                for j in range(16):
                    link_dst = U[:, 2 * j:2 * j + 2, :]
                    act.wait_ge(sem("slot_used"), job_at[("w_ff1", l, j)] + 1)
                    link(nc.scalar.activation(link_dst, pj[bank % 2][:, :, :], ACT.Relu))
                    nc.scalar.activation(link_dst, link_dst, ACT.Square).then_inc(sem("proj_drained"), 1)
                    bank += 1
                if l == DEPTH - 1:
                    act.wait_ge(sem("mem_in"), 16)
                    for t in range(2):
                        link(nc.scalar.activation(wqkv_free[:, :], memtok[:, t, :], ACT.Square, accum_out=mstat[:, 0, t:t + 1]))
                    nc.scalar.activation(mstat[:, 1, :], mstat[:, 0, :], ACT.Sqrt, bias=eps_col[:, 0:1], scale=1.0 / D).then_inc(sem("mem_std"), 1)
                for c in range(CT):
                    drain_y(c, ("w_ff2", l, 2 * c + 1))
                if l == DEPTH - 1:
                    act.wait_ge(sem("mem_turned"), 1)
                    for c in range(CT):
                        i = nc.scalar.activation(memT[:, c, :], st[:, c, :], ACT.Copy, scale=pc2[:, G_MEM2 + c:G_MEM2 + c + 1])
                    i.then_inc(sem("memT_ready"), 1)
                    act.wait_ge(sem("bias_made"), 1)
                    nc.scalar.copy(bias_w[0:NH, 0:T], ms[1][0:NH, 0, :]).then_inc(sem("bias_copied"), 1)
                norm(y)

            def drain2(dst, name, func=ACT.Copy, shape=None):
                nonlocal bank
                act.wait_ge(sem("slot_used"), job_at[(name, 2, 0)] + 1)
                src = pj[bank_of()][:, :, :]
                if shape:
                    src = src.rearrange("p a t -> p (a t)")
                bank += 1
                return nc.scalar.activation(dst, src, func).then_inc(sem("proj_drained"), 1)

            merged_banks = 0

            def bank_of():
                return (bank + merged_banks) % 2

            norm(xT, CT * (2 * DEPTH - 1))
            drain2(cmpT[:, 0], "kcmp")
            drain2(cmpT[:, 1], "vcmp")
            act.wait_ge(sem("proj_drained"), bank)
            act.sem_inc(sem("cmpT_kept"), 1)
            for j in range(4):
                drain2(q2T[:, 2 * j:2 * j + 2, :], f"q{j}")
            act.wait_ge(sem("bias_out"), 16)
            drain2(kselT[:, 0], "ksel")
            drain2(v2[:, 0], "vsel")
            drain2(kselT[:, 1], "kwin")
            drain2(v2[:, 1], "vwin")
            act.wait_ge(sem("bgate_made"), 1)
            nc.scalar.activation(bgate[:, :, :].rearrange("p s n -> p (s n)"), pj[bank_of()][:, 0, 0:96], ACT.Sigmoid).then_inc(sem("proj_drained"), 1)
            bank += 1
            act.wait_ge(sem("cmp_made"), 1)
            nc.scalar.copy(cmpc[:, 0].rearrange("p g c -> p (g c)"), ms[1][:, 0, 0:2 * NCMP])
            nc.scalar.copy(cmpc[:, 1].rearrange("p g c -> p (g c)"), ms[1][:, 0, 32:32 + 2 * NCMP]).then_inc(sem("cmp_kept"), 1)
            drain2(qxT[:, 0:2, :], "qx0")
            drain2(qxT[:, 2:4, :], "qx1")
            act.wait_ge(sem("vc_turned"), 1)
            nc.scalar.copy(vc[:, :, :].rearrange("p g e -> p (g e)"), ms[1][0:NCMP, 1, :]).then_inc(sem("vc_kept"), 1)
            drain2(kxT[:, 0:2, :], "memk0")
            drain2(kxT[:, 2:4, :], "memk1")
            drain2(vx[:, :, 0:256], "memv0")
            drain2(vx[:, :, 256:512], "memv1")
            act.wait_ge(sem("proj_drained"), bank)
            act.sem_inc(sem("vx_kept"), 1)

            turned = 0
            for u, (g, s) in enumerate(UNITS):
                act.wait_ge(sem("max_ready"), u + 1)
                pb, sv = probs[u % 2], stat[:, u % 2]
                n = P * (s + 1)
                if g == "x":
                    for h in range(XH):
                        i = nc.scalar.activation(pb[:, 0, h, :], pb[:, 0, h, :], ACT.Exp, bias=sv[:, 0, 1, h:h + 1], accum_out=sv[:, 1, 1, h:h + 1])
                else:
                    nb = NCMP if s else NCMP // 2
                    for r in range(R):
                        nc.scalar.activation(pcmp[:, u % 2, r, 0:nb], pcmp[:, u % 2, r, 0:nb], ACT.Exp, bias=sv[:, 0, 0, r:r + 1], accum_out=sv[:, 1, 0, r:r + 1])
                        for m in range(2):
                            i = nc.scalar.activation(pb[:, m, r, 0:n], pb[:, m, r, 0:n], ACT.Exp, bias=sv[:, 0, 1 + m, r:r + 1], accum_out=sv[:, 1, 1 + m, r:r + 1])
                i.then_inc(sem("exp_done"), 1)
                for name in FILL[u]:
                    if name[:2] == "gm":
                        j = int(name[2:])
                        drain2(gm[:, 2 * j:2 * j + 2, :], name, ACT.Sigmoid)
                    elif name == "mix":
                        for m in range(2):
                            act.wait_ge(sem("mixed"), m + 1)
                            for k in range(2):
                                c = 2 * m + k
                                i = nc.scalar.activation(poolT[:, c, :], pj[bank_of()][:, k, :], ACT.Copy, scale=pc2[:, POOL_SC2 + c:POOL_SC2 + c + 1])
                            i.then_inc(sem("proj_drained"), 1)
                            bank += 1
                        act.wait_ge(sem("proj_drained"), bank)
                        act.sem_inc(sem("mix_kept"), 1)
                    elif name[:8] == "pool_out":
                        merged_banks += 2
                    elif name[:7] == "nsa_out":
                        merged_banks += 1
                    else:
                        j = int(name[4:])
                        drain2(poolT[:, 2 * j:2 * j + 2, :], name)
                        if j == 1:
                            act.wait_ge(sem("proj_drained"), bank)
                            act.sem_inc(sem("pool_kept"), 1)
                for m in range(1 if g == "x" else 2):
                    for j in range(2 if g == "x" else s + 1):
                        turned += 1
                        act.wait_ge(sem("turned"), turned)
                        nc.scalar.copy(probsT[:, m, j].rearrange("p r t -> p (r t)"), pj[bank_of()][:, :, :].rearrange("p a t -> p (a t)")).then_inc(sem("proj_drained"), 1)
                        bank += 1
                if g != "x":
                    turned += 1
                    act.wait_ge(sem("turned"), turned)
                    nc.scalar.copy(pcmpT[0:nb, :, :].rearrange("p r t -> p (r t)"), pj[bank_of()][0:nb, :, :].rearrange("p a t -> p (a t)")).then_inc(sem("proj_drained"), 1)
                    bank += 1
                act.wait_ge(sem("proj_drained"), bank)
                act.sem_inc(sem("turned_kept"), 1)
                act.wait_ge(sem("o_made"), u + 1)
                o = pj[bank_of()]
                if g == "x":
                    i = nc.scalar.copy(oxT[:, :, P * s:P * s + P], o[:, :, :].rearrange("p a t -> p (a t)").rearrange("p (h t) -> p h t", h=XH))
                else:
                    i = nc.scalar.copy(oT[:, 2 * g:2 * g + 2, P * s:P * s + P], o[:, 0, :].rearrange("p (a t) -> p a t", a=2))
                i.then_inc(sem("proj_drained"), 1)
                bank += 1
                act.wait_ge(sem("proj_drained"), bank)
                act.sem_inc(sem("o_kept"), 1)
            act.sem_inc(sem("attention_done"), 1)
            merged_banks += 8
            act.wait_ge(sem("sub_turned"), 1)
            nc.scalar.copy(subT.rearrange("p c t -> p (c t)"), st[:, :, :].rearrange("p c t -> p (c t)")).then_inc(sem("sub_kept"), 1)
            act.wait_ge(sem("x2_ready"), 1)
            norm(xT)
            for j in range(PH):
                act.wait_ge(sem("slot_used"), job_at[(f"peer_q{j}", 2, 0)] + 1)
                nc.scalar.copy(qpT[:, 2 * j:2 * j + 2, :], pj[bank_of()][:, :, :]).then_inc(sem("qp_kept"), 1)
                act.wait_ge(sem("qp_kept"), j + 1)
                act.sem_inc(sem("proj_drained"), 1)
                bank += 1
                act.wait_ge(sem("sub_scores"), j + 1)
                nc.scalar.copy(s_sb[:, j].rearrange("p c t -> p (c t)"), ms[j % 2][:, :, :].rearrange("p a t -> p (a t)")).then_inc(sem("sub_scores_kept"), 1)
                if j < 2:
                    act.wait_ge(sem("tok_turned"), j + 1)
                    nc.scalar.copy((h_tok, acc)[j].rearrange("p s d -> p (s d)"), st[:, :, :].rearrange("p c t -> p (c t)")).then_inc(sem("tok_kept"), 1)
            for u in range(2 * PH):
                act.wait_ge(sem("best_ready"), u + 1)
                nc.scalar.activation(gate[:, u, :], gate[:, u, :], ACT.Exp, accum_out=gsum[:, u:u + 1]).then_inc(sem("gate_exp"), 1)
                act.wait_ge(sem("dots_ready"), u + 1)
                nc.scalar.activation(wgt[:, u, :], dots[:, u, :], ACT.Gelu).then_inc(sem("gelu_done"), 1)
            for s in range(2):
                act.wait_ge(sem("acc_ready"), s + 1)
                link(nc.scalar.activation(h_tok[:, s, :], acc[:, s, :], ACT.Square, accum_out=mstat[:, 0, s:s + 1]))
                nc.scalar.activation(mstat[:, 1, s:s + 1], mstat[:, 0, s:s + 1], ACT.Sqrt, bias=eps_col[:, 0:1], scale=1.0 / D).then_inc(sem("last_std"), 1)

        @block.vector
        def _(dve):
            steps = 0
            norms = 0

            def count(i):
                nonlocal steps
                steps += 1
                i.then_inc(sem("dve_step"), 1)
                return steps

            def link(i):
                dve.wait_ge(sem("dve_step"), count(i))

            def rsqrt_finish():
                nonlocal norms
                norms += 1
                dve.wait_ge(sem("std_ready"), norms)
                link(nc.vector.reciprocal(rstd[:, :], rstd[:, :]))

            def over_channels(t):
                return t.unsqueeze(1).broadcast_to([P, CT, T])

            def col(l, at, c):
                return pc[:, l, at + c:at + c + 1]

            def pre_norm(l, which):
                if l or which:
                    rsqrt_finish()
                for c in range(CT):
                    i = nc.vector.scalar_tensor_tensor(hT[:, c, :], xT[:, c, :], mod_scale[:, which, c:c + 1], rstd[:, :], ALU.mult, ALU.mult)
                    i.then_inc(sem("h_scaled"), 1)
                dve.wait_ge(sem("h_scaled"), (2 * l + (which == 1) + 1) * CT)
                dve.sem_inc(sem("rstd_used"), 1)

            def post_norm(l, which):
                rsqrt_finish()
                scaled = []
                for c in range(CT):
                    scaled.append(count(nc.vector.scalar_tensor_tensor(y[:, c, :], y[:, c, :], mod_scale[:, which, c:c + 1], rstd[:, :],
                                                                       ALU.mult, ALU.mult)))
                    if c:
                        dve.wait_ge(sem("dve_step"), scaled[c - 1])
                        nc.vector.tensor_tensor(xT[:, c - 1, :], xT[:, c - 1, :], y[:, c - 1, :], ALU.add).then_inc(sem("x_ready"), 1)
                dve.wait_ge(sem("dve_step"), scaled[-1])
                nc.vector.tensor_tensor(xT[:, CT - 1, :], xT[:, CT - 1, :], y[:, CT - 1, :], ALU.add).then_inc(sem("x_ready"), 1)
                dve.sem_inc(sem("rstd_used"), 1)

            last = {}

            def tap(l, dst, src, taps, w, bias, back, signal=None, tiles=CT):
                for c in range(tiles):
                    wc = col(l, w, (taps - 1 - back) * CT + c)
                    if back == 0:
                        i = nc.vector.tensor_scalar(dst[:, c, :], src[:, c, :], wc, col(l, bias, c), ALU.mult, ALU.add)
                    else:
                        dve.wait_ge(sem("dve_step"), last[c])
                        i = nc.vector.scalar_tensor_tensor(dst[:, c, back:T], src[:, c, 0:T - back], wc, dst[:, c, back:T], ALU.mult, ALU.add)
                    if signal and c == tiles - 1:
                        i.then_inc(sem(signal), 1)
                    else:
                        last[c] = count(i)

            done_taps = 0

            def long_taps(l, n):
                nonlocal done_taps
                for back in range(done_taps, min(done_taps + n, KC)):
                    tap(l, U[:, 16:24], U[:, 24:32], KC, W_DW, B_DW, back, "conv_ready" if back == KC - 1 else None, DVE_TILES[l])
                done_taps = min(done_taps + n, KC)

            rsqrt_finish()
            dve.wait_ge(sem("c_ready"), 1)
            for j in range(4):
                dve.wait_ge(sem(f"ada_first{j}"), 16)
                acc_j = ada_acc[:, 512 * j:512 * j + 512]
                for k in range(CT):
                    w = ada_first[j // 2][:, k, 512 * (j % 2):512 * (j % 2) + 512]
                    if k == 0:
                        i = nc.vector.tensor_scalar(acc_j, w, c_act[:, 0:1], None, ALU.mult)
                    else:
                        i = nc.vector.scalar_tensor_tensor(acc_j, w, c_act[:, k:k + 1], acc_j, ALU.mult, ALU.add)
                    if k < CT - 1:
                        link(i)
                i.then_inc(sem("first_partial"), 1)

            dve.wait_ge(sem("consts"), 1)
            dve.wait_ge(sem("consts2"), 1)
            dve.wait_ge(sem("params2_kept"), 1)
            dve.wait_ge(sem("params_kept"), 2)
            dve.wait_ge(sem("x_kept"), 1)
            for l in range(DEPTH):
                def modulation(first, last_col, kinds):
                    link(nc.vector.tensor_tensor(modc[:, first:last_col], ms[1][:, 0, first:last_col], pc[:, l, B_ADA + first:B_ADA + last_col], ALU.add))
                    for n in kinds:
                        src, g, one = ((8, G_PRE_MIX, 1.0), (32, G_PRE_MLP, 1.0), (16, G_POST_MIX, 0.0), (40, G_POST_MLP, 0.0))[n]
                        i = nc.vector.scalar_tensor_tensor(mod_scale[:, n, :], modc[:, src:src + 8], one, pc[:, l, g:g + 8], ALU.add, ALU.mult)
                    link(i)

                dve.wait_ge(sem("mod_first"), l + 1)
                modulation(0, 16, (0,))
                pre_norm(l, 0)

                dve.wait_ge(sem("proj_drained"), 64 * l + 4)
                for back in range(KM):
                    tap(l, xc, U[:, 0:8], KM, W_CONV, B_CONV_M, back, "conv_m_ready" if back == KM - 1 else None)
                dve.wait_ge(sem("proj_drained"), 64 * l + 12)
                nc.vector.tensor_tensor(U[:, 24:32, :], U[:, 16:24, :], U[:, 24:32, :], ALU.mult).then_inc(sem("glu_ready"), 1)
                dve.wait_ge(sem("glu_ready"), l + 1)
                done_taps = 0
                long_taps(l, 19)

                dve.wait_ge(sem("softplus"), l + 1)
                link(nc.vector.scalar_tensor_tensor(lrow[:, 0, :], fgr[:, 0, :], 0.0, fgr[:, 2, :], ALU.min, ALU.subtract))
                link(nc.vector.tensor_tensor_scan(lrow[:, 3, :], lrow[:, 0, :], zrow[:, :], 0.0, ALU.add, ALU.add))
                link(nc.vector.tensor_tensor(lrow[:, 2, :], gates[0:H, :], lrow[:, 3, :], ALU.subtract))
                link(nc.vector.tensor_tensor_scan(lrow[:, 0, :], lrow[:, 2, :], zrow[:, :], 0.0, ALU.max, ALU.add))
                nc.vector.tensor_scalar(rows[:, 0, :], lrow[:, 0, :], -1.0, None, ALU.mult)
                nc.vector.tensor_tensor(lrow[:, 1, :], lrow[:, 3, :], lrow[:, 0, :], ALU.add).then_inc(sem("m_ready"), 1)

                dve.wait_ge(sem("mod_summed"), l + 1)
                modulation(16, 48, (1, 2, 3))
                dve.sem_inc(sem("mod_kept"), 1)
                dve.wait_ge(sem("rcol_kept"), l + 1)
                for h in range(H):
                    hn = l * H + h
                    dve.wait_ge(sem("en_kept"), hn + 1)
                    for s in range(2):
                        i = nc.vector.scalar_tensor_tensor(wlog[:, s, P * s:T], ms[0][:, 0, P * s:T], rcol[:, s, h:h + 1], causal[:, s, P * s:T], ALU.add, ALU.add)
                    i.then_inc(sem("wlog_ready"), 1)
                    long_taps(l, 1)
                    dve.wait_ge(sem("w_ready"), hn + 1)
                    dve.wait_ge(sem("scores_made"), hn + 1)
                    for s in range(2):
                        i = nc.vector.scalar_tensor_tensor(sT[:, s, P * s:T], ms[1][:, s, P * s:T], DH ** -0.5, wlog[:, s, P * s:T], ALU.mult, ALU.mult)
                    i.then_inc(sem("s_ready"), 1)
                    long_taps(l, 1)
                    dve.wait_ge(sem("num_made"), hn + 1)
                    link(nc.vector.tensor_scalar(den[:, :], st[:, 4, :], -1.0, None, ALU.mult))
                    link(nc.vector.tensor_tensor(den[:, :], den[:, :], st[:, 4, :], ALU.max))
                    link(nc.vector.tensor_tensor(den[:, :], den[:, :], en_b[:, :], ALU.max))
                    link(nc.vector.reciprocal(den[:, :], den[:, :]))
                    nc.vector.tensor_tensor(tmp[:, 2 * h:2 * h + 2, :], st[:, 6:8, :], den[:, :].unsqueeze(1).broadcast_to([P, 2, T]), ALU.mult).then_inc(sem("head_done"), 1)
                for h in range(H):
                    dve.wait_ge(sem("hm_summed"), H * l + (2 if h < 2 else 4))
                    for e in range(2):
                        i = nc.vector.scalar_tensor_tensor(tmp[:, 2 * h + e, :], st[:, h, :], -1.0 / DH, tmp[:, 2 * h + e, :], ALU.mult, ALU.add)
                    i.then_inc(sem("hm_centred"), 1)
                long_taps(l, 1)
                dve.wait_ge(sem("var_std"), 2 * l + 1)
                nc.vector.reciprocal(vrow, vrow).then_inc(sem("var_inverse"), 1)
                long_taps(l, 1)
                dve.wait_ge(sem("hm_spread"), l + 1)
                def times_z(b):
                    dve.wait_ge(sem("dve_step"), scaled[b])
                    nc.vector.tensor_tensor(U[:, 8 + 2 * b:10 + 2 * b, :], tmp[:, 2 * b:2 * b + 2, :], U[:, 8 + 2 * b:10 + 2 * b, :],
                                            ALU.mult).then_inc(sem("mlstm_ready"), 1)

                scaled = []
                for b in range(4):
                    for c in (2 * b, 2 * b + 1):
                        i = nc.vector.scalar_tensor_tensor(tmp[:, c, :], tmp[:, c, :], col(l, G_MH, c), st[:, c // 2, :], ALU.mult, ALU.mult)
                    scaled.append(count(i))
                    if b:
                        times_z(b - 1)
                times_z(3)
                long_taps(l, KC)
                for b in range(4):
                    dve.wait_ge(sem("gn_summed"), 4 * l + b + 1)
                    nc.vector.scalar_tensor_tensor(U[:, 16 + 2 * b:18 + 2 * b, :], st[:, 2 * b:2 * b + 2, :], -1.0 / P, U[:, 16 + 2 * b:18 + 2 * b, :],
                                                   ALU.mult, ALU.add).then_inc(sem("gn_centred"), 1)
                dve.wait_ge(sem("var_std"), 2 * l + 2)
                nc.vector.reciprocal(vrow, vrow).then_inc(sem("var_inverse"), 1)
                for b in range(4):
                    dve.wait_ge(sem("gn_spread"), 4 * l + b + 1)
                    nc.vector.tensor_tensor(U[:, 16 + 2 * b:18 + 2 * b, :], U[:, 16 + 2 * b:18 + 2 * b, :], st[:, 2 * b:2 * b + 2, :], ALU.mult).then_inc(sem("gn_scaled"), 1)

                post_norm(l, 2)
                pre_norm(l, 1)
                if l == DEPTH - 1:
                    dve.wait_ge(sem("mem_std"), 1)
                    link(nc.vector.reciprocal(mstat[:, 1, :], mstat[:, 1, :]))
                    for t in range(2):
                        i = nc.vector.tensor_scalar(memtok[:, t, :], memtok[:, t, :], mstat[:, 1, t:t + 1], None, ALU.mult)
                    i.then_inc(sem("mem_scaled"), 1)
                    dve.wait_ge(sem("bias_in"), 32)
                    nc.vector.memset(bias_w[0:NH, T:512], NEG).then_inc(sem("bias_masked"), 1)
                post_norm(l, 3)

            def gain_norm(g, n):
                rsqrt_finish()
                for c in range(CT):
                    i = nc.vector.scalar_tensor_tensor(hT[:, c, :], xT[:, c, :], pc2[:, g + c:g + c + 1], rstd[:, :], ALU.mult, ALU.mult)
                    i.then_inc(sem("h_ready"), 1)
                dve.wait_ge(sem("h_ready"), n * CT)
                dve.sem_inc(sem("rstd_used"), 1)

            dve.wait_ge(sem("x_ready"), 2 * DEPTH * CT)
            gain_norm(G_MIX2, 5)
            dve.wait_ge(sem("cmpT_kept"), 1)
            for m in range(2):
                for g in range(2):
                    for hf in range(2):
                        src = cmpT[:, m, g, 16 * hf:16 * hf + 16 * NCMP].rearrange("p (c i) -> p c i", i=16)
                        i = nc.vector.tensor_tensor(blk[:, m, g, :, 16 * hf:16 * hf + 16], src,
                                                    pe_T[:, m, 16 * hf:16 * hf + 16].unsqueeze(1).broadcast_to([P, NCMP, 16]), ALU.add)
            i.then_inc(sem("blk_ready"), 1)
            dve.wait_ge(sem("proj_drained"), GATE_BANK)
            link(nc.vector.tensor_scalar(bgate[:, 0, 0:NH], bgate[:, 0, 0:NH], has[:, 0:1], None, ALU.mult))
            dve.wait_ge(sem("toeplitz_in"), 32)
            merge_jobs = 0

            def merge(job, tiles, branch, how):
                nonlocal merge_jobs
                sm, v, b = job
                dve.wait_ge(sem(sm), v)
                src = pj[b][:, :, :]
                if how == "x":
                    i = nc.vector.tensor_tensor(xT[:, tiles:tiles + 2, :], xT[:, tiles:tiles + 2, :], src, ALU.add)
                    return i.then_inc(sem("merge_drained"), 1)
                g = gm[:, CT * branch + tiles:CT * branch + tiles + 2, :]
                dst = merged[:, tiles:tiles + 2, :]
                if how == "first":
                    i = nc.vector.tensor_tensor(dst, src, g, ALU.mult)
                    return i.then_inc(sem("merge_drained"), 1)
                link(nc.vector.tensor_tensor(g, src, g, ALU.mult))
                nc.vector.tensor_tensor(dst, dst, g, ALU.add).then_inc(sem("merge_drained"), 1)

            for u, (g, s) in enumerate(UNITS):
                pb, sv = probs[u % 2], stat[:, u % 2]
                n = P * (s + 1)
                dve.wait_ge(sem("scores2_made"), u + 1)
                if u == 1:
                    dve.wait_ge(sem("vx_kept"), 1)
                if g == "x":
                    link(nc.vector.tensor_scalar(pb[:, 0], st[:, 0:R, :], float(P) ** -0.5, None, ALU.mult))
                    dve.sem_inc(sem("scores_kept"), 1)
                    link(nc.vector.tensor_reduce(sv[:, 0, 1, :], pb[:, 0], AX.X, ALU.max))
                    nc.vector.tensor_scalar(sv[:, 0, 1, :], sv[:, 0, 1, :], -1.0, None, ALU.mult).then_inc(sem("max_ready"), 1)
                else:
                    nb = NCMP if s else NCMP // 2
                    bs = bias[s][:, R * g:R * g + R, :]
                    nc.vector.scalar_tensor_tensor(pcmp[:, u % 2, :, 0:nb], ms[0][:, 0, 0:64].rearrange("p (r c) -> p r c", c=16)[:, :, 0:nb],
                                                   HD ** -0.5, bs[:, :, CMP_LEN - 1:CMP_LEN + CMP_STRIDE * (nb - 1):CMP_STRIDE], ALU.mult, ALU.add)
                    for m in range(2):
                        i = nc.vector.scalar_tensor_tensor(pb[:, m, :, 0:n], st[:, R * m:R * m + R, 0:n], HD ** -0.5, bs, ALU.mult, ALU.add)
                    link(i)
                    dve.sem_inc(sem("scores_kept"), 1)
                    nc.vector.tensor_reduce(sv[:, 0, 0, :], pcmp[:, u % 2, :, 0:nb], AX.X, ALU.max)
                    for m in range(2):
                        i = nc.vector.tensor_reduce(sv[:, 0, 1 + m, :], pb[:, m, :, 0:n], AX.X, ALU.max)
                    link(i)
                    nc.vector.tensor_scalar(sv[:, 0], sv[:, 0], -1.0, None, ALU.mult).then_inc(sem("max_ready"), 1)
                if u == 1:
                    dve.wait_ge(sem("pool_kept"), 1)
                    dve.wait_ge(sem("cmp_made"), 1)
                    dve.wait_ge(sem("rcount_in"), 16)
                    src = poolT
                    for k in range(4):
                        sh, dst = 1 << k, win[k % 2]
                        nc.vector.tensor_copy(dst[:, k:4, 0:sh], src[:, k:4, 0:sh])
                        link(nc.vector.tensor_tensor(dst[:, k:4, sh:T], src[:, k:4, sh:T], src[:, k:4, 0:T - sh], ALU.add))
                        src = dst
                    for k in range(4):
                        i = nc.vector.tensor_tensor(win[k % 2][:, k, :], win[k % 2][:, k, :], rc[:, k, :], ALU.mult)
                    link(i)
                    for k in range(4):
                        i = nc.vector.tensor_tensor(win[0][:, k, :], win[k % 2][:, k, :], poolT[:, k, :], ALU.subtract)
                    i.then_inc(sem("pooled"), 1)
                dve.wait_ge(sem("exp_done"), u + 1)
                if g == "x":
                    link(nc.vector.reciprocal(sv[:, 2, 1, :], sv[:, 1, 1, :]))
                    nc.vector.tensor_tensor(pb[:, 0], pb[:, 0], sv[:, 2, 1, :].unsqueeze(2).broadcast_to([P, R, T]), ALU.mult).then_inc(sem("probs_ready"), 1)
                else:
                    link(nc.vector.reciprocal(sv[:, 2], sv[:, 1]))
                    gates3 = bgate[:, s, :].rearrange("p (m h) -> p m h", m=3)[:, :, R * g:R * g + R]
                    link(nc.vector.tensor_tensor(sv[:, 2], sv[:, 2], gates3, ALU.mult))
                    nc.vector.tensor_tensor(pcmp[:, u % 2, :, 0:nb], pcmp[:, u % 2, :, 0:nb], sv[:, 2, 0, :].unsqueeze(2).broadcast_to([P, R, nb]), ALU.mult)
                    for m in range(2):
                        i = nc.vector.tensor_tensor(pb[:, m, :, 0:n], pb[:, m, :, 0:n], sv[:, 2, 1 + m, :].unsqueeze(2).broadcast_to([P, R, n]), ALU.mult)
                    i.then_inc(sem("probs_ready"), 1)
                if FILL[u] and FILL[u][0] == "pool_out0":
                    for j in range(2):
                        for k in range(2):
                            done = ("half_slot", j + 1, MERGE_BANKS[2 * j + k]) if k == 0 else ("slot_used", job_at[(f"pool_out{j}", 2, 0)] + 1, MERGE_BANKS[2 * j + k])
                            merge(done, 4 * j + 2 * k, 0, "first")
                for name in FILL[u]:
                    if name[:7] == "nsa_out":
                        j = int(name[7:])
                        merge(("slot_used", job_at[(name, 2, 0)] + 1, MERGE_BANKS[4 + j]), 2 * j, 1, "more")
            for j in range(2):
                for k in range(2):
                    done = ("half_slot", 2 + j + 1, MERGE_BANKS[8 + 2 * j + k]) if k == 0 else ("slot_used", job_at[(f"x_out{j}", 2, 0)] + 1, MERGE_BANKS[8 + 2 * j + k])
                    merge(done, 4 * j + 2 * k, 2, "more")
            for j in range(4):
                merge(("slot_used", job_at[(f"w_o{j}", 2, 0)] + 1, MERGE_BANKS[12 + j]), 2 * j, 0, "x")
            dve.wait_ge(sem("merge_drained"), 16)
            dve.sem_inc(sem("x2_ready"), 1)
            gain_norm(G_FFN2, 6)
            def retrieve(u):
                h, t = divmod(u, 2)
                dve.wait_ge(sem("sub_scores_kept"), h + 1)
                tv, ti, tf = top_v[:, 2 * t:2 * t + 2], top_i[:, 2 * t:2 * t + 2], top_f[:, 2 * t:2 * t + 2]
                top_of(dve, link, s_sb[:, h, 2 * t:2 * t + 2], tv, ti, 2)
                link(nc.vector.tensor_tensor(cand[:, t, :].rearrange("p (i j) -> p i j", i=TOPK), tv[:, 0, :].unsqueeze(2).broadcast_to([P, TOPK, TOPK]),
                                             tv[:, 1, :].unsqueeze(1).broadcast_to([P, TOPK, TOPK]), ALU.add))
                bt, pt = best[:, t:t + 1], pos[:, t:t + 1]
                top_of(dve, link, cand[:, t:t + 1], bt, pt, 1)
                link(nc.vector.tensor_scalar(gate[:, u, :], best[:, t, :], best[:, t, 0:1], None, ALU.subtract))
                dve.sem_inc(sem("best_ready"), 1)
                lo, hi = TOPK * t, TOPK * t + TOPK
                nc.vector.tensor_single_scalar(half[:, 0, lo:hi], pos[:, t, :], 4, ALU.logical_shift_right)
                nc.vector.tensor_single_scalar(half[:, 1, lo:hi], pos[:, t, :], 15, ALU.bitwise_and)
                link(nc.vector.tensor_copy(tf, ti))
                link(nc.vector.tensor_copy(half_f[:, :, lo:hi], half[:, :, lo:hi]))
                e = eq[:, 512 * t:512 * t + 512].rearrange("p (q k j) -> p q k j", q=2, j=TOPK)
                for q in range(2):
                    i = nc.vector.tensor_tensor(e[:, q], half_f[:, q, lo:hi].unsqueeze(2).broadcast_to([P, TOPK, TOPK]),
                                                iota16[:, :].unsqueeze(1).broadcast_to([P, TOPK, TOPK]), ALU.is_equal)
                link(i)
                link(nc.vector.tensor_tensor(e, e, tf.unsqueeze(2).broadcast_to([P, 2, TOPK, TOPK]), ALU.mult))
                link(nc.vector.tensor_reduce(part[:, :, lo:hi], e, AX.X, ALU.add))
                nc.vector.scalar_tensor_tensor(ids[:, TOPK * u:TOPK * u + TOPK], part[:, 0, lo:hi], float(P), part[:, 1, lo:hi],
                                               ALU.mult, ALU.add).then_inc(sem("ids_ready"), 1)

            retrieve(0)
            retrieve(1)
            dve.wait_ge(sem("tok_kept"), 2)
            total = 2 * PH * TOPK
            for n in range(total + LAG):
                if n % TOPK == 4 and n // TOPK + 2 < 2 * PH:
                    retrieve(n // TOPK + 2)
                if n < total:
                    u, k = divmod(n, TOPK)
                    dve.wait_ge(sem(f"u_row{n % NBUF}"), 16 * (n // NBUF + 1))
                    row = ubuf[:, n % NBUF, :]
                    i = nc.vector.tensor_tensor_reduce(row, row, h_tok[:, u % 2, :], 1.0, 0.0, ALU.mult, ALU.add, dots[:, u, k:k + 1])
                    i.then_inc(sem("u_used"), 1)
                    if k == TOPK - 1:
                        dve.wait_ge(sem("u_used"), n + 1)
                        dve.sem_inc(sem("dots_ready"), 1)
                m = n - LAG
                if m >= 0:
                    u, k = divmod(m, TOPK)
                    if k == 0:
                        dve.wait_ge(sem("gelu_done"), u + 1)
                        link(nc.vector.reciprocal(gsum[:, u:u + 1], gsum[:, u:u + 1]))
                        link(nc.vector.scalar_tensor_tensor(wgt[:, u, :], wgt[:, u, :], gsum[:, u:u + 1], gate[:, u, :], ALU.mult, ALU.mult))
                    dve.wait_ge(sem(f"v_row{m % NBUF}"), 16 * (m // NBUF + 1))
                    if m:
                        dve.wait_ge(sem("v_used"), m)
                    nc.vector.scalar_tensor_tensor(acc[:, u % 2, :], vbuf[:, m % NBUF, :], wgt[:, u, k:k + 1], acc[:, u % 2, :],
                                                   ALU.mult, ALU.add).then_inc(sem("v_used"), 1)
            dve.wait_ge(sem("v_used"), total)
            dve.sem_inc(sem("acc_ready"), 2)
            dve.wait_ge(sem("g_fin_in"), 16)
            for s in range(2):
                dve.wait_ge(sem("last_std"), s + 1)
                link(nc.vector.reciprocal(mstat[:, 1, s:s + 1], mstat[:, 1, s:s + 1]))
                nc.vector.scalar_tensor_tensor(h_tok[:, s, :], acc[:, s, :], mstat[:, 1, s:s + 1], g_fin, ALU.mult, ALU.mult).then_inc(sem("out_ready"), 1)


def kernel(**inputs):
    import numpy as _np
    import concourse.bacc as _bacc
    from concourse.bass_utils import run_bass_kernel_spmd as _run

    nc = _bacc.Bacc("TRN2", target_bir_lowering=False, num_devices=1)
    arrays, aps = {}, {}
    dist = _np.arange(256)
    large = 16 + (_np.log(_np.maximum(dist, 1) / 16.0) / _np.log(128 / 16.0) * 16).astype(_np.int64)
    bucket = _np.where(dist < 16, dist, _np.minimum(large, N_BUCKETS - 1))
    onehot = _np.zeros((N_BUCKETS, 512), _np.float32)
    onehot[bucket, 255 - dist] = 1.0
    t = _np.arange(T)
    rcount = _np.stack([1.0 / _np.minimum(t + 1, w) for w in POOL_WINDOWS]).astype(_np.float32)
    for name, v in list(inputs.items()) + [("onehot", onehot), ("rcount", rcount)]:
        v = _np.ascontiguousarray(v)
        arrays[f"in_{name}"] = v
        aps[name] = nc.dram_tensor(f"in_{name}", v.shape, mybir.dt.from_np(v.dtype), kind="ExternalInput").ap()
    out = nc.dram_tensor("out_0", (1, T, D), F32, kind="ExternalOutput").ap()
    build_program(nc, aps, out)
    r = _run(nc, [arrays], core_ids=[0])
    return r.results[0]["out_0"]
```
